# Optimizing a Trainium2 kernel written in Bass

```python
import jax
import jax.numpy as jnp
from jax import lax
import numpy as np

D_MODEL = 1024
BATCH = 1
SEQ = 512
DEPTH = 1

GRID_W = 64
CTX_LEN = 256
GLA_HEADS = 4
GLA_DK = 64
GLA_DV = 128
GLA_KEY = GLA_HEADS * GLA_DK
GLA_VAL = GLA_HEADS * GLA_DV
GLA_RANK = 16
GLA_CHUNK = 64
GATE_NORMALIZER = 16.0
POOL_WINDOWS = (2, 4, 8, 16)
POOL_GROUPS = 4
POOL_CH = 128
POOL_WIDTH = POOL_GROUPS * POOL_CH
N_BRANCHES = 2
N_EXPERTS = 16
D_EXPERT = 1024
EC_CAPACITY = 2
EPS = 1e-6
CTX_COLS = (GLA_KEY, GLA_VAL, GLA_RANK, GLA_RANK)
N_CTX_COLS = GLA_KEY + GLA_VAL + 2 * GLA_RANK
ALL_COLS = (N_CTX_COLS, GLA_KEY, GLA_VAL, POOL_WIDTH, N_BRANCHES * D_MODEL)
D_IN = N_CTX_COLS + GLA_KEY + GLA_VAL + POOL_WIDTH + N_BRANCHES * D_MODEL


def split_cols(u, sizes):
    points, acc = [], 0
    for s in sizes[:-1]:
        acc += s
        points.append(acc)
    return jnp.split(u, points, axis=-1)

def rms_norm(x, g):
    xf = x.astype(jnp.float32)
    y = xf * lax.rsqrt(jnp.mean(xf * xf, axis=-1, keepdims=True) + EPS)
    return (y * g.astype(jnp.float32)).astype(x.dtype)

def modulate(x, g, shift, scale):
    return rms_norm(x, g) * (1 + scale) + shift

def to_heads(u, d):
    b, l, _ = u.shape
    return u.reshape(b, l, GLA_HEADS, d).transpose(0, 2, 1, 3)

def chunked(u):
    b, h, l, d = u.shape
    return u.reshape(b, h, l // GLA_CHUNK, GLA_CHUNK, d)

def gla_scan(q, k, v, log_a, h0, with_output):
    kc = chunked(k.astype(jnp.float32))
    vc = chunked(v.astype(jnp.float32))
    b = jnp.cumsum(chunked(log_a.astype(jnp.float32)), axis=3)
    b_last = b[:, :, :, -1:, :]
    kv = jnp.einsum('bhncd,bhnce->bhnde', kc * jnp.exp(b_last - b), vc)
    decay = jnp.exp(b_last[:, :, :, 0, :])

    def step(state, inp):
        dec_n, kv_n = inp
        return dec_n[..., None] * state + kv_n, state

    final, starts = lax.scan(step, h0, (jnp.moveaxis(decay, 2, 0), jnp.moveaxis(kv, 2, 0)))
    if not with_output:
        return None, final
    starts = jnp.moveaxis(starts, 0, 2)
    qc = chunked(q.astype(jnp.float32))
    inter = jnp.einsum('bhncd,bhnde->bhnce', qc * jnp.exp(b), starts)
    mid = b[:, :, :, GLA_CHUNK // 2 - 1:GLA_CHUNK // 2, :]
    scores = jnp.einsum('bhnid,bhnjd->bhnij', qc * jnp.exp(b - mid), kc * jnp.exp(mid - b))
    lower = jnp.tril(jnp.ones((GLA_CHUNK, GLA_CHUNK), dtype=bool))
    intra = jnp.einsum('bhnij,bhnje->bhnie', jnp.where(lower, scores, 0.0), vc)
    bsz, h, n, cl, dv = intra.shape
    return (inter + intra).reshape(bsz, h, n * cl, dv), final

def gla_bidirectional(q, k, v, la_f, la_b, h0_f, h0_b, with_output):
    rev = lambda u: jnp.flip(u, axis=2)
    o_f, h_f = gla_scan(q, k, v, la_f, h0_f, with_output)
    q_rev = rev(q) if with_output else None
    o_b, h_b = gla_scan(q_rev, rev(k), rev(v), rev(la_b), h0_b, with_output)
    if not with_output:
        return None, h_f, h_b
    return o_f + rev(o_b), h_f, h_b

def kv_and_decay(proj_kvd, w_decay_up, b_decay):
    k, v, r_f, r_b = split_cols(proj_kvd, CTX_COLS)
    la_f = jax.nn.log_sigmoid((r_f @ w_decay_up[0] + b_decay[0]).astype(jnp.float32)) / GATE_NORMALIZER
    la_b = jax.nn.log_sigmoid((r_b @ w_decay_up[1] + b_decay[1]).astype(jnp.float32)) / GATE_NORMALIZER
    return to_heads(k, GLA_DK), to_heads(v, GLA_DV), to_heads(la_f, GLA_DK), to_heads(la_b, GLA_DK)

def context_states(ctx, g1, shift, scale, w_in, w_decay_up, b_decay):
    h = modulate(ctx, g1, shift, scale)
    k, v, la_f, la_b = kv_and_decay(h @ w_in[:, :N_CTX_COLS], w_decay_up, b_decay)
    zero = jnp.zeros((ctx.shape[0], GLA_HEADS, GLA_DK, GLA_DV), jnp.float32)
    _, h_f, h_b = gla_bidirectional(None, k, v, la_f, la_b, zero, zero, False)
    return h_f, h_b

def box_sum(u, w, axis):
    n = u.shape[axis]
    pad = [(0, 0)] * u.ndim
    pad[axis] = (1, 0)
    cs = jnp.pad(jnp.cumsum(u, axis=axis), pad)
    pos = jnp.arange(n)
    lo = jnp.clip(pos - w // 2, 0, n)
    hi = jnp.clip(pos + w // 2, 0, n)
    s = jnp.take(cs, hi, axis=axis) - jnp.take(cs, lo, axis=axis)
    return s, (hi - lo).astype(jnp.float32)

def pool_latent(u):
    bsz, l, _ = u.shape
    rows = l // GRID_W
    ug = u.astype(jnp.float32).reshape(bsz, rows, GRID_W, POOL_GROUPS, POOL_CH)
    outs = []
    for gi, w in enumerate(POOL_WINDOWS):
        ugi = ug[:, :, :, gi, :]
        s, cnt_c = box_sum(ugi, w, 2)
        s, cnt_r = box_sum(s, w, 1)
        outs.append(s / (cnt_r[:, None] * cnt_c[None, :])[None, :, :, None] - ugi)
    return jnp.stack(outs, axis=3).reshape(bsz, l, POOL_GROUPS, POOL_CH)

def pool_context(u):
    bsz, l, _ = u.shape
    ug = u.astype(jnp.float32).reshape(bsz, l, POOL_GROUPS, POOL_CH)
    outs = []
    for gi, w in enumerate(POOL_WINDOWS):
        ugi = ug[:, :, gi, :]
        s, cnt = box_sum(ugi, w, 1)
        outs.append(s / cnt[None, :, None] - ugi)
    return jnp.stack(outs, axis=2)

def mixer_sublayer(xs, g1, shift, scale, gate, h0_f, h0_b, pool_fn, w_in, w_decay_up, b_decay,
                   gla_norm_g, w_gla_proj, pool_w, pool_scale, w_pool_proj, w_out):
    bsz, l, _ = xs.shape
    h = modulate(xs, g1, shift, scale)
    proj_kvd, q, g, pool_in, merge = split_cols(h @ w_in, ALL_COLS)
    k, v, la_f, la_b = kv_and_decay(proj_kvd, w_decay_up, b_decay)
    q = to_heads(q, GLA_DK) * (GLA_DK ** -0.5)
    o, h_f, h_b = gla_bidirectional(q, k, v, la_f, la_b, h0_f, h0_b, True)
    o = rms_norm(o, gla_norm_g).transpose(0, 2, 1, 3).reshape(bsz, l, GLA_VAL).astype(xs.dtype)
    branch_gla = (o * jax.nn.silu(g)) @ w_gla_proj
    pooled = pool_fn(pool_in)
    mixed = jnp.einsum('blgc,gcd->blgd', pooled, pool_w.astype(jnp.float32)).reshape(bsz, l, POOL_WIDTH)
    branch_pool = (mixed * pool_scale.astype(jnp.float32)).astype(xs.dtype) @ w_pool_proj
    gate_gla, gate_pool = split_cols(jax.nn.sigmoid(merge), (D_MODEL, D_MODEL))
    y = (gate_gla * branch_gla + gate_pool * branch_pool) @ w_out
    return xs + gate * y, h_f, h_b

def ec_moe(h, w_router, w_gate_e, w_up_e, w_down_e):
    l = h.shape[1]
    cap = EC_CAPACITY * l // N_EXPERTS
    aff = jax.nn.softmax((h @ w_router).astype(jnp.float32), axis=-1)
    top_aff, top_idx = lax.top_k(jnp.swapaxes(aff, 1, 2), cap)

    def per_set(hs, idx, wgt):
        xs = hs[idx]
        a = jax.nn.silu(jnp.einsum('ecd,edf->ecf', xs, w_gate_e)) * jnp.einsum('ecd,edf->ecf', xs, w_up_e)
        y = jnp.einsum('ecf,efd->ecd', a, w_down_e) * wgt[..., None].astype(hs.dtype)
        return jnp.zeros_like(hs).at[idx.reshape(-1)].add(y.reshape(-1, hs.shape[-1]))

    return jax.vmap(per_set)(h, top_idx, top_aff)

def ffn_sublayer(xs, g2, shift, scale, gate, w_router, w_gate_e, w_up_e, w_down_e):
    return xs + gate * ec_moe(modulate(xs, g2, shift, scale), w_router, w_gate_e, w_up_e, w_down_e)

def first_inputs(seed: int = 0) -> dict:
    key = jax.random.key(seed)
    ks = jax.random.split(key, 24)
    nrm = lambda k, shape, s: jax.random.normal(k, shape, jnp.float32) * s
    return {
        'x': nrm(ks[0], (BATCH, SEQ, D_MODEL), 1.0),
        'c': nrm(ks[1], (BATCH, D_MODEL), 1.0),
        'ctx': nrm(ks[2], (BATCH, CTX_LEN, D_MODEL), 1.0),
        'c_ctx': nrm(ks[3], (D_MODEL,), 1.0),
        'ada_w': nrm(ks[4], (DEPTH, D_MODEL, 6 * D_MODEL), 0.5 * D_MODEL ** -0.5),
        'ada_b': nrm(ks[5], (DEPTH, 6 * D_MODEL), 0.02),
        'norm1_g': 1.0 + nrm(ks[6], (DEPTH, D_MODEL), 0.02),
        'norm2_g': 1.0 + nrm(ks[7], (DEPTH, D_MODEL), 0.02),
        'w_in': nrm(ks[8], (DEPTH, D_MODEL, D_IN), D_MODEL ** -0.5),
        'w_decay_up': nrm(ks[9], (DEPTH, 2, GLA_RANK, GLA_KEY), GLA_RANK ** -0.5),
        'b_decay': nrm(ks[10], (DEPTH, 2, GLA_KEY), 0.1),
        'gla_norm_g': 1.0 + nrm(ks[11], (DEPTH, GLA_DV), 0.02),
        'w_gla_proj': nrm(ks[12], (DEPTH, GLA_VAL, D_MODEL), GLA_VAL ** -0.5),
        'pool_w': nrm(ks[13], (DEPTH, POOL_GROUPS, POOL_CH, POOL_CH), POOL_CH ** -0.5),
        'pool_scale': 1.0 + nrm(ks[14], (DEPTH, POOL_WIDTH), 0.1),
        'w_pool_proj': nrm(ks[15], (DEPTH, POOL_WIDTH, D_MODEL), POOL_WIDTH ** -0.5),
        'w_out': nrm(ks[16], (DEPTH, D_MODEL, D_MODEL), D_MODEL ** -0.5),
        'w_router': nrm(ks[17], (DEPTH, D_MODEL, N_EXPERTS), D_MODEL ** -0.5),
        'w_gate_e': nrm(ks[18], (DEPTH, N_EXPERTS, D_MODEL, D_EXPERT), D_MODEL ** -0.5),
        'w_up_e': nrm(ks[19], (DEPTH, N_EXPERTS, D_MODEL, D_EXPERT), D_MODEL ** -0.5),
        'w_down_e': nrm(ks[20], (DEPTH, N_EXPERTS, D_EXPERT, D_MODEL), D_EXPERT ** -0.5),
        'final_norm_g': 1.0 + nrm(ks[21], (D_MODEL,), 0.02),
    }

def first_block(x, c, ctx, c_ctx, ada_w, ada_b, norm1_g, norm2_g, w_in, w_decay_up, b_decay,
              gla_norm_g, w_gla_proj, pool_w, pool_scale, w_pool_proj, w_out, w_router,
              w_gate_e, w_up_e, w_down_e, final_norm_g):
    zero_state = jnp.zeros((ctx.shape[0], GLA_HEADS, GLA_DK, GLA_DV), jnp.float32)
    for i in range(DEPTH):
        sh1, sc1, gt1, sh2, sc2, gt2 = jnp.split((jax.nn.silu(c) @ ada_w[i] + ada_b[i])[:, None, :], 6, axis=-1)
        csh1, csc1, cgt1, csh2, csc2, cgt2 = jnp.split(jax.nn.silu(c_ctx) @ ada_w[i] + ada_b[i], 6, axis=-1)
        mix_w = (w_in[i], w_decay_up[i], b_decay[i], gla_norm_g[i], w_gla_proj[i],
                 pool_w[i], pool_scale[i], w_pool_proj[i], w_out[i])
        moe_w = (w_router[i], w_gate_e[i], w_up_e[i], w_down_e[i])
        if i == DEPTH - 1:
            h_f, h_b = context_states(ctx, norm1_g[i], csh1, csc1, w_in[i], w_decay_up[i], b_decay[i])
        else:
            ctx_mixed, h_f, h_b = mixer_sublayer(ctx, norm1_g[i], csh1, csc1, cgt1, zero_state, zero_state,
                                                 pool_context, *mix_w)
            ctx = ffn_sublayer(ctx_mixed, norm2_g[i], csh2, csc2, cgt2, *moe_w)
        x, _, _ = mixer_sublayer(x, norm1_g[i], sh1, sc1, gt1, h_f, h_b, pool_latent, *mix_w)
        x = ffn_sublayer(x, norm2_g[i], sh2, sc2, gt2, *moe_w)
    return rms_norm(x, final_norm_g)


DEPTH_2 = 2

HEAD_DIM = 64
ROPE_THETA = 10000.0
NORM_EPS = 1e-6
QUERY_BLOCK = 128
N_MEM = 256

SWA_HEADS = 8
SWA_KV_HEADS = 2
SWA_WINDOW = 128

NSA_HEADS = 8
NSA_KV_GROUPS = 2
NSA_CMP_BLOCK = 32
NSA_CMP_STRIDE = 16
NSA_SEL_BLOCK = 64
NSA_N_SEL = 16
NSA_WINDOW = 512
NSA_FORCE_BONUS = 1e4

MLA_HEADS = 8
MLA_Q_RANK = 384
MLA_KV_RANK = 256
MLA_NOPE_DIM = 64
MLA_ROPE_DIM = 32
MLA_V_DIM = 64

XATTN_HEADS = 4
XATTN_HEAD_DIM = 128

D_FF = -(-8 * D_MODEL // (3 * 256)) * 256

N_BRANCH = 3
IN_SPLITS = (
    SWA_HEADS * HEAD_DIM, SWA_KV_HEADS * HEAD_DIM, SWA_KV_HEADS * HEAD_DIM,
    NSA_HEADS * HEAD_DIM,
    NSA_KV_GROUPS * HEAD_DIM, NSA_KV_GROUPS * HEAD_DIM,
    NSA_KV_GROUPS * HEAD_DIM, NSA_KV_GROUPS * HEAD_DIM,
    NSA_KV_GROUPS * HEAD_DIM, NSA_KV_GROUPS * HEAD_DIM,
    NSA_HEADS * 3,
    MLA_Q_RANK, MLA_KV_RANK, MLA_ROPE_DIM,
    N_BRANCH * D_MODEL,
)
D_IN_2 = sum(IN_SPLITS)


def rmsnorm(x, g):
    x32 = x.astype(jnp.float32)
    y = x32 * lax.rsqrt(jnp.mean(x32 * x32, axis=-1, keepdims=True) + NORM_EPS)
    return (y * g.astype(jnp.float32)).astype(x.dtype)

def rope(x, pos):
    half = x.shape[-1] // 2
    inv_freq = ROPE_THETA ** (-jnp.arange(half, dtype=jnp.float32) / half)
    ang = pos.astype(jnp.float32)[..., None] * inv_freq
    cos, sin = jnp.cos(ang)[:, :, None, :], jnp.sin(ang)[:, :, None, :]
    x1, x2 = jnp.split(x.astype(jnp.float32), 2, axis=-1)
    return jnp.concatenate([x1 * cos - x2 * sin, x2 * cos + x1 * sin], axis=-1).astype(x.dtype)

def masked_probs(s, mask, sink=None):
    s = jnp.where(mask, s, -jnp.inf)
    m = jnp.max(s, axis=-1, keepdims=True)
    if sink is not None:
        m = jnp.maximum(m, sink)
    m = jnp.where(jnp.isfinite(m), m, 0.0)
    e = jnp.exp(s - m)
    denom = jnp.sum(e, axis=-1, keepdims=True)
    if sink is not None:
        denom = denom + jnp.exp(sink - m)
    return e / jnp.where(denom > 0, denom, 1.0)

def slice_seq(x, start, size):
    return lax.dynamic_slice_in_dim(x, start, size, axis=1)

def pad_front(x, n):
    return jnp.pad(x, ((0, 0), (n, 0), (0, 0), (0, 0)))

def blocked_map(fn, seq_len):
    out = lax.map(fn, jnp.arange(seq_len // QUERY_BLOCK) * QUERY_BLOCK)
    out = jnp.moveaxis(out, 0, 1)
    return out.reshape(out.shape[0], seq_len, *out.shape[3:])

def window_block(q, k_pad, v_pad, qs, window, sink=None):
    B, _, H, d = q.shape
    G = k_pad.shape[2]
    R = H // G
    L = window + QUERY_BLOCK
    qb = slice_seq(q, qs, QUERY_BLOCK).reshape(B, QUERY_BLOCK, G, R, d)
    kb = slice_seq(k_pad, qs, L)
    vb = slice_seq(v_pad, qs, L)
    t = qs + jnp.arange(QUERY_BLOCK)[:, None]
    kpos = qs - window + jnp.arange(L)[None, :]
    mask = (kpos <= t) & (kpos > t - window) & (kpos >= 0)
    s = jnp.einsum('bqgrd,bkgd->bgrqk', qb, kb).astype(jnp.float32) * (d ** -0.5)
    p = masked_probs(s, mask, sink)
    o = jnp.einsum('bgrqk,bkgd->bqgrd', p.astype(vb.dtype), vb)
    return o.reshape(B, QUERY_BLOCK, H, d)

def swa_mixer(q, k, v, pos, sinks):
    B, S, _ = q.shape
    q = rope(q.reshape(B, S, SWA_HEADS, HEAD_DIM), pos)
    k = pad_front(rope(k.reshape(B, S, SWA_KV_HEADS, HEAD_DIM), pos), SWA_WINDOW)
    v = pad_front(v.reshape(B, S, SWA_KV_HEADS, HEAD_DIM), SWA_WINDOW)
    sink = sinks.astype(jnp.float32).reshape(1, SWA_KV_HEADS, SWA_HEADS // SWA_KV_HEADS, 1, 1)
    o = blocked_map(lambda qs: window_block(q, k, v, qs, SWA_WINDOW, sink), S)
    return o.reshape(B, S, SWA_HEADS * HEAD_DIM)

def nsa_compress(k, pe, w1, w2):
    B, S, G, d = k.shape
    n_cmp = (S - NSA_CMP_BLOCK) // NSA_CMP_STRIDE + 1
    idx = np.arange(n_cmp)[:, None] * NSA_CMP_STRIDE + np.arange(NSA_CMP_BLOCK)[None, :]
    blk = k[:, idx] + pe[None, None, :, None, :]
    blk = jnp.swapaxes(blk, 2, 3).reshape(B, n_cmp, G, NSA_CMP_BLOCK * d)
    return jax.nn.silu(blk @ w1) @ w2

def nsa_mixer(q, kc, vc, ks, vs, kw, vw, g_logits, pos, pe_k, pe_v, wk1, wk2, wv1, wv2):
    B, S, _ = q.shape
    H, G, d = NSA_HEADS, NSA_KV_GROUPS, HEAD_DIM
    R = H // G
    shp = (B, S, G, d)
    q = q.reshape(B, S, H, d)
    q_rot = rope(q, pos)
    k_cmp = nsa_compress(kc.reshape(shp), pe_k, wk1, wk2)
    v_cmp = nsa_compress(vc.reshape(shp), pe_v, wv1, wv2)
    n_cmp = k_cmp.shape[1]
    cmp_start = np.arange(n_cmp) * NSA_CMP_STRIDE
    cmp_end = jnp.asarray(cmp_start + NSA_CMP_BLOCK - 1)
    n_slc = S // NSA_SEL_BLOCK
    sel_start = np.arange(n_slc) * NSA_SEL_BLOCK
    cover = (np.minimum(cmp_start[:, None] + NSA_CMP_BLOCK, sel_start[None, :] + NSA_SEL_BLOCK)
             - np.maximum(cmp_start[:, None], sel_start[None, :]))
    cmp_to_sel = jnp.asarray(np.clip(cover, 0, None) / NSA_CMP_STRIDE, dtype=jnp.float32)
    n_sel = min(NSA_N_SEL, n_slc)
    to_blocks = lambda a: jnp.transpose(a.reshape(B, n_slc, NSA_SEL_BLOCK, G, d), (0, 3, 1, 2, 4))
    k_sel_blk = to_blocks(rope(ks.reshape(shp), pos))
    v_sel_blk = to_blocks(vs.reshape(shp))
    k_win = pad_front(rope(kw.reshape(shp), pos), NSA_WINDOW)
    v_win = pad_front(vw.reshape(shp), NSA_WINDOW)
    gate = jax.nn.sigmoid(g_logits.astype(jnp.float32)).reshape(B, S, H, 3)
    gather = jax.vmap(jax.vmap(lambda blocks, ids: blocks[ids]))
    scale = d ** -0.5
    blk_ids = jnp.arange(n_slc)[None, :]
    m_sel = n_sel * NSA_SEL_BLOCK

    def block(qs):
        t = qs + jnp.arange(QUERY_BLOCK)
        qb = slice_seq(q, qs, QUERY_BLOCK).reshape(B, QUERY_BLOCK, G, R, d)
        s = jnp.einsum('bqgrd,bcgd->bgrqc', qb, k_cmp).astype(jnp.float32) * scale
        p_cmp = masked_probs(s, cmp_end[None, :] <= t[:, None])
        o_cmp = jnp.einsum('bgrqc,bcgd->bqgrd', p_cmp.astype(v_cmp.dtype), v_cmp)
        imp = jnp.einsum('bgqc,cj->bgqj', p_cmp.sum(axis=2), cmp_to_sel)
        cur = (t // NSA_SEL_BLOCK)[:, None]
        valid = blk_ids <= cur
        forced = (blk_ids == 0) | (blk_ids == cur) | (blk_ids == cur - 1)
        score = jnp.where(valid, imp + jnp.where(forced, NSA_FORCE_BONUS, 0.0), -jnp.inf)
        top_val, top_idx = lax.top_k(score, n_sel)
        k_g = gather(k_sel_blk, top_idx).reshape(B, G, QUERY_BLOCK, m_sel, d)
        v_g = gather(v_sel_blk, top_idx).reshape(B, G, QUERY_BLOCK, m_sel, d)
        tok = (top_idx[..., None] * NSA_SEL_BLOCK + jnp.arange(NSA_SEL_BLOCK)).reshape(B, G, QUERY_BLOCK, m_sel)
        ok = (tok <= t[:, None]) & jnp.repeat(jnp.isfinite(top_val), NSA_SEL_BLOCK, axis=-1)
        qrb = slice_seq(q_rot, qs, QUERY_BLOCK).reshape(B, QUERY_BLOCK, G, R, d)
        s = jnp.einsum('bqgrd,bgqmd->bgrqm', qrb, k_g).astype(jnp.float32) * scale
        p_sel = masked_probs(s, ok[:, :, None])
        o_sel = jnp.einsum('bgrqm,bgqmd->bqgrd', p_sel.astype(v_g.dtype), v_g)
        o_win = window_block(q_rot, k_win, v_win, qs, NSA_WINDOW)
        g = slice_seq(gate, qs, QUERY_BLOCK).astype(q.dtype)
        return (g[..., 0:1] * o_cmp.reshape(B, QUERY_BLOCK, H, d)
                + g[..., 1:2] * o_sel.reshape(B, QUERY_BLOCK, H, d)
                + g[..., 2:3] * o_win)

    return blocked_map(block, S).reshape(B, S, H * d)

def mla_mixer(q_lat, kv_lat, k_rot, pos, q_norm, w_q_b, kv_norm, w_kv_b):
    B, S, _ = q_lat.shape
    H = MLA_HEADS
    q = (rmsnorm(q_lat, q_norm) @ w_q_b).reshape(B, S, H, MLA_NOPE_DIM + MLA_ROPE_DIM)
    q_nope, q_pe = q[..., :MLA_NOPE_DIM], rope(q[..., MLA_NOPE_DIM:], pos)
    kv = (rmsnorm(kv_lat, kv_norm) @ w_kv_b).reshape(B, S, H, MLA_NOPE_DIM + MLA_V_DIM)
    k_nope, v = kv[..., :MLA_NOPE_DIM], kv[..., MLA_NOPE_DIM:]
    k_pe = rope(k_rot[:, :, None, :], pos)[:, :, 0]
    scale = (MLA_NOPE_DIM + MLA_ROPE_DIM) ** -0.5
    kpos = jnp.arange(S)[None, :]

    def block(qs):
        t = qs + jnp.arange(QUERY_BLOCK)[:, None]
        qn = slice_seq(q_nope, qs, QUERY_BLOCK)
        qp = slice_seq(q_pe, qs, QUERY_BLOCK)
        s = (jnp.einsum('bqhd,bkhd->bhqk', qn, k_nope)
             + jnp.einsum('bqhd,bkd->bhqk', qp, k_pe)).astype(jnp.float32) * scale
        p = masked_probs(s, kpos <= t)
        return jnp.einsum('bhqk,bkhd->bqhd', p.astype(v.dtype), v)

    return blocked_map(block, S).reshape(B, S, H * MLA_V_DIM)

def cross_attn(hx, hm, w_q, w_kv, w_o):
    B, S, _ = hx.shape
    M = hm.shape[1]
    q = (hx @ w_q).reshape(B, S, XATTN_HEADS, XATTN_HEAD_DIM)
    kv = (hm @ w_kv).reshape(B, M, 2, XATTN_HEADS, XATTN_HEAD_DIM)
    k, v = kv[:, :, 0], kv[:, :, 1]
    s = jnp.einsum('bshd,bmhd->bhsm', q, k).astype(jnp.float32) * (XATTN_HEAD_DIM ** -0.5)
    p = jax.nn.softmax(s, axis=-1)
    o = jnp.einsum('bhsm,bmhd->bshd', p.astype(v.dtype), v)
    return o.reshape(B, S, XATTN_HEADS * XATTN_HEAD_DIM) @ w_o

def second_inputs(seed: int = 0) -> dict:
    key = jax.random.key(seed)
    ks = iter(jax.random.split(key, 32))
    f32 = jnp.float32
    L = DEPTH_2

    def dense(shape, fan_in):
        return jax.random.normal(next(ks), shape, f32) * fan_in ** -0.5

    def gain(shape):
        return 1.0 + 0.1 * jax.random.normal(next(ks), shape, f32)

    x = jax.random.normal(next(ks), (BATCH, SEQ, D_MODEL), f32)
    mem = jax.random.normal(next(ks), (BATCH, N_MEM, D_MODEL), f32)
    positions = (jnp.arange(SEQ, dtype=jnp.int32)[None, :]
                 + jax.random.randint(next(ks), (BATCH, 1), 0, 4096, dtype=jnp.int32))
    cmp_in = NSA_CMP_BLOCK * HEAD_DIM
    return {
        'x': x,
        'mem': mem,
        'positions': positions,
        'norm_mix': gain((L, D_MODEL)),
        'w_in': dense((L, D_MODEL, D_IN_2), D_MODEL),
        'swa_sinks': jax.random.normal(next(ks), (L, SWA_HEADS), f32),
        'nsa_pe_k': 0.1 * jax.random.normal(next(ks), (L, NSA_CMP_BLOCK, HEAD_DIM), f32),
        'nsa_pe_v': 0.1 * jax.random.normal(next(ks), (L, NSA_CMP_BLOCK, HEAD_DIM), f32),
        'nsa_wk1': dense((L, cmp_in, HEAD_DIM), cmp_in),
        'nsa_wk2': dense((L, HEAD_DIM, HEAD_DIM), HEAD_DIM),
        'nsa_wv1': dense((L, cmp_in, HEAD_DIM), cmp_in),
        'nsa_wv2': dense((L, HEAD_DIM, HEAD_DIM), HEAD_DIM),
        'mla_q_norm': gain((L, MLA_Q_RANK)),
        'mla_w_q_b': dense((L, MLA_Q_RANK, MLA_HEADS * (MLA_NOPE_DIM + MLA_ROPE_DIM)), MLA_Q_RANK),
        'mla_kv_norm': gain((L, MLA_KV_RANK)),
        'mla_w_kv_b': dense((L, MLA_KV_RANK, MLA_HEADS * (MLA_NOPE_DIM + MLA_V_DIM)), MLA_KV_RANK),
        'w_br_a': dense((L, SWA_HEADS * HEAD_DIM, D_MODEL), SWA_HEADS * HEAD_DIM),
        'w_br_b': dense((L, NSA_HEADS * HEAD_DIM, D_MODEL), NSA_HEADS * HEAD_DIM),
        'w_br_c': dense((L, MLA_HEADS * MLA_V_DIM, D_MODEL), MLA_HEADS * MLA_V_DIM),
        'w_out': dense((L, D_MODEL, D_MODEL), D_MODEL),
        'norm_xattn': gain((L, D_MODEL)),
        'norm_mem': gain((L, D_MODEL)),
        'w_xq': dense((L, D_MODEL, XATTN_HEADS * XATTN_HEAD_DIM), D_MODEL),
        'w_xkv': dense((L, D_MODEL, 2 * XATTN_HEADS * XATTN_HEAD_DIM), D_MODEL),
        'w_xo': dense((L, XATTN_HEADS * XATTN_HEAD_DIM, D_MODEL), XATTN_HEADS * XATTN_HEAD_DIM),
        'norm_ffn': gain((L, D_MODEL)),
        'w_gate_up': dense((L, D_MODEL, 2 * D_FF), D_MODEL),
        'w_down': dense((L, D_FF, D_MODEL), D_FF),
        'norm_final': gain((D_MODEL,)),
    }

def second_block(x, mem, positions, norm_mix, w_in, swa_sinks, nsa_pe_k, nsa_pe_v, nsa_wk1, nsa_wk2,
              nsa_wv1, nsa_wv2, mla_q_norm, mla_w_q_b, mla_kv_norm, mla_w_kv_b, w_br_a, w_br_b,
              w_br_c, w_out, norm_xattn, norm_mem, w_xq, w_xkv, w_xo, norm_ffn, w_gate_up, w_down,
              norm_final):
    B, S, D = x.shape
    offsets = np.cumsum(IN_SPLITS)[:-1].tolist()
    for l in range(DEPTH_2):
        h = rmsnorm(x, norm_mix[l])
        (a_q, a_k, a_v, b_q, b_kc, b_vc, b_ks, b_vs, b_kw, b_vw, b_g,
         c_qa, c_kv, c_kr, g_br) = jnp.split(h @ w_in[l], offsets, axis=-1)
        o_a = swa_mixer(a_q, a_k, a_v, positions, swa_sinks[l])
        o_b = nsa_mixer(b_q, b_kc, b_vc, b_ks, b_vs, b_kw, b_vw, b_g, positions,
                        nsa_pe_k[l], nsa_pe_v[l], nsa_wk1[l], nsa_wk2[l], nsa_wv1[l], nsa_wv2[l])
        o_c = mla_mixer(c_qa, c_kv, c_kr, positions, mla_q_norm[l], mla_w_q_b[l],
                        mla_kv_norm[l], mla_w_kv_b[l])
        g = jax.nn.sigmoid(g_br.astype(jnp.float32)).reshape(B, S, N_BRANCH, D).astype(x.dtype)
        merged = (g[:, :, 0] * (o_a @ w_br_a[l])
                  + g[:, :, 1] * (o_b @ w_br_b[l])
                  + g[:, :, 2] * (o_c @ w_br_c[l]))
        x = x + merged @ w_out[l]
        x = x + cross_attn(rmsnorm(x, norm_xattn[l]), rmsnorm(mem, norm_mem[l]),
                           w_xq[l], w_xkv[l], w_xo[l])
        h = rmsnorm(x, norm_ffn[l])
        gate_h, up_h = jnp.split(h @ w_gate_up[l], 2, axis=-1)
        x = x + (jax.nn.silu(gate_h) * up_h) @ w_down[l]
    return rmsnorm(x, norm_final)


def setup_inputs(seed=0):
    out = dict(first_inputs(seed))
    for name, value in second_inputs(seed + 1).items():
        if name != "x":
            out[name + "_2"] = value
    return out


def reference(
    x, c, ctx, c_ctx, ada_w, ada_b, norm1_g, norm2_g, w_in, w_decay_up, b_decay, gla_norm_g,
    w_gla_proj, pool_w, pool_scale, w_pool_proj, w_out, w_router, w_gate_e, w_up_e, w_down_e,
    final_norm_g, mem_2, positions_2, norm_mix_2, w_in_2, swa_sinks_2, nsa_pe_k_2, nsa_pe_v_2,
    nsa_wk1_2, nsa_wk2_2, nsa_wv1_2, nsa_wv2_2, mla_q_norm_2, mla_w_q_b_2, mla_kv_norm_2,
    mla_w_kv_b_2, w_br_a_2, w_br_b_2, w_br_c_2, w_out_2, norm_xattn_2, norm_mem_2, w_xq_2,
    w_xkv_2, w_xo_2, norm_ffn_2, w_gate_up_2, w_down_2, norm_final_2,
):
    x = first_block(
        x, c, ctx, c_ctx, ada_w, ada_b, norm1_g, norm2_g, w_in, w_decay_up, b_decay, gla_norm_g,
        w_gla_proj, pool_w, pool_scale, w_pool_proj, w_out, w_router, w_gate_e, w_up_e,
        w_down_e, final_norm_g,
    )
    return second_block(
        x, mem_2, positions_2, norm_mix_2, w_in_2, swa_sinks_2, nsa_pe_k_2, nsa_pe_v_2,
        nsa_wk1_2, nsa_wk2_2, nsa_wv1_2, nsa_wv2_2, mla_q_norm_2, mla_w_q_b_2, mla_kv_norm_2,
        mla_w_kv_b_2, w_br_a_2, w_br_b_2, w_br_c_2, w_out_2, norm_xattn_2, norm_mem_2, w_xq_2,
        w_xkv_2, w_xo_2, norm_ffn_2, w_gate_up_2, w_down_2, norm_final_2,
    )


_drawn_inputs = setup_inputs


def setup_inputs(seed=0):
    import zlib

    import numpy as np

    out = dict(_drawn_inputs(seed))
    spreads = {}
    factors = {'ctx': 2.72,
     'c_ctx': 3.761,
     'norm1_g': 6.382,
     'norm2_g': 7.023,
     'b_decay': 6.935,
     'gla_norm_g': 8.0,
     'swa_sinks_2': 5.187,
     'nsa_pe_k_2': 8.0,
     'nsa_pe_v_2': 2.712,
     'mla_q_norm_2': 4.65,
     'mla_kv_norm_2': 2.802,
     'norm_xattn_2': 3.425}
    for name, (base, spread) in spreads.items():
        noise = np.random.default_rng([zlib.crc32(name.encode()), seed]).standard_normal(out[name].shape)
        drawn = base * np.exp(spread * noise) if base else spread * noise
        out[name] = jnp.asarray(drawn.astype(out[name].dtype))
    for name, factor in factors.items():
        out[name] = (out[name] * factor).astype(out[name].dtype)
    return out
```

```python
from contextlib import ExitStack

import concourse.bass as bass
from concourse import mybir
import numpy as np

F32 = mybir.dt.float32
I32 = mybir.dt.int32
U32 = mybir.dt.uint32
ALU = mybir.AluOpType
ACT = mybir.ActivationFunctionType
AX = mybir.AxisListType

P = 128
T, D, CTX, MEM = 512, 1024, 256, 256
KD, TT = D // P, T // P
DKH, DV, CHUNK = 64, 128, 64
WINDOWS = (2, 4, 8, 16)
ROWS, COLS = T // 64, 64
E, CAP, FE = 16, 2 * T // 16, 1024
LAYERS = 2
HEADS, HD = 8, 64
NCMP = (T - 32) // 16 + 1
FF = 2816
NFF = FF // P
MLA_D, MLA_R, MLA_C = 96, 384, 256
EPS = 1e-6
MASKED = -1e30

SLOT = 16
RING = 4
TILES_ONE = 384 + (4 + 2 + 1 + 2 + 4) * 8 + 32 + 8 * 2 * 12 + 64
TILES_EXPERT = 3 * 64
TILES_LAYER = ((5 + 2 + 6 + 1 + 5) * 8 + 32 + 64 + 24 + 16 + 8 + 3 * 8 * 12 + 64 + 4 * 32
               + NFF * 16 + NFF * 8)


def slots_of(tiles):
    return -(-tiles // (SLOT * RING)) * RING


SLOTS_ONE, SLOTS_EXPERT, SLOTS_LAYER = slots_of(TILES_ONE), TILES_EXPERT // SLOT, slots_of(TILES_LAYER)
SLOTS = SLOTS_ONE + E * SLOTS_EXPERT + LAYERS * SLOTS_LAYER


def numbered(stages):
    first, n = {}, 0
    for name, count in stages:
        first[name] = n
        n += count
    return first, n


ONE, N_ONE = numbered([
    ("ada", 3), ("adaT", 3), ("rms_x", 1), ("rms_c", 1), ("pool", 4), ("k", 4), ("r", 2), ("q", 2), ("v", 6), ("g", 4),
    ("poolw", 4), ("zk", 16), ("kv", 22), ("s", 16), ("rms_o", 4), ("merge", 32), ("out", 8),
    ("rms_2", 1), ("h2k", 8), ("logits", 1), ("affT", 1), ("slotT", 1), ("gather", 16), ("selw", 16), ("scatter", 8),
    ("rms_f", 1)])
LAY, N_LAY = numbered([
    ("rms_mix", 1), ("a_fm", 10), ("v", 4), ("ot0", 4), ("merge0", 16),
    ("kcvc", 2), ("b_fm", 12), ("cmp", 4), ("ot1", 4), ("merge1", 16),
    ("kr", 2), ("lat", 5), ("rms_q", 1), ("rms_kv", 1), ("q_fm", 16), ("k_fm", 8), ("v_mla", 4),
    ("ot2", 4), ("merge2", 16), ("out", 8),
    ("rms_x", 1), ("rms_m", 1), ("xq", 4), ("xk", 4), ("xv", 2), ("ot3", 4), ("xo", 8),
    ("rms_f", 1), ("gu", 2 * NFF), ("down", 8)])
BANKS = 3
BANK0 = 5


def rope_order(n):
    order = [("raw", 0)]
    for j in range(n):
        if j + 1 < n:
            order.append(("raw", j + 1))
        order.append(("perm", j))
    return order


def columns(parts):
    at, n = {}, 0
    for name, width in parts:
        at[name] = (n, width)
        n += width
    return at, n


CST, N_CST = columns([("ident", P), ("ones", P), ("causal", P), ("recent", P), ("perm", P), ("permM", P),
                      ("cmp_add", TT * NCMP), ("cmp_mul", TT * NCMP), ("freq", 1), ("freqM", 1),
                      ("sign", 1), ("signM", 1), ("eps", 1)])
CS1, N_CS1 = columns([("maskf", P), ("maskb", P), ("scan", 768)])
CSE, N_CSE = columns([("iota", CAP), ("cidx", 1), ("pairsel", 8 * P)])
PR1, N_PR1 = columns([("ada_b", 48), ("g1", 8), ("g2", 8), ("b_decay", 4), ("gn", 1), ("pool_scale", 4),
                      ("gf", 8), ("gfinal", 8), ("wup", 512), ("wrouter", 128), ("poolw", 512), ("c2", 16)])
PR2, N_PR2 = columns([("norm_mix", 8), ("norm_x", 8), ("norm_mem", 8), ("norm_ffn", 8), ("qn", 3), ("kvn", 2),
                      ("sinks", 8), ("pek", 32), ("pev", 32), ("w2k", P), ("w2v", P)])


def constants():
    c = np.zeros((P, N_CST), np.float32)
    r = np.arange(P)

    def put(arr, at, name, v):
        o, w = at[name]
        arr[:, o:o + w] = v

    put(c, CST, "ident", np.eye(P))
    put(c, CST, "ones", 1.0)
    put(c, CST, "causal", np.where(r[None, :] <= r[:, None], 0.0, MASKED))
    put(c, CST, "recent", np.where(r[None, :] > r[:, None], 0.0, MASKED))
    perm = np.zeros((P, P), np.float32)
    for m in range(P):
        perm[(m // 64) * 64 + (m % 64 + 32) % 64, m] = 1.0
    put(c, CST, "perm", perm)
    perm = np.zeros((P, P), np.float32)
    for m in range(64, 96):
        perm[64 + (m - 64 + 16) % 32, m] = 1.0
    put(c, CST, "permM", perm)
    t = np.arange(T).reshape(TT, P)
    ok = (16 * np.arange(NCMP)[None, None, :] + 31) <= t[:, :, None]
    put(c, CST, "cmp_add", np.where(ok, 0.0, MASKED).transpose(1, 0, 2).reshape(P, -1))
    put(c, CST, "cmp_mul", ok.astype(np.float32).transpose(1, 0, 2).reshape(P, -1))
    f = (np.float32(10000.0) ** (-np.arange(32, dtype=np.float32) / np.float32(32))).astype(np.float32)
    put(c, CST, "freq", f[r % 32][:, None])
    f = (np.float32(10000.0) ** (-np.arange(16, dtype=np.float32) / np.float32(16))).astype(np.float32)
    put(c, CST, "freqM", np.where((r >= 64) & (r < 96), f[r % 16], 0.0)[:, None])
    put(c, CST, "sign", np.where(r % 64 < 32, -1.0, 1.0)[:, None])
    put(c, CST, "signM", np.where(r % 32 < 16, -1.0, 1.0)[:, None])
    put(c, CST, "eps", EPS)
    c1 = np.zeros((P, N_CS1), np.float32)
    same = (r[:, None] // CHUNK) == (r[None, :] // CHUNK)
    put(c1, CS1, "maskf", same & (r[:, None] <= r[None, :]))
    put(c1, CS1, "maskb", same & (r[:, None] >= r[None, :]))
    put(c1, CS1, "scan", (np.arange(768) % CHUNK != 0)[None, :])
    ce = np.zeros((P, N_CSE), np.float32)
    put(ce, CSE, "iota", np.arange(CAP)[None, :])
    put(ce, CSE, "cidx", (r % CAP)[:, None])
    sel = np.zeros((P, 8, P), np.float32)
    for p in range(8):
        sel[2 * p, p, :64] = 1.0
        sel[2 * p + 1, p, 64:] = 1.0
    put(ce, CSE, "pairsel", sel.reshape(P, -1))
    inv = np.zeros((4, ROWS, COLS), np.float32)
    for i, w in enumerate(WINDOWS):
        n = [np.clip(np.arange(m) + w // 2, 0, m) - np.clip(np.arange(m) - w // 2, 0, m) for m in (ROWS, COLS)]
        inv[i] = 1.0 / (n[0][:, None] * n[1][None, :])
    return c, c1, ce, np.ascontiguousarray(np.broadcast_to(inv.reshape(1, -1), (P, 4 * T)))


def two_blocks(nc, stream, xT_d, ctxT_d, memT_d, pos_d, cst_d, cs1_d, cse_d, inv_d, pr1_d, pr2_d, out_d):
    ctx = ExitStack()
    with ctx:
        def sb(name, shape, dt=F32):
            return ctx.enter_context(nc.sbuf_tensor(name, shape, dt))

        def sem(name):
            return ctx.enter_context(nc.semaphore(name))

        x = sb("x", [P, KD, T])
        h = sb("h", [P, KD, T])
        ring = sb("ring", [P, RING, SLOT * P])
        cst = sb("cst", [P, N_CST])
        gfinal = sb("gfinal", [P, KD])
        sq = sb("sq", [P, 2, T])
        rstd = sb("rstd", [P, 2, T])
        sig = sb("sig", [P, 2, T])
        tmp = sb("tmp", [P, T])
        y = sb("y", [P, KD, T])
        bank = ctx.enter_context(nc.psum_tensor("bank", [P, 8, 512], F32))

        ARENA = 28096
        arena = sb("arena", [P, ARENA])
        where = [0]

        def carve(n, dims=None, **sizes):
            a = arena[:, where[0]:where[0] + n]
            where[0] += n
            assert where[0] <= ARENA, where[0]
            return a.rearrange(dims, **sizes) if dims else a

        pr1 = carve(N_PR1)
        mods = carve(96, "p (n c) -> p n c", c=2)
        amp = carve(24, "p (s n) -> p s n", s=3)
        moe_from = where[0]
        cs1 = carve(N_CS1)
        c2 = carve(KD * 32, "p (k c) -> p k c", k=KD)
        hc = carve(2048, "p (k t) -> p k t", k=KD)
        qe = hc.rearrange("p k t -> p (k t)").rearrange("p (d t) -> p d t", d=4)
        kq = carve(2560)
        kall = kq[:, 0:1536].rearrange("p (m t) -> p m t", m=2)
        qx = kq[:, 1536:2560].rearrange("p (m t) -> p m t", m=2)
        osq = kq[:, 0:2048].rearrange("p (m t) -> p m t", m=4)
        vall = carve(3072, "p (m t) -> p m t", m=6)
        rbuf = sig[:, :, :].rearrange("p b t -> p (b t)")[:, 0:768]
        pmask = rbuf[:, 0:512].rearrange("p (b d i) -> p b d i", b=2, d=2)
        las = carve(3 * 768, "p (m t) -> p m t", m=3)
        kd = carve(768)
        oT = arena[:, where[0] - 3072:where[0] - 1024].rearrange("p (m t) -> p m t", m=4)
        qm = carve(2048, "p (d t) -> p d t", d=4)
        km = carve(2048, "p (d t) -> p d t", d=4)
        decay = carve(48, "p (d c) -> p d c", d=4)
        gT = carve(2048, "p (m t) -> p m t", m=4)
        mixT = carve(2048, "p (m t) -> p m t", m=4)
        adar = arena[:, where[0] - 2048:where[0] - 512].rearrange("p (i n) -> p i n", i=3)
        poolreg = carve(6144)
        SS = poolreg.rearrange("p (d c e) -> p d c e", d=4, c=12)
        pu = [poolreg[:, 640 * (g % 2):640 * (g % 2) + 640] for g in range(4)]
        pa = [poolreg[:, 1280 + 1920 * b:1280 + 1920 * (b + 1)] for b in range(2)]
        posi = y[:, 7, :].bitcast(I32)
        yflat = y[:, :, :].rearrange("p k t -> p (k t)")
        inv = yflat[:, 0:2048].rearrange("p (g t) -> p g t", g=4)
        pT = yflat[:, 2048:4096].rearrange("p (g t) -> p g t", g=4)
        kdT = yflat[:, 0:3072].rearrange("p (m d c) -> p m d c", m=6, d=4)

        where[0] = moe_from
        cse = carve(N_CSE)
        h2k = carve(4096, "p (m n) -> p m n", m=TT)
        xs_all = carve(8 * D, "p (e k c) -> p e k c", e=8, k=KD)
        yexp = xs_all.rearrange("p e k c -> p e (k c)")
        xsT = carve(D, "p (k c) -> p k c", k=KD)
        sg = carve(2 * 512, "p (b n) -> p b n", b=2)
        acts = carve(FE)
        aT = carve(FE, "p (k c) -> p k c", k=8)
        selx = carve(TT * E * CAP, "p (m e c) -> p m e c", m=TT, e=E)
        selw = arena[:, where[0] - 8 * T:where[0]].rearrange("p (e t) -> p e t", e=8)
        rows = carve(4 * T, "p (a t) -> p a t", a=4)
        affT, work, slot, mark = [rows[0:E, i, :] for i in range(4)]
        aff = carve(3 * TT * E, "p (a m e) -> p a m e", a=3, m=TT)
        stat = carve(2 * TT, "p (a m) -> p a m", a=2)
        slot_tok = carve(TT * E, "p (m e) -> p m e", m=TT)
        top8 = carve(8)[0:E, :]

        where[0] = 0
        cosT, sinT, cosM, sinM = [carve(T) for _ in range(4)]
        pr2 = carve(N_PR2)
        Q = carve(4096, "p (m t) -> p m t", m=8)
        K = carve(4096, "p (m t) -> p m t", m=8)
        V = carve(2048)
        vtok = V[:, 0:TT * 408].rearrange("p (m n) -> p m n", m=TT)
        vmla = V.rearrange("p (m n) -> p m n", m=TT)
        lat = carve(3072, "p (m t) -> p m t", m=6)
        OT = carve(2048, "p (m t) -> p m t", m=4)
        otok = carve(1024, "p (b n) -> p b n", b=2)
        probs = carve(3 * T, "p (b n) -> p b n", b=3)
        probsT = carve(2 * T, "p (b n) -> p b n", b=2)
        rope1 = carve(2 * T, "p (b n) -> p b n", b=2)
        rope2 = carve(T)
        sgate = carve(TT * 24, "p (m n) -> p m n", m=TT)
        cmpb = carve(32 * NCMP, "p (j c) -> p j c", j=32)
        cmp1 = carve(4 * 32, "p (b n) -> p b n", b=4)
        vcmp = carve(P)
        small = carve(6 * 8, "p (a n) -> p a n", a=6)
        nmax, nbias, den, esink, rden, coef = [small[:, i, :] for i in range(6)]
        nsink = carve(8)
        act_ff = arena[:, N_PR2 + 4 * T:N_PR2 + 4 * T + NFF * T].rearrange("p (f t) -> p f t", f=NFF)
        hm = y[:, 0:4, :].rearrange("p k t -> p (k t)").rearrange("p (k t) -> p k t", k=KD)
        mem = lat[:, 0:4, :].rearrange("p k t -> p (k t)").rearrange("p (k t) -> p k t", k=KD)

        def c_(name):
            o, w = CST[name]
            return cst[:, o:o + w]

        def p1(name, i=None):
            o, w = PR1[name]
            return pr1[:, o:o + w] if i is None else pr1[:, o + i:o + i + 1]

        def p2(name, i=None):
            o, w = PR2[name]
            return pr2[:, o:o + w] if i is None else pr2[:, o + i:o + i + 1]

        def ce_(name):
            o, w = CSE[name]
            return cse[:, o:o + w]

        landed = [sem(f"landed{i}") for i in range(RING)]
        slot_read = sem("slot_read")
        loaded = sem("loaded")
        loaded_inv = sem("loaded_inv")
        loaded_moe = sem("loaded_moe")
        loaded_pos = sem("loaded_pos")
        loaded_pr2 = sem("loaded_pr2")
        loaded_mem = sem("loaded_mem")
        made1, taken1 = sem("made1"), sem("taken1")
        made2, taken2 = sem("made2"), sem("taken2")
        c2_zero, c2_ready = sem("c2_zero"), sem("c2_ready")
        squared, summed = sem("squared"), sem("summed")
        rstd_made = sem("rstd_made")
        h_made = sem("h_made")
        ctx_made = sem("ctx_made")
        gates_made = sem("gates_made")
        pool_in = sem("pool_in")
        pooled = sem("pooled")
        pool_zero = sem("pool_zero")
        la_in, la_abs, la_log = sem("la_in"), sem("la_abs"), sem("la_log")
        expo_in, expo_out = sem("expo_in"), sem("expo_out")
        kd_made = sem("kd_made")
        gla_ops = sem("gla_ops")
        state_made = sem("state_made")
        masked = sem("masked")
        intra_done = sem("intra_done")
        heads_done = sem("heads_done")
        o_squared = sem("o_squared")
        rstd_o = sem("rstd_o")
        o_made = sem("o_made")
        affx, affe = sem("affx"), sem("affe")
        aff_made, slot_made = sem("aff_made"), sem("slot_made")
        sel_ready, xs_taken = sem("sel_ready"), sem("xs_taken")
        gate_made, up_made, silu_made = sem("gate_made"), sem("up_made"), sem("silu_made")
        a_ready, y_made, y_taken = sem("a_ready"), sem("y_made"), sem("y_taken")
        a_turned, aT_ready = sem("a_turned"), sem("aT_ready")
        x_made = sem("x_made")
        ang_made, sin_made = sem("ang_made"), sem("sin_made")
        layer_done = sem("layer_done")
        scored, biased, exped, cmp_masked = sem("scored"), sem("biased"), sem("exped"), sem("cmp_masked")
        turned, turned_out, pv_made, o_taken = sem("turned"), sem("turned_out"), sem("pv_made"), sem("o_taken")
        tok_done = sem("tok_done")
        sgate_made = sem("sgate_made")
        blocks_made, cmp_silu = sem("blocks_made"), sem("cmp_silu")
        lat_normed = sem("lat_normed")
        kheads_made = sem("kheads_made")
        out_sem = sem("out_sem")
        out_ready = sem("out_ready")

        class Numbers:

            def __init__(self, first, made_sem, taken_sem, base):
                self.first, self.made_sem, self.taken_sem, self.base = first, made_sem, taken_sem, base

            def no(self, name, t=0):
                return self.first[name] + t

            def bank(self, n):
                return bank[:, BANK0 + n % BANKS, :]

            def wait_made(self, eng, n):
                eng.wait_ge(self.made_sem, self.base + n + 1)

            def wait_taken(self, eng, n):
                eng.wait_ge(self.taken_sem, self.base + n + 1)

        def units():
            out = []
            for qt in range(TT):
                for hh in range(HEADS):
                    g, t = hh // 4, hh % 4
                    r = slice(64 * g, 64 * g + 64)
                    k0 = max(0, qt - 1)
                    out.append(dict(sec=0, qt=qt, h=hh, q=Q[r, t, P * qt:P * qt + P], k=K[r, 0, P * k0:P * (qt + 1)],
                                    nk=P * (qt + 1 - k0), scale=HD ** -0.5, kind="window",
                                    v=[vtok[:, j, 0:P] for j in range(k0, qt + 1)], vc=64 * g, sink=hh,
                                    gate=None, first=True, col=64 * hh, last=hh == HEADS - 1))
            for qt in range(TT):
                for branch in range(3):
                    for hh in range(HEADS):
                        g, t = hh // 4, hh % 4
                        r = slice(64 * g, 64 * g + 64)
                        u = dict(sec=1, qt=qt, h=hh, scale=HD ** -0.5, sink=None, gate=(qt, 3 * hh + branch),
                                 first=branch == 0, col=64 * hh, last=branch == 2 and hh == HEADS - 1)
                        if branch == 0:
                            u.update(q=Q[r, t, P * qt:P * qt + P], k=cmp1[r, 2, 0:NCMP], nk=NCMP, kind="cmp",
                                     v=[vcmp[0:NCMP, :]], vc=64 * g)
                        else:
                            u.update(q=Q[r, 4 + t, P * qt:P * qt + P], k=K[r, branch - 1, 0:P * (qt + 1)],
                                     nk=P * (qt + 1), kind="causal", vc=64 * g,
                                     v=[vtok[:, j, P * branch:P * branch + P] for j in range(qt + 1)])
                        out.append(u)
            for qt in range(TT):
                for hh in range(HEADS):
                    out.append(dict(sec=2, qt=qt, h=hh, q=Q[0:MLA_D, hh, P * qt:P * qt + P],
                                    k=K[0:MLA_D, hh, 0:P * (qt + 1)], nk=P * (qt + 1), scale=MLA_D ** -0.5,
                                    kind="causal", v=[vmla[:, j, P * (hh // 2):P * (hh // 2) + P] for j in range(qt + 1)],
                                    vc=64 * (hh % 2),
                                    sink=None, gate=None, first=True, col=64 * hh, last=hh == HEADS - 1))
            for qt in range(TT):
                for hh in range(4):
                    out.append(dict(sec=3, qt=qt, h=hh, q=Q[:, hh, P * qt:P * qt + P], k=K[:, hh, 0:MEM], nk=MEM,
                                    scale=P ** -0.5, kind="full",
                                    v=[vmla[:, j, P * hh:P * hh + P] for j in range(2)], vc=0,
                                    sink=None, gate=None, first=True, col=P * hh, last=hh == 3))
            for i, u in enumerate(out):
                u["n"] = i
                u["nb"] = -(-u["nk"] // P)
                u["w"] = 128 if u["sec"] == 3 else 64
            return out

        UNITS = units()
        N_UNITS = len(UNITS)
        SECTION = [[u for u in UNITS if u["sec"] == s] for s in range(4)]
        N_CMPU = sum(u["kind"] == "cmp" for u in UNITS)
        cmp_no = {u["n"]: i for i, u in enumerate(u for u in UNITS if u["kind"] == "cmp")}

        block = ctx.enter_context(nc.Block())

        @block.sync
        def _(sp):
            def load(j, s):
                sp.dma_start(ring[:, s, :], stream[bass.ds(j * RING + s, 1)].rearrange("a p n -> p (a n)")
                             ).then_inc(landed[s], 16)
            for s in range(RING):
                sp.dma_start(ring[:, s, :], stream[s]).then_inc(landed[s], 16)
            with sp.Fori(1, SLOTS // RING) as j:
                for s in range(RING):
                    sp.wait_ge(slot_read, j * RING + (s - RING + 1))
                    load(j, s)

        @block.tensor
        def _(pe):
            class Weights:

                def __init__(self, slots_before):
                    self.rot0, self.pos, self.seen, self.back = slots_before, 0, 0, 0

                def tile(self, n=1):
                    s = self.pos // SLOT
                    assert (self.pos + n - 1) // SLOT == s
                    if s == self.seen:
                        pe.wait_ge(landed[s % RING], self.rot0 * 16 + 16 * (s // RING + 1))
                        self.seen += 1
                    a = ring[:, s % RING, (self.pos % SLOT) * P:(self.pos % SLOT + n) * P]
                    self.pos += n
                    return a

                def pending(self):
                    done = self.pos // SLOT - self.back
                    self.back += done
                    return done

                def finish(self, tiles, slots):
                    assert self.pos == tiles, (self.pos, tiles)
                    while self.seen < slots:
                        pe.wait_ge(landed[self.seen % RING], self.rot0 * 16 + 16 * (self.seen // RING + 1))
                        pe.matmul(bank[0:2, 4, 0:2], ring[:, self.seen % RING, 0:2], ring[:, self.seen % RING, 0:2],
                                  start=True, stop=True)
                        self.seen += 1
                    n = slots - self.back
                    if n:
                        pe.drain().then_inc(slot_read, n)

            W = [None]
            N = [None]

            def mm(out, lhsT, rhs, start, stop, loose=False, hold=False):
                ins = pe.matmul(out, lhsT, rhs, start=start, stop=stop, skip_group_check=loose)
                return ins

            def release():
                n = W[0].pending()
                if n:
                    pe.drain().then_inc(slot_read, n)

            def begin(n):
                if n >= BANKS:
                    N[0].wait_taken(pe, n - BANKS)
                return N[0].bank(n)

            def gemm(n, rhs, nk, width=T, m=P):
                b = begin(n)
                for k in range(nk):
                    ins = mm(b[0:m, 0:width], W[0].tile(), rhs(k), k == 0, k == nk - 1)
                ins.then_inc(N[0].made_sem, 1)
                release()

            def gemm_tok(n0, lhs, count, nk, width):
                quads = [W[0].tile(4) for _ in range(nk)]
                for m in range(count):
                    b = begin(n0 + m)
                    for k in range(nk):
                        ins = mm(b[:, 0:width], lhs(k, m), quads[k][:, 0:width], k == 0, k == nk - 1)
                    ins.then_inc(N[0].made_sem, 1)
                release()

            def rms_sum(n, sq0, nk, width=T):
                b = begin(n)
                for k in range(nk):
                    pe.wait_ge(squared, sq0 + k + 1)
                    ins = mm(b[:, 0:width], c_("ones"), sq[:, k % 2, 0:width], k == 0, k == nk - 1)
                    ins.then_inc(summed, 1)
                pe.drain().then_inc(N[0].made_sem, 1)

            W[0] = Weights(0)
            N[0] = Numbers(ONE, made1, taken1, 0)
            n1 = N[0].no
            pe.wait_ge(c2_ready, 1)
            for i in range(3):
                b = begin(n1("ada", i))
                for k in range(KD):
                    for j in range(4):
                        ins = mm(b[32 * j:32 * j + 32, :], c2[:, k, :], W[0].tile(4), k == 0, k == KD - 1)
                    if k < KD - 1:
                        release()
                ins.then_inc(made1, 1)
                release()
            for i in range(3):
                N[0].wait_taken(pe, n1("ada", i))
                b = begin(n1("adaT", i))
                for q in range(4):
                    ins = pe.transpose(b[:, P * q:P * q + P], adar[:, i, P * q:P * q + P], c_("ident"))
                ins.then_inc(made1, 1)
            rms_sum(n1("rms_x"), 0, KD)
            rms_sum(n1("rms_c"), KD, KD, CTX)
            xh = lambda k: h[:, k, :]
            ch = lambda k: hc[:, k, :]
            pe.wait_ge(h_made, 2 * KD)
            for g in range(4):
                gemm(n1("pool", g), xh, KD)

            def gemm2(n):
                ws = [W[0].tile() for _ in range(KD)]
                for i, (src, w) in enumerate(((xh, T), (ch, CTX))):
                    b = begin(n + i)
                    for k in range(KD):
                        ins = mm(b[:, 0:w], ws[k], src(k), k == 0, k == KD - 1)
                    ins.then_inc(made1, 1)
                release()
            gemm2(n1("k", 0))
            gemm2(n1("k", 2))
            gemm2(n1("r"))
            gemm(n1("q", 0), xh, KD)
            gemm(n1("q", 1), xh, KD)
            gemm_tok(n1("v"), lambda k, m: (hc[:, k, P * m:P * m + P] if m < 2 else h[:, k, P * (m - 2):P * (m - 1)]),
                     6, KD, 512)
            for g in range(4):
                gemm(n1("g", g), xh, KD)
            pwo = PR1["poolw"][0]
            for g in range(4):
                b = begin(n1("poolw", g))
                pe.wait_ge(pooled, g + 1)
                mm(b, pr1[:, pwo + P * g:pwo + P * (g + 1)], pT[:, g, :], True, True).then_inc(made1, 1)
            wuo = PR1["wup"][0]
            N[0].wait_taken(pe, n1("r", 1))
            for d in range(4):
                for i, (o, w) in enumerate(((CTX, T), (0, CTX))):
                    b = begin(n1("zk", 4 * d + i))
                    mm(b[:, 0:w], pr1[:, wuo + P * d:wuo + P * (d + 1)], rbuf[:, o:o + w], True, True
                       ).then_inc(made1, 1)
                pe.wait_ge(kd_made, d + 1)
                for i, (a, b_) in enumerate(((0, 4), (4, 6))):
                    b = begin(n1("zk", 4 * d + 2 + i))
                    for m in range(a, b_):
                        ins = pe.transpose(b[:, P * (m - a):P * (m - a + 1)], kd[:, P * m:P * (m + 1)], c_("ident"))
                    ins.then_inc(made1, 1)
            N[0].wait_taken(pe, n1("zk", 15))
            for i in range(11):
                for dr in range(2):
                    b = begin(n1("kv", 2 * i + dr))
                    c = i if dr == 0 else (3 - i if i < 4 else 15 - i)
                    r = slice(64 * (c % 2), 64 * (c % 2) + 64)
                    for pr in range(2):
                        ins = mm(b[:, 256 * pr:256 * pr + 256], kdT[r, c // 2, 2 * dr + pr, :],
                                 vall[r, c // 2, 256 * pr:256 * pr + 256], True, True, loose=True)
                    ins.then_inc(made1, 1)
            pe.wait_ge(gla_ops, 4)
            pe.wait_ge(state_made, 11)

            def intra(u):
                hh, m = u // 4, u % 4
                pe.wait_ge(masked, u + 1)
                for dr in range(2):
                    ins = mm(bank[:, hh, P * m:P * (m + 1)], vall[:, 2 + m, P * hh:P * (hh + 1)], pmask[:, u % 2, dr, :],
                             m == 0 and dr == 0, False, loose=True)
                ins.then_inc(intra_done, 1)
                r = slice(64 * (hh % 2), 64 * (hh % 2) + 64)
                for dr in range(2):
                    for c in (2 * m, 2 * m + 1):
                        i = 4 + c if dr == 0 else 11 - c
                        ins = mm(bank[:, hh, CHUNK * c:CHUNK * (c + 1)], SS[r, 2 * dr + hh // 2, i, :],
                                 qe[r, 2 * dr + hh // 2, CHUNK * c:CHUNK * (c + 1)], False,
                                 m == 3 and dr == 1 and c == 7, loose=True)
                if m == 3:
                    ins.then_inc(heads_done, 1)
            for u in range(17):
                if u < 16:
                    hh, m = u // 4, u % 4
                    b = begin(n1("s", u))
                    r = slice(64 * (hh % 2), 64 * (hh % 2) + 64)
                    for dr in range(2):
                        d = 2 * dr + hh // 2
                        ins = mm(b[:, P * dr:P * (dr + 1)], km[r, d, P * m:P * (m + 1)], qm[r, d, P * m:P * (m + 1)],
                                 True, True, loose=True)
                    ins.then_inc(made1, 1)
                if u >= 1:
                    intra(u - 1)
            for hh in range(4):
                b = begin(n1("rms_o", hh))
                pe.wait_ge(o_squared, hh + 1)
                mm(b, c_("ones"), osq[:, hh, :], True, True).then_inc(made1, 1)
            pe.wait_ge(o_made, 4)

            def merge(name, b_no, branches, rhs, first):
                for t in range(8):
                    gemm(N[0].no(name, 2 * (t * branches + b_no) + 0), xh, KD)
                    gemm(N[0].no(name, 2 * (t * branches + b_no) + 1), rhs, 4)
            for t in range(8):
                for b_no, rhs in enumerate((lambda k: oT[:, k, :], lambda k: mixT[:, k, :])):
                    gemm(n1("merge", 4 * t + 2 * b_no), xh, KD)
                    gemm(n1("merge", 4 * t + 2 * b_no + 1), rhs, 4)
            N[0].wait_taken(pe, n1("merge", 31))
            for t in range(8):
                gemm(n1("out", t), lambda k: y[:, k, :], KD)
            W[0].finish(TILES_ONE, SLOTS_ONE)

            rms_sum(n1("rms_2"), 2 * KD, KD)
            pe.wait_ge(h_made, 3 * KD)
            for m in range(TT):
                for half in range(2):
                    b = begin(n1("h2k", 2 * m + half))
                    for k in range(4):
                        ins = pe.transpose(b[:, P * k:P * k + P], h[:, 4 * half + k, P * m:P * m + P], c_("ident"))
                    ins.then_inc(made1, 1)
            b = begin(n1("logits"))
            wro = PR1["wrouter"][0]
            for m in range(TT):
                for k in range(KD):
                    ins = mm(b[:, E * m:E * m + E], h[:, k, P * m:P * m + P], pr1[:, wro + E * k:wro + E * k + E],
                             k == 0, k == KD - 1)
            ins.then_inc(made1, 1)
            b = begin(n1("affT"))
            pe.wait_ge(aff_made, 1)
            for m in range(TT):
                ins = pe.transpose(b[0:E, P * m:P * m + P], aff[:, 2, m, :], c_("ident"))
            ins.then_inc(made1, 1)
            b = begin(n1("slotT"))
            pe.wait_ge(slot_made, 1)
            for m in range(TT):
                ins = pe.transpose(b[:, E * m:E * m + E], slot[:, P * m:P * m + P], c_("ident")[0:E, 0:E])
            ins.then_inc(made1, 1)

            for k in range(KD):
                for half in range(2):
                    b = begin(n1("gather", 2 * k + half))
                    for m in range(TT):
                        if k == 0 and half == 0:
                            pe.wait_ge(sel_ready, m + 1)
                        ins = mm(b, h2k[:, m, P * k:P * k + P],
                                 selx[:, m, 8 * half:8 * half + 8, :].rearrange("p e c -> p (e c)"),
                                 m == 0, m == TT - 1)
                    ins.then_inc(made1, 1)

            N[0].wait_taken(pe, n1("gather", 15))
            with pe.Fori(0, E // 2) as pair:
                W[0] = Weights(pair * (2 * SLOTS_EXPERT // RING) + SLOTS_ONE // RING)

                def both(b, lhs):
                    for k in range(8):
                        for j in range(2):
                            ins = mm(b[64 * j:64 * j + 64, :], lhs(k)[:, 64 * j:64 * j + 64], W[0].tile(4),
                                     k == 0, k == 7)
                        if k == 3:
                            release()
                    return ins
                pe.wait_ge(xs_taken, pair + 1)
                for half in range(2):
                    both(bank[:, half, :], lambda k: xsT[:, k, :]).then_inc(gate_made, 1)
                    release()
                    both(bank[:, 2 + half, :], lambda k: xsT[:, k, :]).then_inc(up_made, 1)
                    release()
                for half in range(2):
                    pe.wait_ge(a_ready, pair * 2 + (half + 1))
                    for k in range(4):
                        ins = pe.transpose(bank[:, 4 + half, P * k:P * k + P],
                                           acts[:, P * (4 * half + k):P * (4 * half + k) + P], c_("ident"))
                    ins.then_inc(a_turned, 1)
                pe.wait_ge(aT_ready, pair * 2 + 2)
                for half in range(2):
                    both(bank[:, 6 + half, :], lambda k: aT[:, k, :]).then_inc(y_made, 1)
                    release()
                W[0].finish(2 * TILES_EXPERT, 2 * SLOTS_EXPERT)

            pe.wait_ge(y_taken, E)
            so = CSE["pairsel"][0]
            for p in range(8):
                for i, src in enumerate((slot, affT)):
                    b = begin(n1("selw", 2 * p + i))
                    mm(b, cse[0:E, so + P * p:so + P * p + P], src, True, True).then_inc(made1, 1)
            N[0].wait_taken(pe, n1("selw", 15))
            for t in range(8):
                b = begin(n1("scatter", t))
                for p in range(8):
                    ins = mm(b, yexp[:, p, P * t:P * t + P], selw[:, p, :], p == 0, p == 7)
                ins.then_inc(made1, 1)
            rms_sum(n1("rms_f"), 3 * KD, KD)

            with pe.Fori(0, LAYERS) as l:
                W[0] = Weights(l * (SLOTS_LAYER // RING) + (SLOTS_ONE + E * SLOTS_EXPERT) // RING)
                N[0] = Numbers(LAY, made2, taken2, l * N_LAY)
                no = N[0].no
                ub = l * N_UNITS
                sq0 = l * SQ_LAYER + SQ_ONE

                def rope(name, n_tiles, rhs, nk, perm, raw, m=P):
                    for i, (what, j) in enumerate(rope_order(n_tiles)):
                        if what == "raw":
                            gemm(no(name, i), rhs, nk)
                        else:
                            b = begin(no(name, i))
                            N[0].wait_taken(pe, no(name, rope_order(n_tiles).index(("raw", j))))
                            mm(b[0:m, :], c_(perm)[0:m, 0:m], raw(j)[0:m], True, True).then_inc(made2, 1)

                def attend(sec):
                    us = SECTION[sec]
                    first = us[0]["n"]
                    for s in range(len(us) + 3):
                        if s < len(us):
                            u = us[s]
                            n = u["n"]
                            if s >= 2:
                                pe.wait_ge(exped, ub + n - 1)
                            mm(bank[:, n % 2, 0:u["nk"]], u["q"], u["k"], True, True).then_inc(scored, 1)
                        if 1 <= s <= len(us):
                            u = us[s - 1]
                            n = u["n"]
                            pe.wait_ge(exped, ub + n + 1)
                            if u["kind"] == "cmp":
                                pe.wait_ge(cmp_masked, l * N_CMPU + cmp_no[n] + 1)
                            if s - 1 >= 2:
                                pe.wait_ge(turned_out, ub + n - 1)
                            for b in range(u["nb"]):
                                w = min(P, u["nk"] - P * b)
                                ins = pe.transpose(bank[0:w, 2 + n % 2, P * b:P * b + P],
                                                   probs[:, n % 3, P * b:P * b + w], c_("ident"))
                            ins.then_inc(turned, 1)
                        if 2 <= s <= len(us) + 1:
                            u = us[s - 2]
                            n = u["n"]
                            pe.wait_ge(turned_out, ub + n + 1)
                            if s - 2 >= 2:
                                pe.wait_ge(o_taken, ub + n - 1)
                            for b in range(u["nb"]):
                                w = min(P, u["nk"] - P * b)
                                ins = mm(bank[:, 4 + n % 2, 0:P],
                                         probsT[0:w, n % 2, P * b:P * b + P], u["v"][b], b == 0, b == u["nb"] - 1)
                            ins.then_inc(pv_made, 1)
                        if s >= 3 and us[s - 3]["last"]:
                            qt = us[s - 3]["qt"]
                            n = no(f"ot{sec}", qt)
                            if qt >= 2:
                                N[0].wait_taken(pe, n - 2)
                            b = bank[:, 6 + qt % 2, :]
                            pe.wait_ge(tok_done, l * 16 + 4 * sec + qt + 1)
                            for k in range(4):
                                ins = pe.transpose(b[:, P * k:P * k + P], otok[:, qt % 2, P * k:P * k + P], c_("ident"))
                            ins.then_inc(made2, 1)
                    N[0].wait_taken(pe, no(f"ot{sec}", 3))

                def merge(b_no):
                    for t in range(8):
                        gemm(no(f"merge{b_no}", 2 * t), xh, KD)
                        gemm(no(f"merge{b_no}", 2 * t + 1), lambda k: OT[:, k, :], 4)

                rms_sum(no("rms_mix"), sq0, KD)
                pe.wait_ge(h_made, l * H_LAYER + H_ONE + KD)
                rope("a_fm", 5, xh, KD, "perm", lambda j: (Q[:, j, :] if j < 4 else K[:, 0, :]))
                gemm_tok(no("v"), lambda k, m: h[:, k, P * m:P * m + P], TT, KD, 408)
                N[0].wait_taken(pe, no("v", 3))
                attend(0)
                merge(0)

                gemm(no("kcvc", 0), xh, KD)
                gemm(no("kcvc", 1), xh, KD)
                rope("b_fm", 6, xh, KD, "perm", lambda j: (Q[:, j, :] if j < 4 else K[:, j - 4, :]))
                for i in range(2):
                    b = begin(no("cmp", i))
                    pe.wait_ge(blocks_made, l * 2 + i + 1)
                    for j in range(32):
                        ins = mm(b[:, 0:NCMP], W[0].tile(), cmpb[:, j, :], j == 0, j == 31)
                    ins.then_inc(made2, 1)
                    release()
                pe.wait_ge(cmp_silu, l * 2 + 2)
                b = begin(no("cmp", 2))
                mm(b[:, 0:NCMP], p2("w2k"), cmp1[:, 0, 0:NCMP], True, True).then_inc(made2, 1)
                b = begin(no("cmp", 3))
                mm(b[0:NCMP, 0:P], cmp1[:, 1, 0:NCMP], p2("w2v"), True, True).then_inc(made2, 1)
                N[0].wait_taken(pe, no("cmp", 3))
                attend(1)
                merge(1)

                gemm(no("kr", 0), xh, KD)
                b = begin(no("kr", 1))
                N[0].wait_taken(pe, no("kr", 0))
                mm(b, c_("permM"), lat[:, 5, :], True, True).then_inc(made2, 1)
                for j in range(5):
                    gemm(no("lat", j), xh, KD)
                rms_sum(no("rms_q"), sq0 + 8, 3)
                rms_sum(no("rms_kv"), sq0 + 11, 2)
                pe.wait_ge(lat_normed, l + 1)
                rope("q_fm", 8, lambda k: lat[:, k, :], 3, "permM", lambda j: Q[:, j, :])
                for j in range(8):
                    gemm(no("k_fm", j), lambda k: lat[:, 3 + k, :], 2)
                gemm_tok(no("v_mla"), lambda k, m: lat[:, 3 + k, P * m:P * m + P], TT, 2, 512)
                N[0].wait_taken(pe, no("v_mla", 3))
                attend(2)
                merge(2)
                N[0].wait_taken(pe, no("merge2", 15))
                for t in range(8):
                    gemm(no("out", t), lambda k: y[:, k, :], KD)

                rms_sum(no("rms_x"), sq0 + 13, KD)
                rms_sum(no("rms_m"), sq0 + 21, KD, MEM)
                pe.wait_ge(h_made, l * H_LAYER + H_ONE + 3 * KD)
                for j in range(4):
                    gemm(no("xq", j), xh, KD)
                for j in range(4):
                    gemm(no("xk", j), lambda k: hm[:, k, :], KD, MEM)
                gemm_tok(no("xv"), lambda k, m: hm[:, k, P * m:P * m + P], 2, KD, 512)
                N[0].wait_taken(pe, no("xv", 1))
                attend(3)
                for t in range(8):
                    gemm(no("xo", t), lambda k: OT[:, k, :], 4)

                rms_sum(no("rms_f"), sq0 + 29, KD)
                pe.wait_ge(h_made, l * H_LAYER + H_ONE + 4 * KD)
                for f in range(NFF):
                    gemm(no("gu", 2 * f), xh, KD)
                    gemm(no("gu", 2 * f + 1), xh, KD)
                N[0].wait_taken(pe, no("gu", 2 * NFF - 1))
                for t in range(8):
                    gemm(no("down", t), lambda k: act_ff[:, k, :], NFF)
                W[0].finish(TILES_LAYER, SLOTS_LAYER)

            rms_sum_final = Numbers({"rms_final": 0}, made1, taken1, N_ONE)
            N[0] = rms_sum_final
            b = bank[:, BANK0, :]
            for k in range(KD):
                pe.wait_ge(squared, SQ_ONE + LAYERS * SQ_LAYER + k + 1)
                mm(b, c_("ones"), sq[:, k % 2, :], k == 0, k == KD - 1).then_inc(summed, 1)
            pe.drain().then_inc(made1, 1)

        @block.scalar
        def _(act):
            act.dma_start(pr1, pr1_d).then_inc(loaded, 16)
            act.dma_start(cst[:, :], cst_d).then_inc(loaded, 16)
            act.dma_start(x[:, :, :], xT_d).then_inc(loaded, 16)
            act.dma_start(hc, ctxT_d).then_inc(loaded, 16)
            act.dma_start(cs1, cs1_d).then_inc(loaded, 16)
            act.dma_start(yflat[:, 0:2048], inv_d).then_inc(loaded_inv, 16)
            act.wait_ge(loaded, 16 * 5)
            nsq = [0]

            def squares(src, nk, base, width=T, ready=None):
                for k in range(nk):
                    if ready is not None:
                        ready(k)
                    n = base + k
                    if not (isinstance(n, int) and n < 2):
                        act.wait_ge(summed, n - 1)
                    act.activation(sq[:, k % 2, 0:width], src(k), ACT.Square).then_inc(squared, 1)

            def inv_root(N, n, slot_, features, width=T):
                N.wait_made(act, n)
                act.activation(rstd[:, slot_, 0:width], N.bank(n)[:, 0:width], ACT.Ln, bias=c_("eps"),
                               scale=1.0 / features).then_inc(N.taken_sem, 1)
                act.drain()
                act.activation(rstd[:, slot_, 0:width], rstd[:, slot_, 0:width], ACT.Exp, scale=-0.5
                               ).then_inc(rstd_made, 1)

            N = Numbers(ONE, made1, taken1, 0)
            n1 = N.no
            act.wait_ge(c2_zero, 1)
            act.activation(c2[:, :, 0:2], p1("c2").rearrange("p (k c) -> p k c", c=2), ACT.Silu).then_inc(c2_ready, 1)
            squares(lambda k: x[:, k, :], KD, 0)
            squares(lambda k: hc[:, k, :], KD, KD, CTX)
            N.wait_taken(act, n1("adaT", 2))
            inv_root(N, n1("rms_x"), 0, D)
            inv_root(N, n1("rms_c"), 1, D, CTX)
            N.wait_taken(act, n1("v", 5))
            for g in range(4):
                N.wait_made(act, n1("g", g))
                act.activation(gT[:, g, :], N.bank(n1("g", g)), ACT.Silu).then_inc(taken1, 1)
            for d in range(4):
                act.wait_ge(la_in, d + 1)
                act.activation(las[:, 1, :], las[:, 0, :], ACT.Abs)
                act.drain()
                act.activation(las[:, 1, :], las[:, 1, :], ACT.Exp, scale=-1.0)
                act.drain()
                act.activation(las[:, 1, :], las[:, 1, :], ACT.Ln, bias=1.0).then_inc(la_log, 1)
                s = 1.0 / 16.0
                act.wait_ge(expo_in, d + 1)
                act.activation(decay[:, d, :], las[:, 0, :].rearrange("p (c t) -> p c t", c=12)[:, :, 63 if d < 2 else 0],
                               ACT.Exp, scale=s)
                act.activation(qe[:, d, :], las[:, 0, CTX:], ACT.Exp, scale=s)
                act.activation(qm[:, d, :], las[:, 1, CTX:], ACT.Exp, scale=s)
                act.activation(km[:, d, :], las[:, 1, CTX:], ACT.Exp, scale=-s)
                if d >= 1:
                    N.wait_made(act, n1("zk", 4 * d - 1))
                act.activation(kd, las[:, 2, :], ACT.Exp, scale=-s).then_inc(expo_out, 1)
            for hh in range(4):
                act.wait_ge(heads_done, hh + 1)
                act.activation(osq[:, hh, :], bank[:, hh, :], ACT.Square).then_inc(o_squared, 1)
            N.wait_taken(act, n1("s", 15))
            for hh in range(4):
                n = n1("rms_o", hh)
                N.wait_made(act, n)
                if hh >= 2:
                    act.wait_ge(o_made, hh - 1)
                act.activation(rstd[:, hh % 2, :], N.bank(n), ACT.Ln, bias=c_("eps"), scale=1.0 / DV
                               ).then_inc(taken1, 1)
                act.drain()
                act.activation(rstd[:, hh % 2, :], rstd[:, hh % 2, :], ACT.Exp, scale=-0.5).then_inc(rstd_o, 1)

            def gates(N, name, count, func, base, out=None):
                for t in range(count):
                    N.wait_made(act, N.no(name, 2 * t))
                    if t >= 2:
                        N.wait_taken(act, N.no(name, 2 * t - 3))
                    act.activation(sig[:, t % 2, :], N.bank(N.no(name, 2 * t)), func).then_inc(gates_made, 1)
            gates(N, "merge", 16, ACT.Sigmoid, 0)
            N.wait_taken(act, n1("merge", 31))
            act.dma_start(cse, cse_d).then_inc(loaded_moe, 16)
            N.wait_made(act, n1("out", 7))
            act.dma_start(posi, pos_d).then_inc(loaded_pos, 16)
            squares(lambda k: x[:, k, :], KD, 2 * KD, ready=lambda k: N.wait_taken(act, n1("out", k)))
            inv_root(N, n1("rms_2"), 0, D)
            act.wait_ge(affx, 1)
            act.activation(aff[:, 1, :, :], aff[:, 0, :, :], ACT.Exp).then_inc(affe, 1)
            with act.Fori(0, E // 2) as pair:
                for half in range(2):
                    act.wait_ge(gate_made, pair * 2 + (half + 1))
                    act.activation(sg[:, half, :], bank[:, half, :], ACT.Silu).then_inc(silu_made, 1)
                for half in range(2):
                    act.wait_ge(a_turned, pair * 2 + (half + 1))
                    act.activation(aT[:, 4 * half:4 * half + 4, :].rearrange("p k c -> p (k c)"),
                                   bank[:, 4 + half, :], ACT.Copy).then_inc(aT_ready, 1)
            squares(lambda k: x[:, k, :], KD, 3 * KD, ready=lambda k: N.wait_taken(act, n1("scatter", k)))
            inv_root(N, n1("rms_f"), 0, D)

            for i, (s_, c_t) in enumerate(((sinT, cosT), (sinM, cosM))):
                act.wait_ge(ang_made, i + 1)
                act.activation(c_t, s_, ACT.Sin, scale=0.5)
                act.activation(s_, s_, ACT.Sin).then_inc(sin_made, 1)

            with act.Fori(0, LAYERS) as l:
                N = Numbers(LAY, made2, taken2, l * N_LAY)
                no = N.no
                ub = l * N_UNITS
                sq0 = l * SQ_LAYER + SQ_ONE

                def attend(sec):
                    us = SECTION[sec]
                    for s in range(len(us) + 3):
                        if s < len(us):
                            u = us[s]
                            n = u["n"]
                            act.wait_ge(biased, ub + n + 1)
                            if s >= 3:
                                act.wait_ge(turned, ub + n - 2)
                            if u["sink"] is not None:
                                act.activation(esink[:, n % 8:n % 8 + 1], p2("sinks", u["sink"]), ACT.Exp,
                                               bias=nbias[:, n % 8:n % 8 + 1])
                            act.activation(probs[:, n % 3, 0:u["nk"]], bank[:, n % 2, 0:u["nk"]], ACT.Exp,
                                           bias=nbias[:, n % 8:n % 8 + 1], scale=u["scale"],
                                           accum_out=den[:, n % 8:n % 8 + 1]).then_inc(exped, 1)
                        if 1 <= s <= len(us):
                            u = us[s - 1]
                            n = u["n"]
                            act.wait_ge(turned, ub + n + 1)
                            if s - 1 >= 2:
                                act.wait_ge(pv_made, ub + n - 1)
                            w = min(P, u["nk"])
                            act.activation(probsT[0:w, n % 2, 0:P * u["nb"]], bank[0:w, 2 + n % 2, 0:P * u["nb"]],
                                           ACT.Copy).then_inc(turned_out, 1)
                        if s >= 3 and us[s - 3]["last"]:
                            qt = us[s - 3]["qt"]
                            n = no(f"ot{sec}", qt)
                            N.wait_made(act, n)
                            act.activation(OT[:, :, P * qt:P * qt + P],
                                           bank[:, 6 + qt % 2, :].rearrange("p (k t) -> p k t", k=4), ACT.Copy
                                           ).then_inc(taken2, 1)

                act.wait_ge(x_made, l * KD + KD)
                act.dma_start(pr2, pr2_d[bass.ds(l, 1)].rearrange("a p n -> p (a n)")).then_inc(loaded_pr2, 16)
                squares(lambda k: x[:, k, :], KD, sq0)
                inv_root(N, no("rms_mix"), 0, D)
                N.wait_taken(act, no("v", 3))
                act.activation(sgate, vtok[:, :, 384:408], ACT.Sigmoid).then_inc(sgate_made, 1)
                attend(0)
                gates(N, "merge0", 8, ACT.Sigmoid, 0)
                N.wait_taken(act, no("b_fm", 11))
                for i in range(2):
                    N.wait_made(act, no("cmp", i))
                    act.activation(cmp1[:, i, 0:NCMP], N.bank(no("cmp", i))[:, 0:NCMP], ACT.Silu
                                   ).then_inc(taken2, 1)
                    act.drain().then_inc(cmp_silu, 1)
                attend(1)
                gates(N, "merge1", 8, ACT.Sigmoid, 0)
                squares(lambda k: lat[:, k, :], 3, sq0 + 8, ready=lambda k: N.wait_taken(act, no("lat", k)))
                for k in range(2):
                    N.wait_taken(act, no("lat", 3 + k))
                    act.wait_ge(summed, sq0 + 11)
                    act.activation(sq[:, k % 2, :], lat[:, 3 + k, :], ACT.Square).then_inc(squared, 1)
                inv_root(N, no("rms_q"), 0, MLA_R)
                inv_root(N, no("rms_kv"), 1, MLA_C)
                attend(2)
                gates(N, "merge2", 8, ACT.Sigmoid, 0)
                act.dma_start(mem, memT_d).then_inc(loaded_mem, 16)
                for k in range(KD):
                    N.wait_taken(act, no("out", k))
                    act.wait_ge(summed, sq0 + 13 + k - (1 if k >= 2 else min(k, 1)) if k >= 2 else sq0 + 13)
                    act.activation(sq[:, k % 2, :], x[:, k, :], ACT.Square).then_inc(squared, 1)
                act.wait_ge(loaded_mem, l * 16 + 16)
                squares(lambda k: mem[:, k, :], KD, sq0 + 21, MEM)
                inv_root(N, no("rms_x"), 0, D)
                inv_root(N, no("rms_m"), 1, D, MEM)
                attend(3)
                squares(lambda k: x[:, k, :], KD, sq0 + 29, ready=lambda k: N.wait_taken(act, no("xo", k)))
                inv_root(N, no("rms_f"), 0, D)
                gates(N, "gu", NFF, ACT.Silu, 0)

            act.wait_ge(x_made, LAYERS * KD + KD)
            squares(lambda k: x[:, k, :], KD, SQ_ONE + LAYERS * SQ_LAYER)
            act.wait_ge(made1, N_ONE + 1)
            act.activation(rstd[:, 0, :], bank[:, BANK0, :], ACT.Ln, bias=c_("eps"), scale=1.0 / D)
            act.drain()
            act.activation(rstd[:, 0, :], rstd[:, 0, :], ACT.Exp, scale=-0.5).then_inc(rstd_made, 1)
            for k in range(KD):
                act.wait_ge(out_ready, k + 1)
                act.dma_start(out_d[:, k, :], h[:, k, :]).then_inc(out_sem, 16)
            act.wait_ge(out_sem, 16 * KD)

        @block.gpsimd
        def _(pool):
            pool.memset(c2, 0.0).then_inc(c2_zero, 1)
            pool.memset(poolreg, 0.0)
            pool.drain().then_inc(pool_zero, 1)
            pool.wait_ge(loaded_inv, 16)
            for g, w in enumerate(WINDOWS):
                pool.wait_ge(pool_in, g + 1)
                u = pu[g].rearrange("p (r c) -> p r c", r=ROWS)
                src, at, lo = u, 0, 0
                s = 1
                lo, hi = 0, 80
                while s < w:
                    dst = pa[at][:, 0:640].rearrange("p (r c) -> p r c", r=ROWS)
                    a, b = (1, 0) if s == 1 else (s // 2, s // 2)
                    lo, hi = lo + a, hi - b
                    pool.tensor_tensor(dst[:, :, lo:hi], src[:, :, lo - a:hi - a], src[:, :, lo + b:hi + b], ALU.add)
                    pool.drain()
                    src, at, s = dst, 1 - at, 2 * s
                base = [pa[i].rearrange("p (r c) -> p r c", c=80)[:, :, 0:64] for i in range(2)]
                if at == 1:
                    keep = pa[1][:, 0:640].rearrange("p (r c) -> p r c", r=ROWS)
                    pool.tensor_copy(keep[:, :, 8:72], src[:, :, 8:72])
                    pool.drain()
                    src = keep
                pool.memset(pa[0], 0.0)
                pool.drain()
                pool.tensor_copy(base[0][:, 8:16, :], src[:, :, 8:72])
                pool.drain()
                src, at, s, lo, hi = base[0], 1, 1, 0, 24
                while s < w:
                    dst = base[at]
                    a, b = (1, 0) if s == 1 else (s // 2, s // 2)
                    lo, hi = lo + a, hi - b
                    pool.tensor_tensor(dst[:, lo:hi, :], src[:, lo - a:hi - a, :], src[:, lo + b:hi + b, :], ALU.add)
                    pool.drain()
                    src, at, s = dst, 1 - at, 2 * s
                out = pT[:, g, :].rearrange("p (r c) -> p r c", r=ROWS)
                pool.tensor_tensor(out, src[:, 8:16, :], inv[:, g, :].rearrange("p (r c) -> p r c", r=ROWS), ALU.mult)
                pool.drain()
                pool.tensor_tensor(out, out, u[:, :, 8:72], ALU.subtract).then_inc(pooled, 1)

        @block.vector
        def _(dve):
            dr = dve.drain
            N = Numbers(ONE, made1, taken1, 0)
            n1 = N.no

            def take(N, n, out, src=None, m=P, width=512):
                N.wait_made(dve, n)
                dve.tensor_copy(out, N.bank(n)[0:m, 0:width] if src is None else src).then_inc(N.taken_sem, 1)

            def norm(src, dst, gain, slot_, nk, width=T, shift=None, inc=None):
                for k in range(nk):
                    ins = dve.scalar_tensor_tensor(out=dst(k), in0=src(k), scalar=gain(k), in1=rstd[:, slot_, 0:width],
                                                   op0=ALU.mult, op1=ALU.mult)
                    if shift is None and inc is not None:
                        ins.then_inc(inc, 1)
                if shift is not None:
                    dr()
                    for k in range(nk):
                        ins = dve.tensor_scalar(dst(k), dst(k), shift(k), None, ALU.add)
                        if inc is not None:
                            ins.then_inc(inc, 1)

            dve.wait_ge(loaded, 16 * 5)
            dve.tensor_copy(gfinal[:, :], p1("gfinal"))
            for i in range(3):
                take(N, n1("ada", i), adar[:, i, :])
            for i in range(3):
                n = n1("adaT", i)
                N.wait_made(dve, n)
                dve.tensor_tensor(mods[:, 16 * i:16 * i + 16, :].rearrange("p (j q) c -> p j q c", j=4),
                                  N.bank(n).rearrange("p (q j r) -> p j q r", q=4, j=4)[:, :, :, 0:2],
                                  p1("ada_b")[:, 16 * i:16 * i + 16].rearrange("p (j q c) -> p j q c", j=4, c=1)
                                  .to_broadcast([P, 4, 4, 2]), ALU.add).then_inc(taken1, 1)
            dr()
            for i, (at, c, g) in enumerate(((8, 0, "g1"), (8, 1, "g1"), (32, 0, "g2"))):
                dve.scalar_tensor_tensor(out=amp[:, i, :], in0=mods[:, at:at + 8, c], scalar=1.0, in1=p1(g),
                                         op0=ALU.add, op1=ALU.mult)
            dr()
            dve.wait_ge(rstd_made, 1)
            dve.wait_ge(rstd_made, 2)
            norm(lambda k: x[:, k, :], lambda k: h[:, k, :], lambda k: amp[:, 0, k:k + 1], 0, KD,
                 shift=lambda k: mods[:, k, 0:1], inc=h_made)
            norm(lambda k: hc[:, k, :], lambda k: hc[:, k, :], lambda k: amp[:, 1, k:k + 1], 1, KD, CTX,
                 shift=lambda k: mods[:, k, 1:2], inc=h_made)
            dve.wait_ge(pool_zero, 1)
            for g in range(4):
                N.wait_made(dve, n1("pool", g))
                if g >= 2:
                    dve.wait_ge(pooled, g - 1)
                dve.tensor_copy(pu[g].rearrange("p (r c) -> p r c", r=ROWS)[:, :, 8:72],
                                N.bank(n1("pool", g)).rearrange("p (r c) -> p r c", r=ROWS)).then_inc(taken1, 1)
                dr().then_inc(pool_in, 1)
            for j in range(2):
                take(N, n1("k", 2 * j), kall[:, j, CTX:])
                take(N, n1("k", 2 * j + 1), kall[:, j, 0:CTX], width=CTX)
            take(N, n1("r"), rbuf[:, CTX:])
            take(N, n1("r", 1), rbuf[:, 0:CTX], width=CTX)
            for j in range(2):
                N.wait_made(dve, n1("q", j))
                dve.tensor_scalar(qx[:, j, :], N.bank(n1("q", j)), DKH ** -0.5, None, ALU.mult).then_inc(taken1, 1)
            for m in range(6):
                take(N, n1("v", m), vall[:, m, :])
            N.wait_taken(dve, n1("g", 3))
            for g in range(4):
                N.wait_made(dve, n1("poolw", g))
                dve.tensor_scalar(mixT[:, g, :], N.bank(n1("poolw", g)), p1("pool_scale", g), None, ALU.mult
                                  ).then_inc(taken1, 1)
            for d in range(4):
                if d >= 1:
                    dve.wait_ge(expo_out, d)
                for i, (o, w) in enumerate(((CTX, T), (0, CTX))):
                    n = n1("zk", 4 * d + i)
                    N.wait_made(dve, n)
                    dve.tensor_scalar(las[:, 0, o:o + w], N.bank(n)[:, 0:w], p1("b_decay", d), None, ALU.add
                                      ).then_inc(taken1, 1)
                dr().then_inc(la_in, 1)
                dve.wait_ge(la_log, d + 1)
                dve.scalar_tensor_tensor(out=las[:, 2, :], in0=las[:, 0, :], scalar=0.0, in1=las[:, 1, :],
                                         op0=ALU.min, op1=ALU.subtract)
                dr()
                so = CS1["scan"][0]
                dve.tensor_tensor_scan(las[:, 0, :], cs1[:, so:so + 768], las[:, 2, :], 0.0, ALU.mult, ALU.add)
                dr()
                ch = lambda a: a.rearrange("p (c t) -> p c t", c=12)
                if d >= 2:
                    dve.tensor_tensor(las[:, 1, :], las[:, 2, :], las[:, 0, :], ALU.subtract)
                    dr()
                    dve.tensor_tensor(ch(las[:, 1, :]), ch(las[:, 1, :]),
                                      ch(las[:, 0, :])[:, :, 63:64].to_broadcast([P, 12, CHUNK]), ALU.add)
                    dr()
                    dve.tensor_copy(las[:, 0, :], las[:, 1, :])
                    dr()
                mid, last = (31, 63) if d < 2 else (32, 0)
                b = ch(las[:, 0, :])
                dve.tensor_tensor(ch(las[:, 1, :]), b, b[:, :, mid:mid + 1].to_broadcast([P, 12, CHUNK]), ALU.subtract)
                dve.tensor_tensor(ch(las[:, 2, :]), b, b[:, :, last:last + 1].to_broadcast([P, 12, CHUNK]), ALU.subtract)
                dr().then_inc(expo_in, 1)
                dve.wait_ge(expo_out, d + 1)
                pr = d % 2
                dve.tensor_tensor(kd, kd, kall[:, pr, :], ALU.mult).then_inc(kd_made, 1)
                dve.tensor_tensor(qe[:, d, :], qe[:, d, :], qx[:, pr, :], ALU.mult)
                dve.tensor_tensor(qm[:, d, :], qm[:, d, :], qx[:, pr, :], ALU.mult)
                dve.tensor_tensor(km[:, d, :], km[:, d, :], kall[:, pr, CTX:], ALU.mult).then_inc(gla_ops, 1)
                for i, (a, b_) in enumerate(((0, 4), (4, 6))):
                    n = n1("zk", 4 * d + 2 + i)
                    N.wait_made(dve, n)
                    dve.tensor_copy(kdT[:, a:b_, d, :],
                                    N.bank(n)[:, 0:P * (b_ - a)].rearrange("p (m c) -> p m c", c=P)
                                    ).then_inc(taken1, 1)
            dve.memset(SS[:, :, 0, :], 0.0)
            dve.memset(rbuf, 0.0)
            dr()
            for i in range(11):
                for d_ in range(2):
                    n = n1("kv", 2 * i + d_)
                    N.wait_made(dve, n)
                    c = i if d_ == 0 else (3 - i if i < 4 else 15 - i)
                    for pr in range(2):
                        for half in range(2):
                            r = slice(64 * half, 64 * half + 64)
                            d = 2 * d_ + pr
                            dve.scalar_tensor_tensor(
                                out=SS[r, d, i + 1, :], in0=SS[r, d, i, :], scalar=decay[r, d, c:c + 1],
                                in1=N.bank(n)[r, 256 * pr + P * half:256 * pr + P * half + P],
                                op0=ALU.mult, op1=ALU.add)
                    dr().then_inc(taken1, 1)
                dr().then_inc(state_made, 1)
            for u in range(16):
                n = n1("s", u)
                N.wait_made(dve, n)
                if u >= 2:
                    dve.wait_ge(intra_done, u - 1)
                for d_ in range(2):
                    o = CS1["maskf" if d_ == 0 else "maskb"][0]
                    dve.copy_predicated(pmask[:, u % 2, d_, :], cs1[:, o:o + P].bitcast(U32),
                                        N.bank(n)[:, P * d_:P * d_ + P])
                dr().then_inc(masked, 1)
                dr().then_inc(taken1, 1)
            for hh in range(4):
                dve.wait_ge(rstd_o, hh + 1)
                dve.scalar_tensor_tensor(out=oT[:, hh, :], in0=bank[:, hh, :], scalar=p1("gn"), in1=rstd[:, hh % 2, :],
                                         op0=ALU.mult, op1=ALU.mult)
                dr()
                dve.tensor_tensor(oT[:, hh, :], oT[:, hh, :], gT[:, hh, :], ALU.mult).then_inc(o_made, 1)

            def merge(N, name, t, i, first, gate_no):
                n = N.no(name, i + 1)
                if not first:
                    dr()
                N.wait_made(dve, n)
                dve.wait_ge(gates_made, gate_no)
                half = sig[:, (i // 2) % 2, :]
                if first:
                    dve.tensor_tensor(y[:, t, :], half, N.bank(n), ALU.mult).then_inc(N.taken_sem, 2)
                else:
                    dve.tensor_tensor(tmp[:, :], half, N.bank(n), ALU.mult)
                    dr()
                    dve.tensor_tensor(y[:, t, :], y[:, t, :], tmp[:, :], ALU.add).then_inc(N.taken_sem, 2)
            for t in range(8):
                for b in range(2):
                    merge(N, "merge", t, 4 * t + 2 * b, b == 0, 2 * t + b + 1)
            for t in range(8):
                n = n1("out", t)
                N.wait_made(dve, n)
                dve.scalar_tensor_tensor(out=x[:, t, :], in0=N.bank(n), scalar=mods[:, 16 + t, 0:1], in1=x[:, t, :],
                                         op0=ALU.mult, op1=ALU.add).then_inc(taken1, 1)

            dve.wait_ge(rstd_made, 3)
            norm(lambda k: x[:, k, :], lambda k: h[:, k, :], lambda k: amp[:, 2, k:k + 1], 0, KD,
                 shift=lambda k: mods[:, 24 + k, 0:1], inc=h_made)
            for m in range(TT):
                for half in range(2):
                    take(N, n1("h2k", 2 * m + half), h2k[:, m, 512 * half:512 * half + 512])
            n = n1("logits")
            N.wait_made(dve, n)
            lg = N.bank(n)[:, 0:TT * E].rearrange("p (m e) -> p m e", m=TT)
            dve.tensor_reduce(stat[:, 0, :], lg, AX.X, ALU.max)
            dr()
            dve.tensor_tensor(aff[:, 0, :, :], lg, stat[:, 0, :].rearrange("p (m o) -> p m o", o=1)
                              .to_broadcast([P, TT, E]), ALU.subtract).then_inc(taken1, 1)
            dr().then_inc(affx, 1)
            dve.wait_ge(affe, 1)
            dve.tensor_reduce(stat[:, 1, :], aff[:, 1, :, :], AX.X, ALU.add)
            dr()
            dve.reciprocal(stat[:, 1, :], stat[:, 1, :])
            dr()
            dve.tensor_tensor(aff[:, 2, :, :], aff[:, 1, :, :], stat[:, 1, :].rearrange("p (m o) -> p m o", o=1)
                              .to_broadcast([P, TT, E]), ALU.mult).then_inc(aff_made, 1)
            N.wait_made(dve, n1("affT"))
            dve.tensor_copy(work, N.bank(n1("affT"))[0:E, :])
            take(N, n1("affT"), affT, m=E)
            dr()
            for _r in range(CAP // 8):
                dve.max(top8, work)
                dr()
                dve.match_replace(work, top8, work, -1.0)
                dr()
            dve.tensor_scalar(mark, work, 0.0, None, ALU.is_lt)
            dr()
            dve.memset(work, 1.0)
            dr()
            dve.tensor_tensor_scan(slot, work, mark, 0.0, ALU.mult, ALU.add)
            dr()
            dve.tensor_tensor(slot, slot, mark, ALU.mult)
            dr()
            dve.tensor_scalar(slot, slot, 1.0, None, ALU.subtract).then_inc(slot_made, 1)
            take(N, n1("slotT"), slot_tok,
                 src=N.bank(n1("slotT"))[:, 0:TT * E].rearrange("p (m e) -> p m e", m=TT))
            dr()
            dve.wait_ge(loaded_moe, 16)
            for m in range(TT):
                dve.tensor_tensor(selx[:, m, :, :],
                                  slot_tok[:, m, :].rearrange("p (e c) -> p e c", c=1).to_broadcast([P, E, CAP]),
                                  ce_("iota").rearrange("p (e c) -> p e c", e=1).to_broadcast([P, E, CAP]),
                                  ALU.is_equal).then_inc(sel_ready, 1)
            for k in range(KD):
                for half in range(2):
                    take(N, n1("gather", 2 * k + half), xs_all[:, 4 * half:4 * half + 4, k, :],
                         src=N.bank(n1("gather", 2 * k + half)).rearrange("p (e c) -> p e c", e=4))

            dr()
            with dve.Fori(0, E // 2) as pair:
                dve.tensor_copy(xsT.rearrange("p k c -> p (k c)"),
                                xs_all[:, bass.ds(pair, 1), :, :].rearrange("p e k c -> p (e k c)")
                                ).then_inc(xs_taken, 1)
                for half in range(2):
                    dve.wait_ge(up_made, pair * 2 + (half + 1))
                    dve.wait_ge(silu_made, pair * 2 + (half + 1))
                    dve.tensor_tensor(acts[:, 512 * half:512 * half + 512], sg[:, half, :], bank[:, 2 + half, :],
                                      ALU.mult).then_inc(a_ready, 1)
                dr()
                for half in range(2):
                    dve.wait_ge(y_made, pair * 2 + (half + 1))
                    dve.tensor_copy(top8[:, half:half + 1], bank[0:E, 6 + half, 0:1])
                    dve.tensor_copy(yexp[:, bass.ds(pair, 1), 512 * half:512 * half + 512],
                                    bank[:, 6 + half:7 + half, :]).then_inc(y_taken, 1)
                dr()
            for p in range(8):
                a, b = n1("selw", 2 * p), n1("selw", 2 * p + 1)
                N.wait_made(dve, b)
                dr()
                dve.tensor_scalar(tmp[:, :], N.bank(a), ce_("cidx"), None, ALU.is_equal).then_inc(taken1, 1)
                dr()
                dve.tensor_tensor(selw[:, p, :], tmp[:, :], N.bank(b), ALU.mult).then_inc(taken1, 1)
            for t in range(8):
                n = n1("scatter", t)
                N.wait_made(dve, n)
                dve.scalar_tensor_tensor(out=x[:, t, :], in0=N.bank(n), scalar=mods[:, 40 + t, 0:1], in1=x[:, t, :],
                                         op0=ALU.mult, op1=ALU.add).then_inc(taken1, 1)
            dve.wait_ge(rstd_made, 4)
            norm(lambda k: x[:, k, :], lambda k: x[:, k, :], lambda k: p1("gf", k), 0, KD, inc=x_made)
            dr()
            posf = tmp[:, :]
            dve.wait_ge(loaded_pos, 16)
            dve.tensor_copy(posf, posi)
            dr()
            TWO_PI = 2 * np.pi
            MAGIC = 12582912.0
            C1 = 6.28125
            C2 = float(np.float32(np.floor((TWO_PI - C1) * 2.0 ** 21) / 2.0 ** 21))
            C3 = float(np.float32(TWO_PI - C1 - C2))
            for i, (s_, c_t, f, sg_) in enumerate(((sinT, cosT, "freq", "sign"), (sinM, cosM, "freqM", "signM"))):
                dve.tensor_scalar(s_, posf, c_(f), None, ALU.mult)
                dr()
                dve.tensor_scalar(c_t, s_, float(1 / TWO_PI), MAGIC, ALU.mult, ALU.add)
                dr()
                dve.tensor_scalar(c_t, c_t, MAGIC, None, ALU.subtract)
                for c in (C1, C2, C3):
                    dr()
                    dve.scalar_tensor_tensor(out=s_, in0=c_t, scalar=-c, in1=s_, op0=ALU.mult, op1=ALU.add)
                dr()
                dve.tensor_scalar(s_, s_, 3.1415925, -3.1415925, ALU.min, ALU.max).then_inc(ang_made, 1)
                dve.wait_ge(sin_made, i + 1)
                dve.tensor_scalar(s_, s_, c_(sg_), None, ALU.mult)
                dve.tensor_tensor(c_t, c_t, c_t, ALU.mult)
                dr()
                dve.tensor_scalar(c_t, c_t, -2.0, 1.0, ALU.mult, ALU.add)
                dr()

            with dve.Fori(0, LAYERS) as l:
                N = Numbers(LAY, made2, taken2, l * N_LAY)
                no = N.no
                ub = l * N_UNITS
                rs = l * R_LAYER + R_ONE

                def rope(name, n_tiles, raw, out, cos_, sin_):
                    order = rope_order(n_tiles)
                    for i, (what, j) in enumerate(order):
                        n = no(name, i)
                        dr()
                        N.wait_made(dve, n)
                        if what == "raw":
                            dve.tensor_copy(raw(j), N.bank(n)).then_inc(taken2, 1)
                            dr()
                            dve.tensor_tensor(rope1[:, j % 2, :], raw(j), cos_, ALU.mult)
                        else:
                            dve.tensor_tensor(rope2, N.bank(n), sin_, ALU.mult)
                            dr()
                            dve.tensor_tensor(out(j), rope1[:, j % 2, :], rope2, ALU.add).then_inc(taken2, 1)

                def attend(sec):
                    us = SECTION[sec]
                    for s in range(len(us) + 2):
                        if s < len(us):
                            u = us[s]
                            n, nk, c8 = u["n"], u["nk"], slice(u["n"] % 8, u["n"] % 8 + 1)
                            S = bank[:, n % 2, :]
                            dve.wait_ge(scored, ub + n + 1)
                            if u["kind"] in ("causal", "window"):
                                dve.tensor_tensor(S[:, nk - P:nk], S[:, nk - P:nk], c_("causal"), ALU.add)
                                if u["kind"] == "window" and nk > P:
                                    dve.tensor_tensor(S[:, 0:P], S[:, 0:P], c_("recent"), ALU.add)
                                dr()
                            if u["kind"] == "cmp":
                                o = NCMP * u["qt"]
                                dve.tensor_tensor(S[:, 0:nk], S[:, 0:nk], c_("cmp_add")[:, o:o + NCMP], ALU.add)
                                dr()
                            dve.tensor_reduce(nmax[:, c8], S[:, 0:nk], AX.X, ALU.max, negate=True)
                            dr()
                            if u["sink"] is not None:
                                dve.tensor_scalar(nbias[:, c8], nmax[:, c8], u["scale"],
                                                  nsink[:, u["sink"]:u["sink"] + 1], ALU.mult, ALU.min
                                                  ).then_inc(biased, 1)
                            else:
                                dve.tensor_scalar(nbias[:, c8], nmax[:, c8], u["scale"], None, ALU.mult
                                                  ).then_inc(biased, 1)
                            if u["kind"] == "cmp":
                                dve.wait_ge(exped, ub + n + 1)
                                dve.scalar_tensor_tensor(out=probs[:, n % 3, 0:nk], in0=probs[:, n % 3, 0:nk], scalar=1.0,
                                                         in1=c_("cmp_mul")[:, o:o + NCMP], op0=ALU.mult, op1=ALU.mult)
                                dr().then_inc(cmp_masked, 1)
                                dve.tensor_reduce(den[:, c8], probs[:, n % 3, 0:nk], AX.X, ALU.add)
                        if s >= 2:
                            u = us[s - 2]
                            n, c8 = u["n"], slice(u["n"] % 8, u["n"] % 8 + 1)
                            O = bank[:, 4 + n % 2, u["vc"]:u["vc"] + u["w"]]
                            dst = otok[:, u["qt"] % 2, u["col"]:u["col"] + u["w"]]
                            dve.wait_ge(pv_made, ub + n + 1)
                            if u["sink"] is not None:
                                dve.tensor_tensor(den[:, c8], den[:, c8], esink[:, c8], ALU.add)
                                dr()
                            if u["kind"] == "cmp":
                                dve.tensor_scalar(den[:, c8], den[:, c8], 1e-30, None, ALU.max)
                                dr()
                            dve.reciprocal(rden[:, c8], den[:, c8])
                            dr()
                            if u["first"] and u["h"] == 0 and u["qt"] >= 2:
                                N.wait_made(dve, no(f"ot{sec}", u["qt"] - 2))
                            if u["gate"] is None:
                                ins = dve.tensor_scalar(dst, O, rden[:, c8], None, ALU.mult)
                            else:
                                qt_, gc = u["gate"]
                                gate = sgate[:, qt_, gc:gc + 1]
                                if u["first"]:
                                    ins = dve.tensor_scalar(dst, O, rden[:, c8], gate, ALU.mult, ALU.mult)
                                else:
                                    dve.tensor_tensor(coef[:, c8], rden[:, c8], gate, ALU.mult)
                                    dr()
                                    ins = dve.scalar_tensor_tensor(out=dst, in0=O, scalar=coef[:, c8], in1=dst,
                                                                   op0=ALU.mult, op1=ALU.add)
                            ins.then_inc(o_taken, 1)
                            if u["last"]:
                                dr().then_inc(tok_done, 1)

                dve.wait_ge(loaded_pr2, l * 16 + 16)
                dve.tensor_scalar(nsink, p2("sinks"), -1.0, None, ALU.mult)
                dve.wait_ge(rstd_made, rs + 1)
                norm(lambda k: x[:, k, :], lambda k: h[:, k, :], lambda k: p2("norm_mix", k), 0, KD, inc=h_made)
                rope("a_fm", 5, lambda j: (Q[:, j, :] if j < 4 else K[:, 0, :]),
                     lambda j: (Q[:, j, :] if j < 4 else K[:, 0, :]), cosT, sinT)
                for m in range(TT):
                    take(N, no("v", m), vtok[:, m, :], width=408)
                dr()
                dve.wait_ge(sgate_made, l + 1)
                attend(0)
                g0 = l * G_LAYER + 16
                for t in range(8):
                    merge(N, "merge0", t, 2 * t, True, g0 + t + 1)

                take(N, no("kcvc", 0), K[:, 2, :])
                take(N, no("kcvc", 1), K[:, 3, :])
                dr()

                def blocks(i, name):
                    src = K[:, 2 + i, :]
                    win = bass.AP(tensor=src.tensor, offset=src.offset, ap=[list(src.ap[0]), [1, 32], [16, NCMP]])
                    dve.tensor_tensor(cmpb, win, p2(name).rearrange("p (j o) -> p j o", o=1)
                                      .to_broadcast([P, 32, NCMP]), ALU.add).then_inc(blocks_made, 1)
                blocks(0, "pek")
                rope("b_fm", 6, lambda j: (Q[:, j, :] if j < 4 else K[:, j - 4, :]),
                     lambda j: (Q[:, 4 + j, :] if j < 4 else K[:, j - 4, :]), cosT, sinT)
                N.wait_made(dve, no("cmp", 0))
                blocks(1, "pev")
                take(N, no("cmp", 2), cmp1[:, 2, 0:NCMP], width=NCMP)
                take(N, no("cmp", 3), vcmp[0:NCMP, :], m=NCMP, width=P)
                attend(1)
                for t in range(8):
                    merge(N, "merge1", t, 2 * t, False, g0 + 8 + t + 1)

                n = no("kr", 0)
                take(N, n, lat[:, 5, :])
                dr()
                dve.tensor_tensor(rope1[:, 0, :], lat[:, 5, :], cosM, ALU.mult)
                N.wait_made(dve, no("kr", 1))
                dve.tensor_tensor(rope2, N.bank(no("kr", 1)), sinM, ALU.mult)
                dr()
                dve.tensor_tensor(lat[:, 5, :], rope1[:, 0, :], rope2, ALU.add).then_inc(taken2, 1)
                for j in range(5):
                    take(N, no("lat", j), lat[:, j, :])
                for j in range(8):
                    dve.tensor_copy(K[64:96, j, :], lat[64:96, 5, :])
                dve.wait_ge(rstd_made, rs + 3)
                norm(lambda k: lat[:, k, :], lambda k: lat[:, k, :], lambda k: p2("qn", k), 0, 3)
                norm(lambda k: lat[:, 3 + k, :], lambda k: lat[:, 3 + k, :], lambda k: p2("kvn", k), 1, 2)
                dr().then_inc(lat_normed, 1)
                rope("q_fm", 8, lambda j: Q[:, j, :], lambda j: Q[:, j, :], cosM, sinM)
                for j in range(8):
                    take(N, no("k_fm", j), K[0:64, j, :], m=64)
                for m in range(TT):
                    take(N, no("v_mla", m), vmla[:, m, :])
                attend(2)
                for t in range(8):
                    merge(N, "merge2", t, 2 * t, False, g0 + 16 + t + 1)

                def residual(name):
                    for t in range(8):
                        n = no(name, t)
                        N.wait_made(dve, n)
                        dve.tensor_tensor(x[:, t, :], N.bank(n), x[:, t, :], ALU.add).then_inc(taken2, 1)
                residual("out")
                dve.wait_ge(rstd_made, rs + 5)
                norm(lambda k: x[:, k, :], lambda k: h[:, k, :], lambda k: p2("norm_x", k), 0, KD, inc=h_made)
                norm(lambda k: mem[:, k, :], lambda k: hm[:, k, :], lambda k: p2("norm_mem", k), 1, KD, MEM, inc=h_made)
                for j in range(4):
                    take(N, no("xq", j), Q[:, j, :])
                for j in range(4):
                    take(N, no("xk", j), K[:, j, 0:MEM], width=MEM)
                for m in range(2):
                    take(N, no("xv", m), vmla[:, m, :])
                attend(3)
                residual("xo")
                dve.wait_ge(rstd_made, rs + 6)
                norm(lambda k: x[:, k, :], lambda k: h[:, k, :], lambda k: p2("norm_ffn", k), 0, KD, inc=h_made)
                for f in range(NFF):
                    n = no("gu", 2 * f + 1)
                    N.wait_made(dve, n)
                    dve.wait_ge(gates_made, g0 + 24 + f + 1)
                    dve.tensor_tensor(act_ff[:, f, :], sig[:, f % 2, :], N.bank(n), ALU.mult).then_inc(taken2, 2)
                residual("down")
                dr().then_inc(x_made, KD)

            dve.wait_ge(rstd_made, R_ONE + LAYERS * R_LAYER + 1)
            norm(lambda k: x[:, k, :], lambda k: h[:, k, :], lambda k: gfinal[:, k:k + 1], 0, KD, inc=out_ready)


SQ_ONE, SQ_LAYER = 4 * KD, 37
H_ONE, H_LAYER = 3 * KD, 4 * KD
R_ONE, R_LAYER = 4, 6
G_LAYER = 24 + NFF


def weight_stream(w):
    stream = np.zeros((SLOTS, P, SLOT * P), np.float32)
    at = [0]

    def put(block, tiles=1):
        s, c = divmod(at[0], SLOT)
        stream[s, 0:block.shape[0], c * P:c * P + block.shape[1]] = block
        at[0] += tiles

    def fm(m, c0, k=KD, width=P):
        for i in range(k):
            put(m[P * i:P * i + P, c0:c0 + width])

    def columns_of(m, parts):
        return np.concatenate([m[:, a:b] for a, b in parts], axis=1)

    def quads(m, k):
        for i in range(k):
            put(m[P * i:P * i + P], 4)

    def align(slots):
        at[0] = slots * SLOT

    ada, win = w["ada_w"][0], w["w_in"][0]
    for i in range(3):
        for k in range(KD):
            for j in range(4):
                put(ada[P * k:P * k + P, 512 * (4 * i + j):512 * (4 * i + j + 1)], 4)
    for g in range(4):
        fm(win, 1568 + P * g)
    fm(win, 0)
    fm(win, P)
    r = np.zeros((D, P), np.float32)
    r[:, 0:16], r[:, 32:48] = win[:, 768:784], win[:, 784:800]
    fm(r, 0)
    fm(win, 800)
    fm(win, 928)
    quads(win[:, 256:768], KD)
    for g in range(4):
        fm(win, 1056 + P * g)
    for t in range(8):
        fm(win, 2080 + P * t)
        fm(w["w_gla_proj"][0], P * t, 4)
        fm(win, 3104 + P * t)
        fm(w["w_pool_proj"][0], P * t, 4)
    for t in range(8):
        fm(w["w_out"][0], P * t)
    assert at[0] == TILES_ONE
    align(SLOTS_ONE)
    for e in range(0, E, 2):
        for half, name in ((0, "w_gate_e"), (0, "w_up_e"), (1, "w_gate_e"), (1, "w_up_e"),
                           (0, "w_down_e"), (1, "w_down_e")):
            for k in range(8):
                for j in range(2):
                    put(w[name][0, e + j, P * k:P * k + P, 512 * half:512 * half + 512], 4)
    for l in range(LAYERS):
        align(SLOTS_ONE + E * SLOTS_EXPERT + l * SLOTS_LAYER)
        start = at[0]
        win = w["w_in_2"][l]

        def head_pairs(c0):
            for t in range(4):
                fm(columns_of(win, [(c0 + 64 * t, c0 + 64 * t + 64), (c0 + 64 * t + 256, c0 + 64 * t + 320)]), 0)

        def merge(b, name):
            for t in range(8):
                fm(win, 2744 + 1024 * b + P * t)
                fm(w[name][l], P * t, 4)
        head_pairs(0)
        fm(win, 512)
        quads(columns_of(win, [(640, 768), (1664, 1792), (1920, 2048), (2048, 2072)]), KD)
        merge(0, "w_br_a_2")
        fm(win, 1280)
        fm(win, 1408)
        head_pairs(768)
        fm(win, 1536)
        fm(win, 1792)
        for name in ("nsa_wk1_2", "nsa_wv1_2"):
            for j in range(32):
                b = np.zeros((P, P), np.float32)
                b[0:64, 0:64] = b[64:, 64:] = w[name][l, 64 * j:64 * j + 64]
                put(b)
        merge(1, "w_br_b_2")
        r = np.zeros((D, P), np.float32)
        r[:, 64:96] = win[:, 2712:2744]
        fm(r, 0)
        for j in range(5):
            fm(win, 2072 + P * j)
        for hh in range(HEADS):
            fm(w["mla_w_q_b_2"][l], MLA_D * hh, 3, MLA_D)
        for hh in range(HEADS):
            fm(w["mla_w_kv_b_2"][l], P * hh, 2, 64)
        quads(columns_of(w["mla_w_kv_b_2"][l], [(P * hh + 64, P * hh + 128) for hh in range(HEADS)]), 2)
        merge(2, "w_br_c_2")
        for t in range(8):
            fm(w["w_out_2"][l], P * t)
        for t in range(4):
            fm(w["w_xq_2"][l], P * t)
        for t in range(4):
            fm(w["w_xkv_2"][l], P * t)
        quads(w["w_xkv_2"][l, :, 512:1024], KD)
        for t in range(8):
            fm(w["w_xo_2"][l], P * t, 4)
        for f in range(NFF):
            fm(w["w_gate_up_2"][l], P * f)
            fm(w["w_gate_up_2"][l], FF + P * f)
        for t in range(8):
            fm(w["w_down_2"][l], P * t, NFF)
        assert at[0] == start + TILES_LAYER
    return stream


def feature_major(a):
    return np.ascontiguousarray(a.T.reshape(-1, P, a.shape[0]).transpose(1, 0, 2))


def tiles_of(v):
    return v.reshape(-1, P).T


def small_weights(w):
    p1 = np.zeros((P, N_PR1), np.float32)

    def put(arr, at, name, v):
        o, n = at[name]
        arr[:, o:o + n] = v

    for name, v in (("ada_b", w["ada_b"][0]), ("g1", w["norm1_g"][0]), ("g2", w["norm2_g"][0]),
                    ("b_decay", w["b_decay"][0]), ("gn", w["gla_norm_g"][0]), ("pool_scale", w["pool_scale"][0]),
                    ("gf", w["final_norm_g"]), ("gfinal", w["norm_final_2"])):
        put(p1, PR1, name, tiles_of(v))
    wup = np.zeros((P, 4, P), np.float32)
    for d in range(2):
        wup[32 * d:32 * d + 16, 2 * d:2 * d + 2] = w["w_decay_up"][0, d].reshape(16, 2, P)
    put(p1, PR1, "wup", wup.reshape(P, -1))
    put(p1, PR1, "wrouter", w["w_router"][0].reshape(KD, P, E).transpose(1, 0, 2).reshape(P, -1))
    put(p1, PR1, "poolw", w["pool_w"][0].transpose(1, 0, 2).reshape(P, -1))
    put(p1, PR1, "c2", np.stack([w["c"][0], w["c_ctx"]], 1).reshape(KD, P, 2).transpose(1, 0, 2).reshape(P, -1))
    p2 = np.zeros((LAYERS, P, N_PR2), np.float32)
    for l in range(LAYERS):
        for name, v in (("norm_mix", "norm_mix_2"), ("norm_x", "norm_xattn_2"), ("norm_mem", "norm_mem_2"),
                        ("norm_ffn", "norm_ffn_2"), ("qn", "mla_q_norm_2"), ("kvn", "mla_kv_norm_2")):
            put(p2[l], PR2, name, tiles_of(w[v][l]))
        put(p2[l], PR2, "sinks", w["swa_sinks_2"][l][None, :])
        for name, v in (("pek", "nsa_pe_k_2"), ("pev", "nsa_pe_v_2")):
            put(p2[l], PR2, name, np.concatenate([w[v][l].T, w[v][l].T], axis=0))
        for name, v in (("w2k", "nsa_wk2_2"), ("w2v", "nsa_wv2_2")):
            o = PR2[name][0]
            p2[l, 0:64, o:o + 64] = p2[l, 64:128, o + 64:o + 128] = w[v][l]
    return p1, p2


def kernel(**inputs):
    import concourse.bacc as _bacc
    from concourse.bass_utils import run_bass_kernel_spmd as _run

    w = {name: np.asarray(a) for name, a in inputs.items()}
    c, c1, ce, inv = constants()
    p1, p2 = small_weights(w)
    arrays = {
        "stream": weight_stream(w), "xT": feature_major(w["x"][0]), "ctxT": feature_major(w["ctx"][0]),
        "memT": feature_major(w["mem_2"][0]),
        "pos": np.ascontiguousarray(np.broadcast_to(w["positions_2"], (P, T))),
        "cst": c, "cs1": c1, "cse": ce, "inv": inv, "pr1": p1, "pr2": p2,
    }
    arrays = {f"in_{name}": a for name, a in arrays.items()}
    nc = _bacc.Bacc("TRN2", target_bir_lowering=False, num_devices=1)
    args = [nc.dram_tensor(name, a.shape, mybir.dt.from_np(a.dtype), kind="ExternalInput").ap()
            for name, a in arrays.items()]
    args.append(nc.dram_tensor("outT", (P, KD, T), F32, kind="ExternalOutput").ap())
    two_blocks(nc, *args)
    r = _run(nc, [arrays], core_ids=[0])
    return r.results[0]["outT"].transpose(2, 1, 0).reshape(1, T, D)
```

```python
from contextlib import ExitStack

import concourse.bass as bass
from concourse import mybir
import numpy as np

F32 = mybir.dt.float32
I32 = mybir.dt.int32
U32 = mybir.dt.uint32
ALU = mybir.AluOpType
ACT = mybir.ActivationFunctionType
AX = mybir.AxisListType

P = 128
T, D, CTX, MEM = 512, 1024, 256, 256
KD, TT = D // P, T // P
DKH, DV, CHUNK = 64, 128, 64
WINDOWS = (2, 4, 8, 16)
ROWS, COLS = T // 64, 64
E, CAP, FE = 16, 2 * T // 16, 1024
LAYERS = 2
HEADS, HD = 8, 64
NCMP = (T - 32) // 16 + 1
FF = 2816
NFF = FF // P
MLA_D, MLA_R, MLA_C = 96, 384, 256
EPS = 1e-6
MASKED = -1e30

SLOT = 16
RING = 4
TILES_ONE = 384 + (4 + 2 + 1 + 2 + 4) * 8 + 32 + 8 * 2 * 12 + 64
TILES_EXPERT = 3 * 64
TILES_LAYER = ((5 + 2 + 6 + 1 + 5) * 8 + 32 + 64 + 24 + 16 + 8 + 3 * 8 * 12 + 64 + 4 * 32
               + NFF * 16 + NFF * 8)


def slots_of(tiles):
    return -(-tiles // (SLOT * RING)) * RING


SLOTS_ONE, SLOTS_EXPERT, SLOTS_LAYER = slots_of(TILES_ONE), TILES_EXPERT // SLOT, slots_of(TILES_LAYER)
SLOTS = SLOTS_ONE + E * SLOTS_EXPERT + LAYERS * SLOTS_LAYER


def numbered(stages):
    first, n = {}, 0
    for name, count in stages:
        first[name] = n
        n += count
    return first, n


ONE, N_ONE = numbered([
    ("rms_x", 1), ("rms_c", 1), ("ada", 1), ("adaT", 1), ("pool", 4), ("k", 4), ("r", 2), ("q", 2), ("v", 2),
    ("poolw", 4), ("zk", 24), ("kv", 22), ("s", 16), ("rms_o", 4), ("merge", 32), ("out", 8),
    ("rms_2", 1), ("h2k", 8), ("logits", 1), ("affT", 1), ("slotT", 1), ("gather", 16), ("selw", 16), ("scatter", 8),
    ("rms_f", 1)])
LAY, N_LAY = numbered([
    ("rms_mix", 1), ("a_fm", 10), ("v", 4), ("ot0", 4), ("merge0", 16),
    ("kcvc", 2), ("b_fm", 12), ("cmp", 4), ("ot1", 4), ("merge1", 16),
    ("lat", 5), ("rms_q", 1), ("rms_kv", 1), ("kr", 2), ("q_fm", 16), ("k_fm", 8), ("v_mla", 4),
    ("ot2", 4), ("rms_m", 1), ("merge2", 16), ("out", 8),
    ("rms_x", 1), ("xk", 4), ("xv", 2), ("xq", 4), ("ot3", 4), ("xo", 8),
    ("rms_f", 1), ("gu", 2 * NFF), ("down", 8)])
BANKS = 3
BANK0 = 5
LAST_DOWN = max(t for t in range(8) if (LAY["down"] + t) % BANKS == 0)


def rope_order(n):
    order = [("raw", 0)]
    for j in range(n):
        if j + 1 < n:
            order.append(("raw", j + 1))
        order.append(("perm", j))
    return order


def columns(parts):
    at, n = {}, 0
    for name, width in parts:
        at[name] = (n, width)
        n += width
    return at, n


CST, N_CST = columns([("ident", P), ("ones", P), ("causal", P), ("recent", P), ("perm", P), ("permM", P),
                      ("cmp_add", TT * NCMP), ("cmp_mul", TT * NCMP), ("freq", 1), ("freqM", 1),
                      ("sign", 1), ("signM", 1), ("eps", 1)])
CS1, N_CS1 = columns([("maskf", P), ("maskb", P), ("scan", 768)])
CSE, N_CSE = columns([("iota", CAP), ("cidx", 1), ("pairsel", 8 * P)])
PR1, N_PR1 = columns([("ada_b", 48), ("g1", 8), ("g2", 8), ("b_decay", 4), ("gn", 1), ("pool_scale", 4),
                      ("gf", 8), ("gfinal", 8), ("wup", 512), ("wrouter", 128), ("poolw", 512), ("c2", 16)])
PR2, N_PR2 = columns([("norm_mix", 8), ("norm_x", 8), ("norm_mem", 8), ("norm_ffn", 8), ("qn", 3), ("kvn", 2),
                      ("sinks", 8), ("pek", 32), ("pev", 32), ("w2k", P), ("w2v", P)])


def constants():
    c = np.zeros((P, N_CST), np.float32)
    r = np.arange(P)

    def put(arr, at, name, v):
        o, w = at[name]
        arr[:, o:o + w] = v

    put(c, CST, "ident", np.eye(P))
    put(c, CST, "ones", 1.0)
    put(c, CST, "causal", np.where(r[None, :] <= r[:, None], 0.0, MASKED))
    put(c, CST, "recent", np.where(r[None, :] > r[:, None], 0.0, MASKED))
    perm = np.zeros((P, P), np.float32)
    for m in range(P):
        perm[(m // 64) * 64 + (m % 64 + 32) % 64, m] = 1.0
    put(c, CST, "perm", perm)
    perm = np.zeros((P, P), np.float32)
    for m in range(64, 96):
        perm[64 + (m - 64 + 16) % 32, m] = 1.0
    put(c, CST, "permM", perm)
    t = np.arange(T).reshape(TT, P)
    ok = (16 * np.arange(NCMP)[None, None, :] + 31) <= t[:, :, None]
    put(c, CST, "cmp_add", np.where(ok, 0.0, MASKED).transpose(1, 0, 2).reshape(P, -1))
    put(c, CST, "cmp_mul", ok.astype(np.float32).transpose(1, 0, 2).reshape(P, -1))
    f = (np.float32(10000.0) ** (-np.arange(32, dtype=np.float32) / np.float32(32))).astype(np.float32)
    put(c, CST, "freq", f[r % 32][:, None])
    f = (np.float32(10000.0) ** (-np.arange(16, dtype=np.float32) / np.float32(16))).astype(np.float32)
    put(c, CST, "freqM", np.where((r >= 64) & (r < 96), f[r % 16], 0.0)[:, None])
    put(c, CST, "sign", np.where(r % 64 < 32, -1.0, 1.0)[:, None])
    put(c, CST, "signM", np.where(r % 32 < 16, -1.0, 1.0)[:, None])
    put(c, CST, "eps", EPS)
    c1 = np.zeros((P, N_CS1), np.float32)
    same = (r[:, None] // CHUNK) == (r[None, :] // CHUNK)
    put(c1, CS1, "maskf", same & (r[:, None] <= r[None, :]))
    put(c1, CS1, "maskb", same & (r[:, None] >= r[None, :]))
    put(c1, CS1, "scan", (np.arange(768) % CHUNK != 0)[None, :])
    ce = np.zeros((P, N_CSE), np.float32)
    put(ce, CSE, "iota", np.arange(CAP)[None, :])
    put(ce, CSE, "cidx", (r % CAP)[:, None])
    sel = np.zeros((P, 8, P), np.float32)
    for p in range(8):
        sel[2 * p, p, :64] = 1.0
        sel[2 * p + 1, p, 64:] = 1.0
    put(ce, CSE, "pairsel", sel.reshape(P, -1))
    inv = np.zeros((4, ROWS, COLS), np.float32)
    for i, w in enumerate(WINDOWS):
        n = [np.clip(np.arange(m) + w // 2, 0, m) - np.clip(np.arange(m) - w // 2, 0, m) for m in (ROWS, COLS)]
        inv[i] = 1.0 / (n[0][:, None] * n[1][None, :])
    return c, c1, ce, np.ascontiguousarray(np.broadcast_to(inv.reshape(1, -1), (P, 4 * T)))


def two_blocks(nc, stream, xT_d, ctxT_d, memT_d, pos_d, cst_d, cs1_d, cse_d, inv_d, pr1_d, pr2_d, out_d):
    ctx = ExitStack()
    with ctx:
        def sb(name, shape, dt=F32):
            return ctx.enter_context(nc.sbuf_tensor(name, shape, dt))

        def sem(name):
            return ctx.enter_context(nc.semaphore(name))

        x = sb("x", [P, KD, T])
        h = sb("h", [P, KD, T])
        ring = sb("ring", [P, RING, SLOT * P])
        cst = sb("cst", [P, N_CST])
        gfinal = sb("gfinal", [P, KD])
        sq = sb("sq", [P, 2, T])
        rstd = sb("rstd", [P, 2, T])
        sig = sb("sig", [P, 2, T])
        tmp = sb("tmp", [P, T])
        y = sb("y", [P, KD, T])
        bank = ctx.enter_context(nc.psum_tensor("bank", [P, 8, 512], F32))

        ARENA = 28096
        arena = sb("arena", [P, ARENA])
        where = [0]

        def carve(n, dims=None, **sizes):
            a = arena[:, where[0]:where[0] + n]
            where[0] += n
            assert where[0] <= ARENA, where[0]
            return a.rearrange(dims, **sizes) if dims else a

        pr1 = carve(N_PR1)
        mods = carve(96, "p (n c) -> p n c", c=2)
        amp = carve(24, "p (s n) -> p s n", s=3)
        moe_from = where[0]
        cs1 = carve(N_CS1)
        c2 = carve(KD * 32, "p (k c) -> p k c", k=KD)
        hc = carve(2048, "p (k t) -> p k t", k=KD)
        qe = hc.rearrange("p k t -> p (k t)").rearrange("p (d t) -> p d t", d=4)
        kq = carve(2560)
        kall = kq[:, 0:1536].rearrange("p (m t) -> p m t", m=2)
        qx = kq[:, 1536:2560].rearrange("p (m t) -> p m t", m=2)
        osq = kq[:, 0:2048].rearrange("p (m t) -> p m t", m=4)
        vall = carve(3072, "p (m t) -> p m t", m=6)
        rbuf = sig[:, :, :].rearrange("p b t -> p (b t)")[:, 0:768]
        pmask = rbuf[:, 0:512].rearrange("p (b d i) -> p b d i", b=2, d=2)
        las = carve(3 * 768, "p (m t) -> p m t", m=3)
        kd = carve(768)
        oT = arena[:, where[0] - 3072:where[0] - 1024].rearrange("p (m t) -> p m t", m=4)
        qm = carve(2048, "p (d t) -> p d t", d=4)
        km = carve(2048, "p (d t) -> p d t", d=4)
        decay = carve(48, "p (d c) -> p d c", d=4)
        gT = carve(2048, "p (m t) -> p m t", m=4)
        mixT = carve(2048, "p (m t) -> p m t", m=4)
        adar = arena[:, where[0] - 2048:where[0] - 1536]
        poolreg = carve(6144)
        SS = poolreg.rearrange("p (d c e) -> p d c e", d=4, c=12)
        adar_late = poolreg[:, 0:1024].rearrange("p (i n) -> p i n", i=2)
        pu = [poolreg[:, 640 * (g % 2):640 * (g % 2) + 640] for g in range(4)]
        pa = [poolreg[:, 1280 + 1920 * b:1280 + 1920 * (b + 1)] for b in range(2)]
        posi = y[:, 7, :].bitcast(I32)
        yflat = y[:, :, :].rearrange("p k t -> p (k t)")
        inv = yflat[:, 0:2048].rearrange("p (g t) -> p g t", g=4)
        pT = yflat[:, 2048:4096].rearrange("p (g t) -> p g t", g=4)
        kdT = yflat[:, 0:3072].rearrange("p (m d c) -> p m d c", m=6, d=4)

        where[0] = moe_from
        cse = carve(N_CSE)
        h2k = carve(4096, "p (m n) -> p m n", m=TT)
        xs_all = carve(8 * D, "p (e k c) -> p e k c", e=8, k=KD)
        yexp = xs_all.rearrange("p e k c -> p e (k c)")
        xsT = carve(D, "p (k c) -> p k c", k=KD)
        sg = carve(2 * 512, "p (b n) -> p b n", b=2)
        acts = carve(FE)
        aT = carve(FE, "p (k c) -> p k c", k=8)
        selx = carve(TT * E * CAP, "p (m e c) -> p m e c", m=TT, e=E)
        selw = arena[:, where[0] - 8 * T:where[0]].rearrange("p (e t) -> p e t", e=8)
        rows = carve(4 * T, "p (a t) -> p a t", a=4)
        affT, work, slot, mark = [rows[0:E, i, :] for i in range(4)]
        aff = carve(3 * TT * E, "p (a m e) -> p a m e", a=3, m=TT)
        stat = carve(2 * TT, "p (a m) -> p a m", a=2)
        slot_tok = carve(TT * E, "p (m e) -> p m e", m=TT)
        top8 = carve(8)[0:E, :]

        where[0] = 0
        cosT, sinT, cosM, sinM = [carve(T) for _ in range(4)]
        pr2 = carve(N_PR2)
        Q = carve(4096, "p (m t) -> p m t", m=8)
        K = carve(4096, "p (m t) -> p m t", m=8)
        V = carve(2048)
        vtok = V[:, 0:TT * 408].rearrange("p (m n) -> p m n", m=TT)
        vmla = V.rearrange("p (m n) -> p m n", m=TT)
        lat = carve(3072, "p (m t) -> p m t", m=6)
        OT = carve(2048, "p (m t) -> p m t", m=4)
        otok = carve(1024, "p (b n) -> p b n", b=2)
        probs = carve(3 * T, "p (b n) -> p b n", b=3)
        probsT = carve(3 * T, "p (b n) -> p b n", b=3)
        rope1 = carve(2 * T, "p (b n) -> p b n", b=2)
        rope2 = carve(T)
        sgate = carve(TT * 24, "p (m n) -> p m n", m=TT)
        cmpb = carve(32 * NCMP, "p (j c) -> p j c", j=32)
        cmp1 = carve(4 * 32, "p (b n) -> p b n", b=4)
        vcmp = carve(P)
        small = carve(6 * 8, "p (a n) -> p a n", a=6)
        nmax, nbias, den, esink, rden, coef = [small[:, i, :] for i in range(6)]
        nsink = carve(8)
        tables = arena[:, 0:4 * T]
        tables_early = h[:, 0:4, :].rearrange("p k t -> p (k t)")
        act_ff = arena[:, N_PR2 + 4 * T:N_PR2 + 4 * T + NFF * T].rearrange("p (f t) -> p f t", f=NFF)
        hm = Q[:, 4:8, :].rearrange("p k t -> p (k t)").rearrange("p (k t) -> p k t", k=KD)
        mem = lat[:, 0:4, :].rearrange("p k t -> p (k t)").rearrange("p (k t) -> p k t", k=KD)

        def c_(name):
            o, w = CST[name]
            return cst[:, o:o + w]

        def p1(name, i=None):
            o, w = PR1[name]
            return pr1[:, o:o + w] if i is None else pr1[:, o + i:o + i + 1]

        def p2(name, i=None):
            o, w = PR2[name]
            return pr2[:, o:o + w] if i is None else pr2[:, o + i:o + i + 1]

        def ce_(name):
            o, w = CSE[name]
            return cse[:, o:o + w]

        landed = [sem(f"landed{i}") for i in range(RING)]
        slot_read = sem("slot_read")
        loaded = sem("loaded")
        loaded_pr1 = sem("loaded_pr1")
        late_made, late_copied, late_turned = sem("late_made"), sem("late_copied"), sem("late_turned")
        loaded_inv = sem("loaded_inv")
        loaded_moe = sem("loaded_moe")
        loaded_pos = sem("loaded_pos")
        loaded_pr2 = sem("loaded_pr2")
        loaded_mem = sem("loaded_mem")
        made1, taken1 = sem("made1"), sem("taken1")
        made2, taken2 = sem("made2"), sem("taken2")
        c2_zero, c2_ready = sem("c2_zero"), sem("c2_ready")
        squared, summed = sem("squared"), sem("summed")
        rstd_made = sem("rstd_made")
        h_made = sem("h_made")
        ctx_made = sem("ctx_made")
        gates_made = sem("gates_made")
        pool_in = sem("pool_in")
        pooled = sem("pooled")
        pool_zero = sem("pool_zero")
        la_in, la_abs, la_log = sem("la_in"), sem("la_abs"), sem("la_log")
        expo_in, expo_out = sem("expo_in"), sem("expo_out")
        kd_made = sem("kd_made")
        gla_ops = sem("gla_ops")
        state_made = sem("state_made")
        masked = sem("masked")
        intra_done = sem("intra_done")
        heads_done = sem("heads_done")
        o_squared = sem("o_squared")
        rstd_o = sem("rstd_o")
        g_silu = sem("g_silu")
        o_made = sem("o_made")
        affx, affe = sem("affx"), sem("affe")
        aff_made, slot_made = sem("aff_made"), sem("slot_made")
        sel_ready, xs_taken = sem("sel_ready"), sem("xs_taken")
        gate_made, up_made, silu_made = sem("gate_made"), sem("up_made"), sem("silu_made")
        a_ready, y_made, y_taken = sem("a_ready"), sem("y_made"), sem("y_taken")
        a_turned, aT_ready = sem("a_turned"), sem("aT_ready")
        x_made = sem("x_made")
        ang_made, sin_made = sem("ang_made"), sem("sin_made")
        layer_done = sem("layer_done")
        scored, biased, exped, cmp_masked = sem("scored"), sem("biased"), sem("exped"), sem("cmp_masked")
        turned, turned_out, pv_made, o_taken = sem("turned"), sem("turned_out"), sem("pv_made"), sem("o_taken")
        tok_done = sem("tok_done")
        sgate_made = sem("sgate_made")
        blocks_made, cmp_silu = sem("blocks_made"), sem("cmp_silu")
        lat_normed = sem("lat_normed")
        kheads_made = sem("kheads_made")
        out_sem = sem("out_sem")
        out_ready = sem("out_ready")

        class Numbers:

            def __init__(self, first, made_sem, taken_sem, base):
                self.first, self.made_sem, self.taken_sem, self.base = first, made_sem, taken_sem, base

            def no(self, name, t=0):
                return self.first[name] + t

            def bank(self, n):
                return bank[:, BANK0 + n % BANKS, :]

            def wait_made(self, eng, n):
                eng.wait_ge(self.made_sem, self.base + n + 1)

            def wait_taken(self, eng, n):
                eng.wait_ge(self.taken_sem, self.base + n + 1)

        def units():
            out = []
            for qt in range(TT):
                for hh in range(HEADS):
                    g, t = hh // 4, hh % 4
                    r = slice(64 * g, 64 * g + 64)
                    k0 = max(0, qt - 1)
                    out.append(dict(sec=0, qt=qt, h=hh, q=Q[r, t, P * qt:P * qt + P], k=K[r, 0, P * k0:P * (qt + 1)],
                                    nk=P * (qt + 1 - k0), kind="window",
                                    v=[vtok[:, j, 0:P] for j in range(k0, qt + 1)], vc=64 * g, sink=hh,
                                    gate=None, first=True, col=64 * hh, last=hh == HEADS - 1))
            for qt in range(TT):
                for branch in range(3):
                    for hh in range(HEADS):
                        g, t = hh // 4, hh % 4
                        r = slice(64 * g, 64 * g + 64)
                        u = dict(sec=1, qt=qt, h=hh, sink=None, gate=(qt, 3 * hh + branch),
                                 first=branch == 0, col=64 * hh, last=branch == 2 and hh == HEADS - 1)
                        if branch == 0:
                            u.update(q=Q[r, t, P * qt:P * qt + P], k=cmp1[r, 2, 0:NCMP], nk=NCMP, kind="cmp",
                                     v=[vcmp[0:NCMP, :]], vc=64 * g)
                        else:
                            u.update(q=Q[r, 4 + t, P * qt:P * qt + P], k=K[r, branch - 1, 0:P * (qt + 1)],
                                     nk=P * (qt + 1), kind="causal", vc=64 * g,
                                     v=[vtok[:, j, P * branch:P * branch + P] for j in range(qt + 1)])
                        out.append(u)
            for qt in range(TT):
                for hh in range(HEADS):
                    out.append(dict(sec=2, qt=qt, h=hh, q=Q[0:MLA_D, hh, P * qt:P * qt + P],
                                    k=K[0:MLA_D, hh, 0:P * (qt + 1)], nk=P * (qt + 1),
                                    kind="causal", v=[vmla[:, j, P * (hh // 2):P * (hh // 2) + P] for j in range(qt + 1)],
                                    vc=64 * (hh % 2),
                                    sink=None, gate=None, first=True, col=64 * hh, last=hh == HEADS - 1))
            for qt in range(TT):
                for hh in range(4):
                    out.append(dict(sec=3, qt=qt, h=hh, q=Q[:, hh, P * qt:P * qt + P], k=K[:, hh, 0:MEM], nk=MEM,
                                    kind="full",
                                    v=[vmla[:, j, P * hh:P * hh + P] for j in range(2)], vc=0,
                                    sink=None, gate=None, first=True, col=P * hh, last=hh == 3))
            for i, u in enumerate(out):
                u["n"] = i
                u["nb"] = -(-u["nk"] // P)
                u["w"] = 128 if u["sec"] == 3 else 64
            return out

        UNITS = units()
        N_UNITS = len(UNITS)
        SECTION = [[u for u in UNITS if u["sec"] == s] for s in range(4)]
        N_CMPU = sum(u["kind"] == "cmp" for u in UNITS)
        cmp_no = {u["n"]: i for i, u in enumerate(u for u in UNITS if u["kind"] == "cmp")}

        block = ctx.enter_context(nc.Block())

        @block.sync
        def _(sp):
            def load(j, s):
                sp.dma_start(ring[:, s, :], stream[bass.ds(j * RING + s, 1)].rearrange("a p n -> p (a n)")
                             ).then_inc(landed[s], 16)
            for s in range(RING):
                sp.dma_start(ring[:, s, :], stream[s]).then_inc(landed[s], 16)
            with sp.Fori(1, SLOTS // RING) as j:
                for s in range(RING):
                    sp.wait_ge(slot_read, j * RING + (s - RING + 1))
                    load(j, s)

        @block.tensor
        def _(pe):
            class Weights:

                def __init__(self, slots_before):
                    self.rot0, self.pos, self.seen, self.back = slots_before, 0, 0, 0
                    self.held = False

                def tile(self, n=1):
                    s = self.pos // SLOT
                    assert (self.pos + n - 1) // SLOT == s
                    if s == self.seen:
                        pe.wait_ge(landed[s % RING], self.rot0 * 16 + 16 * (s // RING + 1))
                        self.seen += 1
                    a = ring[:, s % RING, (self.pos % SLOT) * P:(self.pos % SLOT + n) * P]
                    self.pos += n
                    return a

                def pending(self):
                    if self.held:
                        return 0
                    done = self.pos // SLOT - self.back
                    self.back += done
                    return done

                def finish(self, tiles, slots):
                    assert self.pos == tiles, (self.pos, tiles)
                    while self.seen < slots:
                        pe.wait_ge(landed[self.seen % RING], self.rot0 * 16 + 16 * (self.seen // RING + 1))
                        pe.matmul(bank[0:2, 4, 0:2], ring[:, self.seen % RING, 0:2], ring[:, self.seen % RING, 0:2],
                                  start=True, stop=True)
                        self.seen += 1
                    n = slots - self.back
                    if n:
                        pe.drain().then_inc(slot_read, n)

            W = [None]
            N = [None]

            def mm(out, lhsT, rhs, start, stop, loose=False, hold=False):
                ins = pe.matmul(out, lhsT, rhs, start=start, stop=stop, skip_group_check=loose)
                return ins

            def release():
                n = W[0].pending()
                if n:
                    pe.drain().then_inc(slot_read, n)

            def begin(n):
                if n >= BANKS:
                    N[0].wait_taken(pe, n - BANKS)
                return N[0].bank(n)

            def gemm(n, rhs, nk, width=T, m=P, normed=None):
                b = begin(n)
                for k in range(nk):
                    if normed is not None:
                        pe.wait_ge(h_made, normed + k + 1)
                    ins = mm(b[0:m, 0:width], W[0].tile(), rhs(k), k == 0, k == nk - 1)
                ins.then_inc(N[0].made_sem, 1)
                release()

            def gemm_tok(n0, lhs, count, nk, width):
                quads = [W[0].tile(4) for _ in range(nk)]
                for m in range(count):
                    b = begin(n0 + m)
                    for k in range(nk):
                        ins = mm(b[:, 0:width], lhs(k, m), quads[k][:, 0:width], k == 0, k == nk - 1)
                    ins.then_inc(N[0].made_sem, 1)
                release()

            def rms_sum(n, sq0, nk, width=T):
                b = begin(n)
                for k in range(nk):
                    pe.wait_ge(squared, sq0 + k + 1)
                    ins = mm(b[:, 0:width], c_("ones"), sq[:, k % 2, 0:width], k == 0, k == nk - 1)
                    ins.then_inc(summed, 1)
                pe.drain().then_inc(N[0].made_sem, 1)

            W[0] = Weights(0)
            N[0] = Numbers(ONE, made1, taken1, 0)
            n1 = N[0].no
            pe.wait_ge(c2_ready, 1)

            def ada_step(b, k):
                for j in range(4):
                    ins = mm(b[32 * j:32 * j + 32, :], c2[:, k, :], W[0].tile(4), k == 0, k == KD - 1, loose=True)
                return ins
            ada_bank = begin(n1("ada"))
            for k in range(4):
                ada_step(ada_bank, k)
                release()
            rms_sum(n1("rms_x"), 0, KD)
            rms_sum(n1("rms_c"), KD, KD, CTX)
            for k in range(4, KD):
                ins = ada_step(ada_bank, k)
                if k < KD - 1:
                    release()
            ins.then_inc(made1, 1)
            release()
            N[0].wait_taken(pe, n1("ada"))
            b = begin(n1("adaT"))
            for q in range(4):
                ins = pe.transpose(b[:, P * q:P * q + P], adar[:, P * q:P * q + P], c_("ident"))
            ins.then_inc(made1, 1)
            xh = lambda k: h[:, k, :]
            ch = lambda k: hc[:, k, :]
            for g in range(4):
                gemm(n1("pool", g), xh, KD, normed=0 if g == 0 else None)
            pe.wait_ge(h_made, 2 * KD)

            def gemm2(n):
                ws = [W[0].tile() for _ in range(KD)]
                for i, (src, w) in enumerate(((xh, T), (ch, CTX))):
                    b = begin(n + i)
                    for k in range(KD):
                        ins = mm(b[:, 0:w], ws[k], src(k), k == 0, k == KD - 1)
                    ins.then_inc(made1, 1)
                release()
            gemm2(n1("k", 0))
            gemm2(n1("k", 2))
            gemm2(n1("r"))
            gemm(n1("q", 0), xh, KD)
            gemm(n1("q", 1), xh, KD)
            quads = [W[0].tile(4) for _ in range(KD)]
            W[0].held = True

            def values(n, m):
                b = begin(n)
                for k in range(KD):
                    lhs = hc[:, k, P * m:P * m + P] if m < 2 else h[:, k, P * (m - 2):P * (m - 1)]
                    ins = mm(b, lhs, quads[k], k == 0, k == KD - 1)
                ins.then_inc(made1, 1)
            values(n1("v", 0), 0)
            values(n1("v", 1), 1)
            pwo = PR1["poolw"][0]
            for g in range(4):
                b = begin(n1("poolw", g))
                pe.wait_ge(pooled, g + 1)
                mm(b, pr1[:, pwo + P * g:pwo + P * (g + 1)], pT[:, g, :], True, True).then_inc(made1, 1)
            wuo = PR1["wup"][0]
            N[0].wait_taken(pe, n1("r", 1))
            for d in range(4):
                for i, (o, w) in enumerate(((CTX, T), (0, CTX))):
                    b = begin(n1("zk", 6 * d + i))
                    mm(b[:, 0:w], pr1[:, wuo + P * d:wuo + P * (d + 1)], rbuf[:, o:o + w], True, True
                       ).then_inc(made1, 1)
                values(n1("zk", 6 * d + 2), 2 + d)
                if d == 3:
                    W[0].held = False
                    release()
                gemm(n1("zk", 6 * d + 3), xh, KD)
                pe.wait_ge(kd_made, d + 1)
                for i, (a, b_) in enumerate(((0, 4), (4, 6))):
                    b = begin(n1("zk", 6 * d + 4 + i))
                    for m in range(a, b_):
                        ins = pe.transpose(b[:, P * (m - a):P * (m - a + 1)], kd[:, P * m:P * (m + 1)], c_("ident"))
                    ins.then_inc(made1, 1)
            N[0].wait_taken(pe, n1("zk", 23))
            for i in range(11):
                for dr in range(2):
                    b = begin(n1("kv", 2 * i + dr))
                    c = i if dr == 0 else (3 - i if i < 4 else 15 - i)
                    r = slice(64 * (c % 2), 64 * (c % 2) + 64)
                    for hh in range(4):
                        half = slice(64 * (hh % 2), 64 * (hh % 2) + 64)
                        ins = mm(b[half, P * (hh // 2):P * (hh // 2) + P], kdT[r, c // 2, 2 * dr + hh // 2, half],
                                 vall[r, c // 2, P * hh:P * hh + P], True, True, loose=True)
                    ins.then_inc(made1, 1)
            pe.wait_ge(gla_ops, 4)
            pe.wait_ge(state_made, 11)

            def intra(u):
                hh, m = u // 4, u % 4
                pe.wait_ge(masked, u + 1)
                for dr in range(2):
                    ins = mm(bank[:, hh, P * m:P * (m + 1)], vall[:, 2 + m, P * hh:P * (hh + 1)], pmask[:, u % 2, dr, :],
                             m == 0 and dr == 0, False, loose=True)
                ins.then_inc(intra_done, 1)
                r = slice(64 * (hh % 2), 64 * (hh % 2) + 64)
                for dr in range(2):
                    for c in (2 * m, 2 * m + 1):
                        i = 4 + c if dr == 0 else 11 - c
                        ins = mm(bank[:, hh, CHUNK * c:CHUNK * (c + 1)], SS[r, 2 * dr + hh // 2, i, :],
                                 qe[r, 2 * dr + hh // 2, CHUNK * c:CHUNK * (c + 1)], False,
                                 m == 3 and dr == 1 and c == 7, loose=True)
                if m == 3:
                    ins.then_inc(heads_done, 1)
            for u in range(17):
                if u < 16:
                    hh, m = u // 4, u % 4
                    b = begin(n1("s", u))
                    r = slice(64 * (hh % 2), 64 * (hh % 2) + 64)
                    for dr in range(2):
                        d = 2 * dr + hh // 2
                        ins = mm(b[:, P * dr:P * (dr + 1)], km[r, d, P * m:P * (m + 1)], qm[r, d, P * m:P * (m + 1)],
                                 True, True, loose=True)
                    ins.then_inc(made1, 1)
                if u >= 1:
                    intra(u - 1)
            for hh in range(4):
                b = begin(n1("rms_o", hh))
                pe.wait_ge(o_squared, hh + 1)
                mm(b, c_("ones"), osq[:, hh, :], True, True).then_inc(made1, 1)

            def merge(name, b_no, branches, rhs, first):
                for t in range(8):
                    gemm(N[0].no(name, 2 * (t * branches + b_no) + 0), xh, KD)
                    gemm(N[0].no(name, 2 * (t * branches + b_no) + 1), rhs, 4)
            for t in range(8):
                for b_no, rhs in enumerate((lambda k: oT[:, k, :], lambda k: mixT[:, k, :])):
                    it = 2 * t + b_no
                    if 1 <= it <= 8:
                        for k in (2 * ((it - 1) % 4), 2 * ((it - 1) % 4) + 1):
                            ins = ada_step(bank[:, 4 - (it - 1) // 4, :], k)
                            if k < KD - 1:
                                release()
                        if k == KD - 1:
                            ins.then_inc(late_made, 1)
                            release()
                    if it == 11:
                        pe.wait_ge(late_copied, 2)
                        for i in range(2):
                            for q in range(4):
                                ins = pe.transpose(bank[:, 4 - i, P * q:P * q + P], adar_late[:, i, P * q:P * q + P],
                                                   c_("ident"))
                            ins.then_inc(late_turned, 1)
                    gemm(n1("merge", 4 * t + 2 * b_no), xh, KD)
                    if t == 0 and b_no == 0:
                        pe.wait_ge(o_made, 4)
                    gemm(n1("merge", 4 * t + 2 * b_no + 1), rhs, 4)
            N[0].wait_taken(pe, n1("merge", 31))
            for t in range(8):
                gemm(n1("out", t), lambda k: y[:, k, :], KD)
            W[0].finish(TILES_ONE, SLOTS_ONE)

            rms_sum(n1("rms_2"), 2 * KD, KD)
            pe.wait_ge(h_made, 3 * KD)
            for m in range(TT):
                for half in range(2):
                    b = begin(n1("h2k", 2 * m + half))
                    for k in range(4):
                        ins = pe.transpose(b[:, P * k:P * k + P], h[:, 4 * half + k, P * m:P * m + P], c_("ident"))
                    ins.then_inc(made1, 1)
            b = begin(n1("logits"))
            wro = PR1["wrouter"][0]
            for m in range(TT):
                for k in range(KD):
                    ins = mm(b[:, E * m:E * m + E], h[:, k, P * m:P * m + P], pr1[:, wro + E * k:wro + E * k + E],
                             k == 0, k == KD - 1)
            ins.then_inc(made1, 1)
            b = begin(n1("affT"))
            pe.wait_ge(aff_made, 1)
            for m in range(TT):
                ins = pe.transpose(b[0:E, P * m:P * m + P], aff[:, 2, m, :], c_("ident"))
            ins.then_inc(made1, 1)
            b = begin(n1("slotT"))
            pe.wait_ge(slot_made, 1)
            for m in range(TT):
                ins = pe.transpose(b[:, E * m:E * m + E], slot[:, P * m:P * m + P], c_("ident")[0:E, 0:E])
            ins.then_inc(made1, 1)

            for k in range(KD):
                for half in range(2):
                    b = begin(n1("gather", 2 * k + half))
                    for m in range(TT):
                        if k == 0 and half == 0:
                            pe.wait_ge(sel_ready, m + 1)
                        ins = mm(b, h2k[:, m, P * k:P * k + P],
                                 selx[:, m, 8 * half:8 * half + 8, :].rearrange("p e c -> p (e c)"),
                                 m == 0, m == TT - 1)
                    ins.then_inc(made1, 1)

            N[0].wait_taken(pe, n1("gather", 15))
            with pe.Fori(0, E // 2) as pair:
                W[0] = Weights(pair * (2 * SLOTS_EXPERT // RING) + SLOTS_ONE // RING)

                def both(b, lhs):
                    for k in range(8):
                        for j in range(2):
                            ins = mm(b[64 * j:64 * j + 64, :], lhs(k)[:, 64 * j:64 * j + 64], W[0].tile(4),
                                     k == 0, k == 7)
                        if k == 3:
                            release()
                    return ins
                pe.wait_ge(xs_taken, pair + 1)
                for half in range(2):
                    both(bank[:, half, :], lambda k: xsT[:, k, :]).then_inc(gate_made, 1)
                    release()
                    both(bank[:, 2 + half, :], lambda k: xsT[:, k, :]).then_inc(up_made, 1)
                    release()
                for half in range(2):
                    pe.wait_ge(a_ready, pair * 2 + (half + 1))
                    for k in range(4):
                        ins = pe.transpose(bank[:, 4 + half, P * k:P * k + P],
                                           acts[:, P * (4 * half + k):P * (4 * half + k) + P], c_("ident"))
                    ins.then_inc(a_turned, 1)
                pe.wait_ge(aT_ready, pair * 2 + 2)
                for half in range(2):
                    both(bank[:, 6 + half, :], lambda k: aT[:, k, :]).then_inc(y_made, 1)
                    release()
                W[0].finish(2 * TILES_EXPERT, 2 * SLOTS_EXPERT)

            pe.wait_ge(y_taken, E)
            so = CSE["pairsel"][0]
            for p in range(8):
                for i, src in enumerate((slot, affT)):
                    b = begin(n1("selw", 2 * p + i))
                    mm(b, cse[0:E, so + P * p:so + P * p + P], src, True, True).then_inc(made1, 1)
            N[0].wait_taken(pe, n1("selw", 15))
            for t in range(8):
                b = begin(n1("scatter", t))
                for p in range(8):
                    ins = mm(b, yexp[:, p, P * t:P * t + P], selw[:, p, :], p == 0, p == 7)
                ins.then_inc(made1, 1)
            rms_sum(n1("rms_f"), 3 * KD, KD)

            with pe.Fori(0, LAYERS) as l:
                W[0] = Weights(l * (SLOTS_LAYER // RING) + (SLOTS_ONE + E * SLOTS_EXPERT) // RING)
                N[0] = Numbers(LAY, made2, taken2, l * N_LAY)
                no = N[0].no
                ub = l * N_UNITS
                sq0 = l * SQ_LAYER + SQ_ONE

                def rope(name, n_tiles, rhs, nk, perm, raw, m=P, normed=None):
                    for i, (what, j) in enumerate(rope_order(n_tiles)):
                        if what == "raw":
                            gemm(no(name, i), rhs, nk, normed=normed if i == 0 else None)
                        else:
                            b = begin(no(name, i))
                            N[0].wait_taken(pe, no(name, rope_order(n_tiles).index(("raw", j))))
                            mm(b[0:m, :], c_(perm)[0:m, 0:m], raw(j)[0:m], True, True).then_inc(made2, 1)

                def attend(sec):
                    us = SECTION[sec]
                    first = us[0]["n"]
                    for s in range(len(us) + 5):
                        if s < len(us):
                            u = us[s]
                            n = u["n"]
                            if s >= 3:
                                pe.wait_ge(exped, ub + n - 2)
                            mm(bank[:, n % 3, 0:u["nk"]], u["q"], u["k"], True, True).then_inc(scored, 1)
                        if 2 <= s <= len(us) + 1:
                            u = us[s - 2]
                            n = u["n"]
                            pe.wait_ge(exped, ub + n + 1)
                            if u["kind"] == "cmp":
                                pe.wait_ge(cmp_masked, l * N_CMPU + cmp_no[n] + 1)
                            if s - 2 >= 2:
                                pe.wait_ge(turned_out, ub + n - 1)
                            for b in range(u["nb"]):
                                w = min(P, u["nk"] - P * b)
                                ins = pe.transpose(bank[0:w, 3 + n % 2, P * b:P * b + P],
                                                   probs[:, n % 3, P * b:P * b + w], c_("ident"))
                            ins.then_inc(turned, 1)
                        if 4 <= s <= len(us) + 3:
                            u = us[s - 4]
                            n = u["n"]
                            pe.wait_ge(turned_out, ub + n + 1)
                            if s - 4 >= 2:
                                pe.wait_ge(o_taken, ub + n - 1)
                            for b in range(u["nb"]):
                                w = min(P, u["nk"] - P * b)
                                ins = mm(bank[:, 5 + n % 2, 0:P],
                                         probsT[0:w, n % 3, P * b:P * b + P], u["v"][b], b == 0, b == u["nb"] - 1)
                            ins.then_inc(pv_made, 1)
                        if s >= 5 and us[s - 5]["last"]:
                            qt = us[s - 5]["qt"]
                            n = no(f"ot{sec}", qt)
                            if qt >= 1:
                                N[0].wait_taken(pe, n - 1)
                            b = bank[:, 7, :]
                            pe.wait_ge(tok_done, l * 16 + 4 * sec + qt + 1)
                            for k in range(4):
                                ins = pe.transpose(b[:, P * k:P * k + P], otok[:, qt % 2, P * k:P * k + P], c_("ident"))
                            ins.then_inc(made2, 1)
                    N[0].wait_taken(pe, no(f"ot{sec}", 3))

                def merge(b_no):
                    for t in range(8):
                        gemm(no(f"merge{b_no}", 2 * t), xh, KD)
                        gemm(no(f"merge{b_no}", 2 * t + 1), lambda k: OT[:, k, :], 4)

                pe.wait_ge(x_made, l * KD + LAST_DOWN + 1)
                rms_sum(no("rms_mix"), sq0, KD)
                hb = l * H_LAYER + H_ONE
                rope("a_fm", 5, xh, KD, "perm", lambda j: (Q[:, j, :] if j < 4 else K[:, 0, :]), normed=hb)
                gemm_tok(no("v"), lambda k, m: h[:, k, P * m:P * m + P], TT, KD, 408)
                N[0].wait_taken(pe, no("v", 3))
                attend(0)
                merge(0)

                gemm(no("kcvc", 0), xh, KD)
                gemm(no("kcvc", 1), xh, KD)
                rope("b_fm", 6, xh, KD, "perm", lambda j: (Q[:, j, :] if j < 4 else K[:, j - 4, :]))
                for i in range(2):
                    b = begin(no("cmp", i))
                    pe.wait_ge(blocks_made, l * 2 + i + 1)
                    for j in range(32):
                        ins = mm(b[:, 0:NCMP], W[0].tile(), cmpb[:, j, :], j == 0, j == 31)
                    ins.then_inc(made2, 1)
                    release()
                pe.wait_ge(cmp_silu, l * 2 + 2)
                b = begin(no("cmp", 2))
                mm(b[:, 0:NCMP], p2("w2k"), cmp1[:, 0, 0:NCMP], True, True).then_inc(made2, 1)
                b = begin(no("cmp", 3))
                mm(b[0:NCMP, 0:P], cmp1[:, 1, 0:NCMP], p2("w2v"), True, True).then_inc(made2, 1)
                N[0].wait_taken(pe, no("cmp", 3))
                attend(1)
                merge(1)

                for j in range(5):
                    gemm(no("lat", j), xh, KD)
                rms_sum(no("rms_q"), sq0 + 8, 3)
                rms_sum(no("rms_kv"), sq0 + 11, 2)
                gemm(no("kr", 0), xh, KD)
                b = begin(no("kr", 1))
                N[0].wait_taken(pe, no("kr", 0))
                mm(b, c_("permM"), lat[:, 5, :], True, True).then_inc(made2, 1)
                pe.wait_ge(lat_normed, l + 1)
                rope("q_fm", 8, lambda k: lat[:, k, :], 3, "permM", lambda j: Q[:, j, :])
                for j in range(8):
                    gemm(no("k_fm", j), lambda k: lat[:, 3 + k, :], 2)
                gemm_tok(no("v_mla"), lambda k, m: lat[:, 3 + k, P * m:P * m + P], TT, 2, 512)
                N[0].wait_taken(pe, no("v_mla", 3))
                attend(2)
                rms_sum(no("rms_m"), sq0 + 13, KD, MEM)
                merge(2)
                N[0].wait_taken(pe, no("merge2", 15))
                for t in range(8):
                    gemm(no("out", t), lambda k: y[:, k, :], KD)

                rms_sum(no("rms_x"), sq0 + 21, KD)
                pe.wait_ge(h_made, hb + 2 * KD)
                for j in range(4):
                    gemm(no("xk", j), lambda k: hm[:, k, :], KD, MEM)
                gemm_tok(no("xv"), lambda k, m: hm[:, k, P * m:P * m + P], 2, KD, 512)
                for j in range(4):
                    gemm(no("xq", j), xh, KD, normed=hb + 2 * KD if j == 0 else None)
                N[0].wait_taken(pe, no("xq", 3))
                attend(3)
                for t in range(8):
                    gemm(no("xo", t), lambda k: OT[:, k, :], 4)

                rms_sum(no("rms_f"), sq0 + 29, KD)
                for f in range(NFF):
                    gemm(no("gu", 2 * f), xh, KD, normed=hb + 3 * KD if f == 0 else None)
                    gemm(no("gu", 2 * f + 1), xh, KD)
                N[0].wait_taken(pe, no("gu", 2 * NFF - 1))
                for t in range(8):
                    gemm(no("down", t), lambda k: act_ff[:, k, :], NFF)
                W[0].finish(TILES_LAYER, SLOTS_LAYER)

            rms_sum_final = Numbers({"rms_final": 0}, made1, taken1, N_ONE)
            N[0] = rms_sum_final
            b = bank[:, BANK0, :]
            pe.wait_ge(x_made, LAYERS * KD + LAST_DOWN + 1)
            for k in range(KD):
                pe.wait_ge(squared, SQ_ONE + LAYERS * SQ_LAYER + k + 1)
                mm(b, c_("ones"), sq[:, k % 2, :], k == 0, k == KD - 1).then_inc(summed, 1)
            pe.drain().then_inc(made1, 1)

        @block.scalar
        def _(act):
            act.dma_start(pr1, pr1_d).then_inc(loaded_pr1, 16)
            act.dma_start(x[:, :, :], xT_d).then_inc(loaded, 16)
            act.dma_start(cst[:, :], cst_d).then_inc(loaded, 16)
            act.dma_start(hc, ctxT_d).then_inc(loaded, 16)
            act.dma_start(cs1, cs1_d).then_inc(loaded, 16)
            act.dma_start(yflat[:, 0:2048], inv_d).then_inc(loaded_inv, 16)

            def squares(src, nk, base, width=T, ready=None):
                for k in range(nk):
                    if ready is not None:
                        ready(k)
                    n = base + k
                    if not (isinstance(n, int) and n < 2):
                        act.wait_ge(summed, n - 1)
                    act.activation(sq[:, k % 2, 0:width], src(k), ACT.Square).then_inc(squared, 1)

            def inv_root(N, n, slot_, features, width=T):
                N.wait_made(act, n)
                act.activation(rstd[:, slot_, 0:width], N.bank(n)[:, 0:width], ACT.Ln, bias=c_("eps"),
                               scale=1.0 / features).then_inc(N.taken_sem, 1)
                act.drain()
                act.activation(rstd[:, slot_, 0:width], rstd[:, slot_, 0:width], ACT.Exp, scale=-0.5
                               ).then_inc(rstd_made, 1)

            N = Numbers(ONE, made1, taken1, 0)
            n1 = N.no
            act.wait_ge(loaded_pr1, 16)
            act.wait_ge(c2_zero, 1)
            act.activation(c2[:, :, 0:2], p1("c2").rearrange("p (k c) -> p k c", c=2), ACT.Silu).then_inc(c2_ready, 1)
            act.wait_ge(loaded, 16 * 4)
            squares(lambda k: x[:, k, :], KD, 0)
            squares(lambda k: hc[:, k, :], KD, KD, CTX)
            inv_root(N, n1("rms_x"), 0, D)
            inv_root(N, n1("rms_c"), 1, D, CTX)
            for d in range(4):
                act.wait_ge(la_in, d + 1)
                act.activation(las[:, 1, :], las[:, 0, :], ACT.Abs)
                act.drain()
                act.activation(las[:, 1, :], las[:, 1, :], ACT.Exp, scale=-1.0)
                act.drain()
                act.activation(las[:, 1, :], las[:, 1, :], ACT.Ln, bias=1.0).then_inc(la_log, 1)
                s = 1.0 / 16.0
                act.wait_ge(expo_in, d + 1)
                act.activation(decay[:, d, :], las[:, 0, :].rearrange("p (c t) -> p c t", c=12)[:, :, 63 if d < 2 else 0],
                               ACT.Exp, scale=s)
                act.activation(qe[:, d, :], las[:, 0, CTX:], ACT.Exp, scale=s)
                act.activation(qm[:, d, :], las[:, 1, CTX:], ACT.Exp, scale=s)
                act.activation(km[:, d, :], las[:, 1, CTX:], ACT.Exp, scale=-s)
                if d >= 1:
                    N.wait_made(act, n1("zk", 6 * d - 1))
                act.activation(kd, las[:, 2, :], ACT.Exp, scale=-s).then_inc(expo_out, 1)
            for hh in range(4):
                N.wait_taken(act, n1("zk", 6 * hh + 3))
                act.activation(gT[:, hh, :], gT[:, hh, :], ACT.Silu).then_inc(g_silu, 1)
            for hh in range(4):
                act.wait_ge(heads_done, hh + 1)
                act.activation(osq[:, hh, :], bank[:, hh, :], ACT.Square).then_inc(o_squared, 1)
            N.wait_taken(act, n1("s", 15))
            for hh in range(4):
                n = n1("rms_o", hh)
                N.wait_made(act, n)
                if hh >= 2:
                    act.wait_ge(o_made, hh - 1)
                act.activation(rstd[:, hh % 2, :], N.bank(n), ACT.Ln, bias=c_("eps"), scale=1.0 / DV
                               ).then_inc(taken1, 1)
                act.drain()
                act.activation(rstd[:, hh % 2, :], rstd[:, hh % 2, :], ACT.Exp, scale=-0.5).then_inc(rstd_o, 1)

            def gates(N, name, count, func, base, out=None):
                for t in range(count):
                    N.wait_made(act, N.no(name, 2 * t))
                    if t >= 2:
                        N.wait_taken(act, N.no(name, 2 * t - 3))
                    act.activation(sig[:, t % 2, :], N.bank(N.no(name, 2 * t)), func).then_inc(gates_made, 1)
            gates(N, "merge", 16, ACT.Sigmoid, 0)
            N.wait_taken(act, n1("merge", 31))
            act.dma_start(cse, cse_d).then_inc(loaded_moe, 16)
            N.wait_made(act, n1("out", 7))
            act.dma_start(posi, pos_d).then_inc(loaded_pos, 16)
            squares(lambda k: x[:, k, :], KD, 2 * KD, ready=lambda k: N.wait_taken(act, n1("out", k)))
            inv_root(N, n1("rms_2"), 0, D)
            act.wait_ge(affx, 1)
            act.activation(aff[:, 1, :, :], aff[:, 0, :, :], ACT.Exp).then_inc(affe, 1)
            for i, (s_, c_t) in enumerate(((h[:, 1, :], h[:, 0, :]), (h[:, 3, :], h[:, 2, :]))):
                act.wait_ge(ang_made, i + 1)
                act.activation(c_t, s_, ACT.Sin, scale=0.5)
                act.activation(s_, s_, ACT.Sin).then_inc(sin_made, 1)

            with act.Fori(0, E // 2) as pair:
                for half in range(2):
                    act.wait_ge(gate_made, pair * 2 + (half + 1))
                    act.activation(sg[:, half, :], bank[:, half, :], ACT.Silu).then_inc(silu_made, 1)
                for half in range(2):
                    act.wait_ge(a_turned, pair * 2 + (half + 1))
                    act.activation(aT[:, 4 * half:4 * half + 4, :].rearrange("p k c -> p (k c)"),
                                   bank[:, 4 + half, :], ACT.Copy).then_inc(aT_ready, 1)
            squares(lambda k: x[:, k, :], KD, 3 * KD, ready=lambda k: N.wait_taken(act, n1("scatter", k)))
            inv_root(N, n1("rms_f"), 0, D)

            with act.Fori(0, LAYERS) as l:
                N = Numbers(LAY, made2, taken2, l * N_LAY)
                no = N.no
                ub = l * N_UNITS
                sq0 = l * SQ_LAYER + SQ_ONE

                def attend(sec):
                    us = SECTION[sec]
                    for s in range(len(us) + 5):
                        if s < len(us):
                            u = us[s]
                            n = u["n"]
                            act.wait_ge(biased, ub + n + 1)
                            if s >= 3:
                                act.wait_ge(turned, ub + n - 2)
                            if u["sink"] is not None:
                                act.activation(esink[:, n % 8:n % 8 + 1], p2("sinks", u["sink"]), ACT.Exp,
                                               bias=nbias[:, n % 8:n % 8 + 1])
                            act.activation(probs[:, n % 3, 0:u["nk"]], bank[:, n % 3, 0:u["nk"]], ACT.Exp,
                                           bias=nbias[:, n % 8:n % 8 + 1],
                                           accum_out=den[:, n % 8:n % 8 + 1]).then_inc(exped, 1)
                        if 2 <= s <= len(us) + 1:
                            u = us[s - 2]
                            n = u["n"]
                            act.wait_ge(turned, ub + n + 1)
                            if s - 2 >= 3:
                                act.wait_ge(pv_made, ub + n - 2)
                            w = min(P, u["nk"])
                            act.activation(probsT[0:w, n % 3, 0:P * u["nb"]], bank[0:w, 3 + n % 2, 0:P * u["nb"]],
                                           ACT.Copy).then_inc(turned_out, 1)
                        if s >= 5 and us[s - 5]["last"]:
                            qt = us[s - 5]["qt"]
                            n = no(f"ot{sec}", qt)
                            N.wait_made(act, n)
                            act.activation(OT[:, :, P * qt:P * qt + P],
                                           bank[:, 7, :].rearrange("p (k t) -> p k t", k=4), ACT.Copy
                                           ).then_inc(taken2, 1)

                act.wait_ge(x_made, l * KD + 1)
                act.dma_start(pr2, pr2_d[bass.ds(l, 1)].rearrange("a p n -> p (a n)")).then_inc(loaded_pr2, 16)
                squares(lambda k: x[:, k, :], KD, sq0, ready=lambda k: act.wait_ge(x_made, l * KD + k + 1))
                inv_root(N, no("rms_mix"), 0, D)
                N.wait_taken(act, no("v", 3))
                act.activation(sgate, vtok[:, :, 384:408], ACT.Sigmoid).then_inc(sgate_made, 1)
                attend(0)
                gates(N, "merge0", 8, ACT.Sigmoid, 0)
                N.wait_taken(act, no("b_fm", 11))
                for i in range(2):
                    N.wait_made(act, no("cmp", i))
                    act.activation(cmp1[:, i, 0:NCMP], N.bank(no("cmp", i))[:, 0:NCMP], ACT.Silu
                                   ).then_inc(taken2, 1)
                    act.drain().then_inc(cmp_silu, 1)
                attend(1)
                gates(N, "merge1", 8, ACT.Sigmoid, 0)
                squares(lambda k: lat[:, k, :], 3, sq0 + 8, ready=lambda k: N.wait_taken(act, no("lat", k)))
                for k in range(2):
                    N.wait_taken(act, no("lat", 3 + k))
                    act.wait_ge(summed, sq0 + 11)
                    act.activation(sq[:, k % 2, :], lat[:, 3 + k, :], ACT.Square).then_inc(squared, 1)
                inv_root(N, no("rms_q"), 0, MLA_R)
                inv_root(N, no("rms_kv"), 1, MLA_C)
                N.wait_made(act, no("v_mla", 3))
                act.dma_start(mem, memT_d).then_inc(loaded_mem, 16)
                attend(2)
                act.wait_ge(loaded_mem, l * 16 + 16)
                squares(lambda k: mem[:, k, :], KD, sq0 + 13, MEM)
                inv_root(N, no("rms_m"), 1, D, MEM)
                gates(N, "merge2", 8, ACT.Sigmoid, 0)
                squares(lambda k: x[:, k, :], KD, sq0 + 21, ready=lambda k: N.wait_taken(act, no("out", k)))
                inv_root(N, no("rms_x"), 0, D)
                attend(3)
                squares(lambda k: x[:, k, :], KD, sq0 + 29, ready=lambda k: N.wait_taken(act, no("xo", k)))
                inv_root(N, no("rms_f"), 0, D)
                gates(N, "gu", NFF, ACT.Silu, 0)

            squares(lambda k: x[:, k, :], KD, SQ_ONE + LAYERS * SQ_LAYER,
                    ready=lambda k: act.wait_ge(x_made, LAYERS * KD + k + 1))
            act.wait_ge(made1, N_ONE + 1)
            act.activation(rstd[:, 0, :], bank[:, BANK0, :], ACT.Ln, bias=c_("eps"), scale=1.0 / D)
            act.drain()
            act.activation(rstd[:, 0, :], rstd[:, 0, :], ACT.Exp, scale=-0.5).then_inc(rstd_made, 1)
            for k in range(KD):
                act.wait_ge(out_ready, k + 1)
                act.dma_start(out_d[:, k, :], h[:, k, :]).then_inc(out_sem, 16)
            act.wait_ge(out_sem, 16 * KD)

        @block.gpsimd
        def _(pool):
            pool.memset(c2, 0.0).then_inc(c2_zero, 1)
            pool.memset(poolreg, 0.0)
            pool.drain().then_inc(pool_zero, 1)
            pool.wait_ge(loaded_inv, 16)
            for g, w in enumerate(WINDOWS):
                pool.wait_ge(pool_in, g + 1)
                u = pu[g].rearrange("p (r c) -> p r c", r=ROWS)
                src, at, lo = u, 0, 0
                s = 1
                lo, hi = 0, 80
                while s < w:
                    dst = pa[at][:, 0:640].rearrange("p (r c) -> p r c", r=ROWS)
                    a, b = (1, 0) if s == 1 else (s // 2, s // 2)
                    lo, hi = lo + a, hi - b
                    pool.tensor_tensor(dst[:, :, lo:hi], src[:, :, lo - a:hi - a], src[:, :, lo + b:hi + b], ALU.add)
                    pool.drain()
                    src, at, s = dst, 1 - at, 2 * s
                base = [pa[i].rearrange("p (r c) -> p r c", c=80)[:, :, 0:64] for i in range(2)]
                if at == 1:
                    keep = pa[1][:, 0:640].rearrange("p (r c) -> p r c", r=ROWS)
                    pool.tensor_copy(keep[:, :, 8:72], src[:, :, 8:72])
                    pool.drain()
                    src = keep
                pool.memset(pa[0], 0.0)
                pool.drain()
                pool.tensor_copy(base[0][:, 8:16, :], src[:, :, 8:72])
                pool.drain()
                src, at, s, lo, hi = base[0], 1, 1, 0, 24
                while s < w:
                    dst = base[at]
                    a, b = (1, 0) if s == 1 else (s // 2, s // 2)
                    lo, hi = lo + a, hi - b
                    pool.tensor_tensor(dst[:, lo:hi, :], src[:, lo - a:hi - a, :], src[:, lo + b:hi + b, :], ALU.add)
                    pool.drain()
                    src, at, s = dst, 1 - at, 2 * s
                out = pT[:, g, :].rearrange("p (r c) -> p r c", r=ROWS)
                pool.tensor_tensor(out, src[:, 8:16, :], inv[:, g, :].rearrange("p (r c) -> p r c", r=ROWS), ALU.mult)
                pool.drain()
                pool.tensor_tensor(out, out, u[:, :, 8:72], ALU.subtract).then_inc(pooled, 1)

        @block.vector
        def _(dve):
            dr = dve.drain
            N = Numbers(ONE, made1, taken1, 0)
            n1 = N.no

            def take(N, n, out, src=None, m=P, width=512):
                N.wait_made(dve, n)
                dve.tensor_copy(out, N.bank(n)[0:m, 0:width] if src is None else src).then_inc(N.taken_sem, 1)

            def norm(src, dst, gain, slot_, nk, width=T, shift=None, inc=None):
                for k in range(nk):
                    ins = dve.scalar_tensor_tensor(out=dst(k), in0=src(k), scalar=gain(k), in1=rstd[:, slot_, 0:width],
                                                   op0=ALU.mult, op1=ALU.mult)
                    if shift is None and inc is not None:
                        ins.then_inc(inc, 1)
                if shift is not None:
                    dr()
                    for k in range(nk):
                        ins = dve.tensor_scalar(dst(k), dst(k), shift(k), None, ALU.add)
                        if inc is not None:
                            ins.then_inc(inc, 1)

            dve.wait_ge(loaded_pr1, 16)
            dve.tensor_copy(gfinal[:, :], p1("gfinal"))
            dve.wait_ge(loaded, 16 * 4)
            dve.wait_ge(rstd_made, 2)

            def modulations(i, turned_):
                return dve.tensor_tensor(mods[:, 16 * i:16 * i + 16, :].rearrange("p (j q) c -> p j q c", j=4),
                                         turned_.rearrange("p (q j r) -> p j q r", q=4, j=4)[:, :, :, 0:2],
                                         p1("ada_b")[:, 16 * i:16 * i + 16].rearrange("p (j q c) -> p j q c", j=4, c=1)
                                         .to_broadcast([P, 4, 4, 2]), ALU.add)

            def gain(i, at, c, g):
                dve.scalar_tensor_tensor(out=amp[:, i, :], in0=mods[:, at:at + 8, c], scalar=1.0, in1=p1(g),
                                         op0=ALU.add, op1=ALU.mult)
            take(N, n1("ada"), adar)
            N.wait_made(dve, n1("adaT"))
            modulations(0, N.bank(n1("adaT"))).then_inc(taken1, 1)
            dr()
            gain(0, 8, 0, "g1")
            gain(1, 8, 1, "g1")
            dr()
            norm(lambda k: x[:, k, :], lambda k: h[:, k, :], lambda k: amp[:, 0, k:k + 1], 0, KD,
                 shift=lambda k: mods[:, k, 0:1], inc=h_made)
            norm(lambda k: hc[:, k, :], lambda k: hc[:, k, :], lambda k: amp[:, 1, k:k + 1], 1, KD, CTX,
                 shift=lambda k: mods[:, k, 1:2], inc=h_made)
            dve.wait_ge(pool_zero, 1)
            for g in range(4):
                N.wait_made(dve, n1("pool", g))
                if g >= 2:
                    dve.wait_ge(pooled, g - 1)
                dve.tensor_copy(pu[g].rearrange("p (r c) -> p r c", r=ROWS)[:, :, 8:72],
                                N.bank(n1("pool", g)).rearrange("p (r c) -> p r c", r=ROWS)).then_inc(taken1, 1)
                dr().then_inc(pool_in, 1)
            for j in range(2):
                take(N, n1("k", 2 * j), kall[:, j, CTX:])
                take(N, n1("k", 2 * j + 1), kall[:, j, 0:CTX], width=CTX)
            take(N, n1("r"), rbuf[:, CTX:])
            take(N, n1("r", 1), rbuf[:, 0:CTX], width=CTX)
            for j in range(2):
                N.wait_made(dve, n1("q", j))
                dve.tensor_scalar(qx[:, j, :], N.bank(n1("q", j)), DKH ** -0.5, None, ALU.mult).then_inc(taken1, 1)
            for m in range(2):
                take(N, n1("v", m), vall[:, m, :])
            for g in range(4):
                N.wait_made(dve, n1("poolw", g))
                dve.tensor_scalar(mixT[:, g, :], N.bank(n1("poolw", g)), p1("pool_scale", g), None, ALU.mult
                                  ).then_inc(taken1, 1)
            for d in range(4):
                if d >= 1:
                    dve.wait_ge(expo_out, d)
                for i, (o, w) in enumerate(((CTX, T), (0, CTX))):
                    n = n1("zk", 6 * d + i)
                    N.wait_made(dve, n)
                    dve.tensor_scalar(las[:, 0, o:o + w], N.bank(n)[:, 0:w], p1("b_decay", d), None, ALU.add
                                      ).then_inc(taken1, 1)
                dr().then_inc(la_in, 1)
                dve.wait_ge(la_log, d + 1)
                dve.scalar_tensor_tensor(out=las[:, 2, :], in0=las[:, 0, :], scalar=0.0, in1=las[:, 1, :],
                                         op0=ALU.min, op1=ALU.subtract)
                dr()
                so = CS1["scan"][0]
                dve.tensor_tensor_scan(las[:, 0, :], cs1[:, so:so + 768], las[:, 2, :], 0.0, ALU.mult, ALU.add)
                dr()
                ch = lambda a: a.rearrange("p (c t) -> p c t", c=12)
                if d >= 2:
                    dve.tensor_tensor(las[:, 1, :], las[:, 2, :], las[:, 0, :], ALU.subtract)
                    dr()
                    dve.tensor_tensor(ch(las[:, 1, :]), ch(las[:, 1, :]),
                                      ch(las[:, 0, :])[:, :, 63:64].to_broadcast([P, 12, CHUNK]), ALU.add)
                    dr()
                    dve.tensor_copy(las[:, 0, :], las[:, 1, :])
                    dr()
                mid, last = (31, 63) if d < 2 else (32, 0)
                b = ch(las[:, 0, :])
                dve.tensor_tensor(ch(las[:, 1, :]), b, b[:, :, mid:mid + 1].to_broadcast([P, 12, CHUNK]), ALU.subtract)
                dve.tensor_tensor(ch(las[:, 2, :]), b, b[:, :, last:last + 1].to_broadcast([P, 12, CHUNK]), ALU.subtract)
                dr().then_inc(expo_in, 1)
                dve.wait_ge(expo_out, d + 1)
                pr = d % 2
                dve.tensor_tensor(kd, kd, kall[:, pr, :], ALU.mult).then_inc(kd_made, 1)
                dve.tensor_tensor(qe[:, d, :], qe[:, d, :], qx[:, pr, :], ALU.mult)
                dve.tensor_tensor(qm[:, d, :], qm[:, d, :], qx[:, pr, :], ALU.mult)
                dve.tensor_tensor(km[:, d, :], km[:, d, :], kall[:, pr, CTX:], ALU.mult).then_inc(gla_ops, 1)
                take(N, n1("zk", 6 * d + 2), vall[:, 2 + d, :])
                take(N, n1("zk", 6 * d + 3), gT[:, d, :])
                for i, (a, b_) in enumerate(((0, 4), (4, 6))):
                    n = n1("zk", 6 * d + 4 + i)
                    N.wait_made(dve, n)
                    dve.tensor_copy(kdT[:, a:b_, d, :],
                                    N.bank(n)[:, 0:P * (b_ - a)].rearrange("p (m c) -> p m c", c=P)
                                    ).then_inc(taken1, 1)
            dve.memset(SS[:, :, 0, :], 0.0)
            dve.memset(rbuf, 0.0)
            dr()
            for i in range(11):
                for d_ in range(2):
                    n = n1("kv", 2 * i + d_)
                    N.wait_made(dve, n)
                    c = i if d_ == 0 else (3 - i if i < 4 else 15 - i)
                    for pr in range(2):
                        d = 2 * d_ + pr
                        dve.scalar_tensor_tensor(out=SS[:, d, i + 1, :], in0=SS[:, d, i, :], scalar=decay[:, d, c:c + 1],
                                                 in1=N.bank(n)[:, P * pr:P * pr + P], op0=ALU.mult, op1=ALU.add)
                    dr().then_inc(taken1, 1)
                dr().then_inc(state_made, 1)
            for u in range(16):
                n = n1("s", u)
                N.wait_made(dve, n)
                if u >= 2:
                    dve.wait_ge(intra_done, u - 1)
                for d_ in range(2):
                    o = CS1["maskf" if d_ == 0 else "maskb"][0]
                    dve.copy_predicated(pmask[:, u % 2, d_, :], cs1[:, o:o + P].bitcast(U32),
                                        N.bank(n)[:, P * d_:P * d_ + P])
                dr().then_inc(masked, 1)
                dr().then_inc(taken1, 1)
            for hh in range(4):
                dve.wait_ge(rstd_o, hh + 1)
                dve.scalar_tensor_tensor(out=oT[:, hh, :], in0=bank[:, hh, :], scalar=p1("gn"), in1=rstd[:, hh % 2, :],
                                         op0=ALU.mult, op1=ALU.mult)
                dr()
                dve.wait_ge(g_silu, hh + 1)
                dve.tensor_tensor(oT[:, hh, :], oT[:, hh, :], gT[:, hh, :], ALU.mult).then_inc(o_made, 1)

            def merge(N, name, t, i, first, gate_no):
                n = N.no(name, i + 1)
                if not first:
                    dr()
                N.wait_made(dve, n)
                dve.wait_ge(gates_made, gate_no)
                half = sig[:, (i // 2) % 2, :]
                if first:
                    dve.tensor_tensor(y[:, t, :], half, N.bank(n), ALU.mult).then_inc(N.taken_sem, 2)
                else:
                    dve.tensor_tensor(tmp[:, :], half, N.bank(n), ALU.mult)
                    dr()
                    dve.tensor_tensor(y[:, t, :], y[:, t, :], tmp[:, :], ALU.add).then_inc(N.taken_sem, 2)
            for t in range(8):
                for b in range(2):
                    merge(N, "merge", t, 4 * t + 2 * b, b == 0, 2 * t + b + 1)
                if t == 4:
                    for i in range(2):
                        dve.wait_ge(late_made, i + 1)
                        dve.tensor_copy(adar_late[:, i, :], bank[:, 4 - i, :]).then_inc(late_copied, 1)
                if t == 6:
                    for i in range(2):
                        dve.wait_ge(late_turned, i + 1)
                        modulations(i + 1, bank[:, 4 - i, :])
                    dr()
                    gain(2, 32, 0, "g2")
            for t in range(8):
                n = n1("out", t)
                N.wait_made(dve, n)
                dve.scalar_tensor_tensor(out=x[:, t, :], in0=N.bank(n), scalar=mods[:, 16 + t, 0:1], in1=x[:, t, :],
                                         op0=ALU.mult, op1=ALU.add).then_inc(taken1, 1)

            dve.wait_ge(rstd_made, 3)
            norm(lambda k: x[:, k, :], lambda k: h[:, k, :], lambda k: amp[:, 2, k:k + 1], 0, KD,
                 shift=lambda k: mods[:, 24 + k, 0:1], inc=h_made)
            for m in range(TT):
                for half in range(2):
                    take(N, n1("h2k", 2 * m + half), h2k[:, m, 512 * half:512 * half + 512])
            n = n1("logits")
            N.wait_made(dve, n)
            lg = N.bank(n)[:, 0:TT * E].rearrange("p (m e) -> p m e", m=TT)
            dve.tensor_reduce(stat[:, 0, :], lg, AX.X, ALU.max)
            dr()
            dve.tensor_tensor(aff[:, 0, :, :], lg, stat[:, 0, :].rearrange("p (m o) -> p m o", o=1)
                              .to_broadcast([P, TT, E]), ALU.subtract).then_inc(taken1, 1)
            dr().then_inc(affx, 1)
            dve.wait_ge(affe, 1)
            dve.tensor_reduce(stat[:, 1, :], aff[:, 1, :, :], AX.X, ALU.add)
            dr()
            dve.reciprocal(stat[:, 1, :], stat[:, 1, :])
            dr()
            dve.tensor_tensor(aff[:, 2, :, :], aff[:, 1, :, :], stat[:, 1, :].rearrange("p (m o) -> p m o", o=1)
                              .to_broadcast([P, TT, E]), ALU.mult).then_inc(aff_made, 1)
            N.wait_made(dve, n1("affT"))
            dve.tensor_copy(work, N.bank(n1("affT"))[0:E, :])
            take(N, n1("affT"), affT, m=E)
            dr()
            for _r in range(CAP // 8):
                dve.max(top8, work)
                dr()
                dve.match_replace(work, top8, work, -1.0)
                dr()
            dve.tensor_scalar(mark, work, 0.0, None, ALU.is_lt)
            dr()
            dve.memset(work, 1.0)
            dr()
            dve.tensor_tensor_scan(slot, work, mark, 0.0, ALU.mult, ALU.add)
            dr()
            dve.tensor_tensor(slot, slot, mark, ALU.mult)
            dr()
            dve.tensor_scalar(slot, slot, 1.0, None, ALU.subtract).then_inc(slot_made, 1)
            take(N, n1("slotT"), slot_tok,
                 src=N.bank(n1("slotT"))[:, 0:TT * E].rearrange("p (m e) -> p m e", m=TT))
            dr()
            dve.wait_ge(loaded_moe, 16)
            for m in range(TT):
                dve.tensor_tensor(selx[:, m, :, :],
                                  slot_tok[:, m, :].rearrange("p (e c) -> p e c", c=1).to_broadcast([P, E, CAP]),
                                  ce_("iota").rearrange("p (e c) -> p e c", e=1).to_broadcast([P, E, CAP]),
                                  ALU.is_equal).then_inc(sel_ready, 1)
            for k in range(KD):
                for half in range(2):
                    take(N, n1("gather", 2 * k + half), xs_all[:, 4 * half:4 * half + 4, k, :],
                         src=N.bank(n1("gather", 2 * k + half)).rearrange("p (e c) -> p e c", e=4))

            dr()
            dve.tensor_copy(xsT.rearrange("p k c -> p (k c)"), xs_all[:, 0, :, :].rearrange("p k c -> p (k c)")
                            ).then_inc(xs_taken, 1)
            dr()
            posf = tmp[:, :]
            dve.wait_ge(loaded_pos, 16)
            dve.tensor_copy(posf, posi)
            dr()
            TWO_PI = 2 * np.pi
            MAGIC = 12582912.0
            C1 = 6.28125
            C2 = float(np.float32(np.floor((TWO_PI - C1) * 2.0 ** 21) / 2.0 ** 21))
            C3 = float(np.float32(TWO_PI - C1 - C2))
            for i, (s_, c_t, f, sg_) in enumerate(((h[:, 1, :], h[:, 0, :], "freq", "sign"),
                                                (h[:, 3, :], h[:, 2, :], "freqM", "signM"))):
                dve.tensor_scalar(s_, posf, c_(f), None, ALU.mult)
                dr()
                dve.tensor_scalar(c_t, s_, float(1 / TWO_PI), MAGIC, ALU.mult, ALU.add)
                dr()
                dve.tensor_scalar(c_t, c_t, MAGIC, None, ALU.subtract)
                for c in (C1, C2, C3):
                    dr()
                    dve.scalar_tensor_tensor(out=s_, in0=c_t, scalar=-c, in1=s_, op0=ALU.mult, op1=ALU.add)
                dr()
                dve.tensor_scalar(s_, s_, 3.1415925, -3.1415925, ALU.min, ALU.max).then_inc(ang_made, 1)
                dve.wait_ge(sin_made, i + 1)
                dve.tensor_scalar(s_, s_, c_(sg_), None, ALU.mult)
                dve.tensor_tensor(c_t, c_t, c_t, ALU.mult)
                dr()
                dve.tensor_scalar(c_t, c_t, -2.0, 1.0, ALU.mult, ALU.add)
                dr()

            def experts(pair, y_of_pair):
                for half in range(2):
                    dve.wait_ge(up_made, pair * 2 + (half + 1))
                    dve.wait_ge(silu_made, pair * 2 + (half + 1))
                    dve.tensor_tensor(acts[:, 512 * half:512 * half + 512], sg[:, half, :], bank[:, 2 + half, :],
                                      ALU.mult).then_inc(a_ready, 1)
                dr()
                for half in range(2):
                    dve.wait_ge(y_made, pair * 2 + (half + 1))
                    dve.tensor_copy(top8[:, half:half + 1], bank[0:E, 6 + half, 0:1])
                    dve.tensor_copy(y_of_pair[:, :, 512 * half:512 * half + 512],
                                    bank[:, 6 + half:7 + half, :]).then_inc(y_taken, 1)
                dr()
            with dve.Fori(0, E // 2 - 1) as pair:
                experts(pair, yexp[:, bass.ds(pair, 1), :])
                dve.tensor_copy(xsT.rearrange("p k c -> p (k c)"),
                                xs_all[:, bass.ds(pair + 1, 1), :, :].rearrange("p e k c -> p (e k c)")
                                ).then_inc(xs_taken, 1)
            experts(E // 2 - 1, yexp[:, E // 2 - 1:E // 2, :])
            for p in range(8):
                a, b = n1("selw", 2 * p), n1("selw", 2 * p + 1)
                N.wait_made(dve, b)
                dr()
                dve.tensor_scalar(tmp[:, :], N.bank(a), ce_("cidx"), None, ALU.is_equal).then_inc(taken1, 1)
                dr()
                dve.tensor_tensor(selw[:, p, :], tmp[:, :], N.bank(b), ALU.mult).then_inc(taken1, 1)
            for t in range(8):
                n = n1("scatter", t)
                N.wait_made(dve, n)
                dve.scalar_tensor_tensor(out=x[:, t, :], in0=N.bank(n), scalar=mods[:, 40 + t, 0:1], in1=x[:, t, :],
                                         op0=ALU.mult, op1=ALU.add).then_inc(taken1, 1)
            dve.wait_ge(rstd_made, 4)
            norm(lambda k: x[:, k, :], lambda k: x[:, k, :], lambda k: p1("gf", k), 0, KD, inc=x_made)
            dr()
            dve.tensor_copy(tables, tables_early)
            dr()

            with dve.Fori(0, LAYERS) as l:
                N = Numbers(LAY, made2, taken2, l * N_LAY)
                no = N.no
                ub = l * N_UNITS
                rs = l * R_LAYER + R_ONE

                def rope(name, n_tiles, raw, out, cos_, sin_, scaled, factor):
                    order = rope_order(n_tiles)
                    for i, (what, j) in enumerate(order):
                        n = no(name, i)
                        dr()
                        N.wait_made(dve, n)
                        if what == "raw":
                            dve.tensor_scalar(raw(j), N.bank(n), factor if j < scaled else 1.0, None, ALU.mult
                                              ).then_inc(taken2, 1)
                            dr()
                            dve.tensor_tensor(rope1[:, j % 2, :], raw(j), cos_, ALU.mult)
                        else:
                            dve.tensor_tensor(rope2, N.bank(n), sin_, ALU.mult)
                            dr()
                            dve.tensor_tensor(out(j), rope1[:, j % 2, :], rope2, ALU.add).then_inc(taken2, 1)

                def attend(sec):
                    us = SECTION[sec]
                    c8 = lambda u: slice(u["n"] % 8, u["n"] % 8 + 1)
                    for s in range(len(us) + 4):
                        now = us[s] if s < len(us) else None
                        if now:
                            n, nk = now["n"], now["nk"]
                            S = bank[:, n % 3, :]
                            if now["kind"] != "full":
                                dve.wait_ge(scored, ub + n + 1)
                            if now["kind"] in ("causal", "window"):
                                dve.tensor_tensor(S[:, nk - P:nk], S[:, nk - P:nk], c_("causal"), ALU.add)
                                if now["kind"] == "window" and nk > P:
                                    dve.tensor_tensor(S[:, 0:P], S[:, 0:P], c_("recent"), ALU.add)
                            if now["kind"] == "cmp":
                                o = NCMP * now["qt"]
                                dve.tensor_tensor(S[:, 0:nk], S[:, 0:nk], c_("cmp_add")[:, o:o + NCMP], ALU.add)
                        two = us[s - 2] if 2 <= s <= len(us) + 1 else None
                        if two:
                            d8 = c8(two)
                            if two["sink"] is not None or two["kind"] == "cmp":
                                dve.wait_ge(exped, ub + two["n"] + 1)
                            if two["sink"] is not None:
                                dve.tensor_tensor(den[:, d8], den[:, d8], esink[:, d8], ALU.add)
                            if two["kind"] == "cmp":
                                dve.tensor_scalar(den[:, d8], den[:, d8], 1e-30, None, ALU.max)
                        dr()
                        if now:
                            if now["kind"] == "full":
                                dve.wait_ge(scored, ub + n + 1)
                            if now["sink"] is None:
                                dve.tensor_reduce(nbias[:, c8(now)], S[:, 0:nk], AX.X, ALU.max, negate=True
                                                  ).then_inc(biased, 1)
                            else:
                                dve.tensor_reduce(nmax[:, c8(now)], S[:, 0:nk], AX.X, ALU.max, negate=True)
                                dr()
                                dve.tensor_tensor(nbias[:, c8(now)], nmax[:, c8(now)],
                                                  nsink[:, now["sink"]:now["sink"] + 1], ALU.min).then_inc(biased, 1)
                        if two:
                            if two["sink"] is None and two["kind"] != "cmp":
                                dve.wait_ge(exped, ub + two["n"] + 1)
                            dve.reciprocal(rden[:, d8], den[:, d8])
                        if 3 <= s <= len(us) + 2 and us[s - 3]["gate"] is not None and not us[s - 3]["first"]:
                            u = us[s - 3]
                            dve.tensor_tensor(coef[:, c8(u)], rden[:, c8(u)],
                                              sgate[:, u["gate"][0], u["gate"][1]:u["gate"][1] + 1], ALU.mult)
                        if 1 <= s <= len(us) and us[s - 1]["kind"] == "cmp":
                            u = us[s - 1]
                            n, w, o = u["n"], u["nk"], NCMP * u["qt"]
                            dve.wait_ge(exped, ub + n + 1)
                            dve.tensor_tensor(probs[:, n % 3, 0:w], probs[:, n % 3, 0:w], c_("cmp_mul")[:, o:o + NCMP],
                                              ALU.mult)
                            dr().then_inc(cmp_masked, 1)
                            dve.tensor_reduce(den[:, c8(u)], probs[:, n % 3, 0:w], AX.X, ALU.add)
                            dr()
                        if s >= 4:
                            u = us[s - 4]
                            n = u["n"]
                            O = bank[:, 5 + n % 2, u["vc"]:u["vc"] + u["w"]]
                            dst = otok[:, u["qt"] % 2, u["col"]:u["col"] + u["w"]]
                            dve.wait_ge(pv_made, ub + n + 1)
                            if u["first"] and u["h"] == 0 and u["qt"] >= 2:
                                N.wait_made(dve, no(f"ot{sec}", u["qt"] - 2))
                            if u["gate"] is None:
                                ins = dve.tensor_scalar(dst, O, rden[:, c8(u)], None, ALU.mult)
                            elif u["first"]:
                                ins = dve.tensor_scalar(dst, O, rden[:, c8(u)],
                                                        sgate[:, u["gate"][0], u["gate"][1]:u["gate"][1] + 1],
                                                        ALU.mult, ALU.mult)
                            else:
                                ins = dve.scalar_tensor_tensor(out=dst, in0=O, scalar=coef[:, c8(u)], in1=dst,
                                                               op0=ALU.mult, op1=ALU.add)
                            ins.then_inc(o_taken, 1)
                            if u["last"]:
                                dr().then_inc(tok_done, 1)

                dve.wait_ge(loaded_pr2, l * 16 + 16)
                dve.tensor_scalar(nsink, p2("sinks"), -1.0, None, ALU.mult)
                dve.wait_ge(rstd_made, rs + 1)
                norm(lambda k: x[:, k, :], lambda k: h[:, k, :], lambda k: p2("norm_mix", k), 0, KD, inc=h_made)
                rope("a_fm", 5, lambda j: (Q[:, j, :] if j < 4 else K[:, 0, :]),
                     lambda j: (Q[:, j, :] if j < 4 else K[:, 0, :]), cosT, sinT, 4, HD ** -0.5)
                for m in range(TT):
                    take(N, no("v", m), vtok[:, m, :], width=408)
                dr()
                dve.wait_ge(sgate_made, l + 1)
                attend(0)
                g0 = l * G_LAYER + 16
                for t in range(8):
                    merge(N, "merge0", t, 2 * t, True, g0 + t + 1)

                take(N, no("kcvc", 0), K[:, 2, :])
                take(N, no("kcvc", 1), K[:, 3, :])
                dr()

                def blocks(i, name):
                    src = K[:, 2 + i, :]
                    win = bass.AP(tensor=src.tensor, offset=src.offset, ap=[list(src.ap[0]), [1, 32], [16, NCMP]])
                    dve.tensor_tensor(cmpb, win, p2(name).rearrange("p (j o) -> p j o", o=1)
                                      .to_broadcast([P, 32, NCMP]), ALU.add).then_inc(blocks_made, 1)
                blocks(0, "pek")
                rope("b_fm", 6, lambda j: (Q[:, j, :] if j < 4 else K[:, j - 4, :]),
                     lambda j: (Q[:, 4 + j, :] if j < 4 else K[:, j - 4, :]), cosT, sinT, 4, HD ** -0.5)
                N.wait_made(dve, no("cmp", 0))
                blocks(1, "pev")
                take(N, no("cmp", 2), cmp1[:, 2, 0:NCMP], width=NCMP)
                take(N, no("cmp", 3), vcmp[0:NCMP, :], m=NCMP, width=P)
                attend(1)
                for t in range(8):
                    merge(N, "merge1", t, 2 * t, False, g0 + 8 + t + 1)

                for j in range(5):
                    take(N, no("lat", j), lat[:, j, :])
                dve.wait_ge(rstd_made, rs + 3)
                norm(lambda k: lat[:, k, :], lambda k: lat[:, k, :], lambda k: p2("qn", k), 0, 3)
                norm(lambda k: lat[:, 3 + k, :], lambda k: lat[:, 3 + k, :], lambda k: p2("kvn", k), 1, 2)
                dr().then_inc(lat_normed, 1)
                n = no("kr", 0)
                take(N, n, lat[:, 5, :])
                dr()
                dve.tensor_tensor(rope1[:, 0, :], lat[:, 5, :], cosM, ALU.mult)
                N.wait_made(dve, no("kr", 1))
                dve.tensor_tensor(rope2, N.bank(no("kr", 1)), sinM, ALU.mult)
                dr()
                dve.tensor_tensor(lat[:, 5, :], rope1[:, 0, :], rope2, ALU.add).then_inc(taken2, 1)
                dr()
                for j in range(8):
                    dve.tensor_copy(K[64:96, j, :], lat[64:96, 5, :])
                rope("q_fm", 8, lambda j: Q[:, j, :], lambda j: Q[:, j, :], cosM, sinM,
                     8, MLA_D ** -0.5)
                for j in range(8):
                    take(N, no("k_fm", j), K[0:64, j, :], m=64)
                for m in range(TT):
                    take(N, no("v_mla", m), vmla[:, m, :])
                attend(2)
                dve.wait_ge(rstd_made, rs + 4)
                norm(lambda k: mem[:, k, :], lambda k: hm[:, k, :], lambda k: p2("norm_mem", k), 1, KD, MEM, inc=h_made)
                for t in range(8):
                    merge(N, "merge2", t, 2 * t, False, g0 + 16 + t + 1)

                def residual(name, tell=False):
                    for t in range(8):
                        n = no(name, t)
                        N.wait_made(dve, n)
                        dve.tensor_tensor(x[:, t, :], N.bank(n), x[:, t, :], ALU.add).then_inc(taken2, 1)
                        if tell:
                            dr().then_inc(x_made, 1)
                residual("out")
                dve.wait_ge(rstd_made, rs + 5)
                norm(lambda k: x[:, k, :], lambda k: h[:, k, :], lambda k: p2("norm_x", k), 0, KD, inc=h_made)
                for j in range(4):
                    take(N, no("xk", j), K[:, j, 0:MEM], width=MEM)
                for m in range(2):
                    take(N, no("xv", m), vmla[:, m, :])
                for j in range(4):
                    N.wait_made(dve, no("xq", j))
                    dve.tensor_scalar(Q[:, j, :], N.bank(no("xq", j)), P ** -0.5, None, ALU.mult).then_inc(taken2, 1)
                attend(3)
                residual("xo")
                dve.wait_ge(rstd_made, rs + 6)
                norm(lambda k: x[:, k, :], lambda k: h[:, k, :], lambda k: p2("norm_ffn", k), 0, KD, inc=h_made)
                for f in range(NFF):
                    n = no("gu", 2 * f + 1)
                    N.wait_made(dve, n)
                    dve.wait_ge(gates_made, g0 + 24 + f + 1)
                    dve.tensor_tensor(act_ff[:, f, :], sig[:, f % 2, :], N.bank(n), ALU.mult).then_inc(taken2, 2)
                residual("down", tell=True)

            dve.wait_ge(rstd_made, R_ONE + LAYERS * R_LAYER + 1)
            norm(lambda k: x[:, k, :], lambda k: h[:, k, :], lambda k: gfinal[:, k:k + 1], 0, KD, inc=out_ready)


SQ_ONE, SQ_LAYER = 4 * KD, 37
H_ONE, H_LAYER = 3 * KD, 4 * KD
R_ONE, R_LAYER = 4, 6
G_LAYER = 24 + NFF


def weight_stream(w):
    stream = np.zeros((SLOTS, P, SLOT * P), np.float32)
    at = [0]

    def put(block, tiles=1):
        s, c = divmod(at[0], SLOT)
        stream[s, 0:block.shape[0], c * P:c * P + block.shape[1]] = block
        at[0] += tiles

    def fm(m, c0, k=KD, width=P):
        for i in range(k):
            put(m[P * i:P * i + P, c0:c0 + width])

    def columns_of(m, parts):
        return np.concatenate([m[:, a:b] for a, b in parts], axis=1)

    def quads(m, k):
        for i in range(k):
            put(m[P * i:P * i + P], 4)

    def align(slots):
        at[0] = slots * SLOT

    ada, win = w["ada_w"][0], w["w_in"][0]

    def modulation_rows(i, k):
        for j in range(4):
            put(ada[P * k:P * k + P, 512 * (4 * i + j):512 * (4 * i + j + 1)], 4)
    for k in range(KD):
        modulation_rows(0, k)
    for g in range(4):
        fm(win, 1568 + P * g)
    fm(win, 0)
    fm(win, P)
    r = np.zeros((D, P), np.float32)
    r[:, 0:16], r[:, 32:48] = win[:, 768:784], win[:, 784:800]
    fm(r, 0)
    fm(win, 800)
    fm(win, 928)
    quads(win[:, 256:768], KD)
    for g in range(4):
        fm(win, 1056 + P * g)
    for it in range(16):
        t, b_no = it // 2, it % 2
        if 1 <= it <= 8:
            for k in (2 * ((it - 1) % 4), 2 * ((it - 1) % 4) + 1):
                modulation_rows(1 + (it - 1) // 4, k)
        fm(win, (2080, 3104)[b_no] + P * t)
        fm(w[("w_gla_proj", "w_pool_proj")[b_no]][0], P * t, 4)
    for t in range(8):
        fm(w["w_out"][0], P * t)
    assert at[0] == TILES_ONE
    align(SLOTS_ONE)
    for e in range(0, E, 2):
        for half, name in ((0, "w_gate_e"), (0, "w_up_e"), (1, "w_gate_e"), (1, "w_up_e"),
                           (0, "w_down_e"), (1, "w_down_e")):
            for k in range(8):
                for j in range(2):
                    put(w[name][0, e + j, P * k:P * k + P, 512 * half:512 * half + 512], 4)
    for l in range(LAYERS):
        align(SLOTS_ONE + E * SLOTS_EXPERT + l * SLOTS_LAYER)
        start = at[0]
        win = w["w_in_2"][l]

        def head_pairs(c0):
            for t in range(4):
                fm(columns_of(win, [(c0 + 64 * t, c0 + 64 * t + 64), (c0 + 64 * t + 256, c0 + 64 * t + 320)]), 0)

        def merge(b, name):
            for t in range(8):
                fm(win, 2744 + 1024 * b + P * t)
                fm(w[name][l], P * t, 4)
        head_pairs(0)
        fm(win, 512)
        quads(columns_of(win, [(640, 768), (1664, 1792), (1920, 2048), (2048, 2072)]), KD)
        merge(0, "w_br_a_2")
        fm(win, 1280)
        fm(win, 1408)
        head_pairs(768)
        fm(win, 1536)
        fm(win, 1792)
        for name in ("nsa_wk1_2", "nsa_wv1_2"):
            for j in range(32):
                b = np.zeros((P, P), np.float32)
                b[0:64, 0:64] = b[64:, 64:] = w[name][l, 64 * j:64 * j + 64]
                put(b)
        merge(1, "w_br_b_2")
        for j in range(5):
            fm(win, 2072 + P * j)
        r = np.zeros((D, P), np.float32)
        r[:, 64:96] = win[:, 2712:2744]
        fm(r, 0)
        for hh in range(HEADS):
            fm(w["mla_w_q_b_2"][l], MLA_D * hh, 3, MLA_D)
        for hh in range(HEADS):
            fm(w["mla_w_kv_b_2"][l], P * hh, 2, 64)
        quads(columns_of(w["mla_w_kv_b_2"][l], [(P * hh + 64, P * hh + 128) for hh in range(HEADS)]), 2)
        merge(2, "w_br_c_2")
        for t in range(8):
            fm(w["w_out_2"][l], P * t)
        for t in range(4):
            fm(w["w_xkv_2"][l], P * t)
        quads(w["w_xkv_2"][l, :, 512:1024], KD)
        for t in range(4):
            fm(w["w_xq_2"][l], P * t)
        for t in range(8):
            fm(w["w_xo_2"][l], P * t, 4)
        for f in range(NFF):
            fm(w["w_gate_up_2"][l], P * f)
            fm(w["w_gate_up_2"][l], FF + P * f)
        for t in range(8):
            fm(w["w_down_2"][l], P * t, NFF)
        assert at[0] == start + TILES_LAYER
    return stream


def feature_major(a):
    return np.ascontiguousarray(a.T.reshape(-1, P, a.shape[0]).transpose(1, 0, 2))


def tiles_of(v):
    return v.reshape(-1, P).T


def small_weights(w):
    p1 = np.zeros((P, N_PR1), np.float32)

    def put(arr, at, name, v):
        o, n = at[name]
        arr[:, o:o + n] = v

    for name, v in (("ada_b", w["ada_b"][0]), ("g1", w["norm1_g"][0]), ("g2", w["norm2_g"][0]),
                    ("b_decay", w["b_decay"][0]), ("gn", w["gla_norm_g"][0]), ("pool_scale", w["pool_scale"][0]),
                    ("gf", w["final_norm_g"]), ("gfinal", w["norm_final_2"])):
        put(p1, PR1, name, tiles_of(v))
    wup = np.zeros((P, 4, P), np.float32)
    for d in range(2):
        wup[32 * d:32 * d + 16, 2 * d:2 * d + 2] = w["w_decay_up"][0, d].reshape(16, 2, P)
    put(p1, PR1, "wup", wup.reshape(P, -1))
    put(p1, PR1, "wrouter", w["w_router"][0].reshape(KD, P, E).transpose(1, 0, 2).reshape(P, -1))
    put(p1, PR1, "poolw", w["pool_w"][0].transpose(1, 0, 2).reshape(P, -1))
    put(p1, PR1, "c2", np.stack([w["c"][0], w["c_ctx"]], 1).reshape(KD, P, 2).transpose(1, 0, 2).reshape(P, -1))
    p2 = np.zeros((LAYERS, P, N_PR2), np.float32)
    for l in range(LAYERS):
        for name, v in (("norm_mix", "norm_mix_2"), ("norm_x", "norm_xattn_2"), ("norm_mem", "norm_mem_2"),
                        ("norm_ffn", "norm_ffn_2"), ("qn", "mla_q_norm_2"), ("kvn", "mla_kv_norm_2")):
            put(p2[l], PR2, name, tiles_of(w[v][l]))
        put(p2[l], PR2, "sinks", w["swa_sinks_2"][l][None, :])
        for name, v in (("pek", "nsa_pe_k_2"), ("pev", "nsa_pe_v_2")):
            put(p2[l], PR2, name, np.concatenate([w[v][l].T, w[v][l].T], axis=0))
        for name, v in (("w2k", "nsa_wk2_2"), ("w2v", "nsa_wv2_2")):
            o = PR2[name][0]
            p2[l, 0:64, o:o + 64] = p2[l, 64:128, o + 64:o + 128] = w[v][l]
    return p1, p2


def kernel(**inputs):
    import concourse.bacc as _bacc
    from concourse.bass_utils import run_bass_kernel_spmd as _run

    w = {name: np.asarray(a) for name, a in inputs.items()}
    c, c1, ce, inv = constants()
    p1, p2 = small_weights(w)
    arrays = {
        "stream": weight_stream(w), "xT": feature_major(w["x"][0]), "ctxT": feature_major(w["ctx"][0]),
        "memT": feature_major(w["mem_2"][0]),
        "pos": np.ascontiguousarray(np.broadcast_to(w["positions_2"], (P, T))),
        "cst": c, "cs1": c1, "cse": ce, "inv": inv, "pr1": p1, "pr2": p2,
    }
    arrays = {f"in_{name}": a for name, a in arrays.items()}
    nc = _bacc.Bacc("TRN2", target_bir_lowering=False, num_devices=1)
    args = [nc.dram_tensor(name, a.shape, mybir.dt.from_np(a.dtype), kind="ExternalInput").ap()
            for name, a in arrays.items()]
    args.append(nc.dram_tensor("outT", (P, KD, T), F32, kind="ExternalOutput").ap())
    two_blocks(nc, *args)
    r = _run(nc, [arrays], core_ids=[0])
    return r.results[0]["outT"].transpose(2, 1, 0).reshape(1, T, D)
```
